# Optimizing a Trainium2 kernel written in Bass

```python
import math
import jax
import jax.numpy as jnp
from jax import lax
import numpy as np

D_MODEL = 1024
BATCH = 1
SEQ = 256
DEPTH = 2

CTX_LEN = 256
GRID_W = 64
HEAD_DIM = 64
N_GROUPS = 4
GROUP_W = D_MODEL // N_GROUPS
MIX_W = N_GROUPS * GROUP_W
HEADS_PER_GROUP = GROUP_W // HEAD_DIM
CHUNK = 128
DIFF_D = HEAD_DIM // 2
NA_ROWS = 8
NA_COLS = 16
NA_QCOLS = 16
NA_KCOLS = 32
N_EXPERTS = 16
EXPERT_FF = D_MODEL
CAPACITY_FACTOR = 2
ROPE_BASE = 10000.0
EPS = 1e-6
DIFF_Q_BLOCK = 128
A_END = 2 * GROUP_W
B_END = A_END + GROUP_W
C_END = B_END + 3 * GROUP_W
IN_W = C_END + 3 * GROUP_W


def rms_norm(x, g=None, eps=EPS):
    xf = x.astype(jnp.float32)
    y = xf * lax.rsqrt(jnp.mean(xf * xf, axis=-1, keepdims=True) + eps)
    if g is not None:
        y = y * g.astype(jnp.float32)
    return y.astype(x.dtype)

def axial_rope_tables(n_tokens, dim):
    half = dim // 2
    inv = 1.0 / (ROPE_BASE ** (jnp.arange(0, half, 2, dtype=jnp.float32) / half))
    t = jnp.arange(n_tokens)
    row = (t // GRID_W).astype(jnp.float32)[:, None] * inv
    col = (t % GRID_W).astype(jnp.float32)[:, None] * inv
    return (jnp.cos(row), jnp.sin(row), jnp.cos(col), jnp.sin(col))

def _rotate(x, cos, sin):
    x1, x2 = jnp.split(x, 2, axis=-1)
    return jnp.concatenate([x1 * cos - x2 * sin, x2 * cos + x1 * sin], axis=-1)

def apply_axial_rope(x, rope):
    n = x.shape[1]
    shp = (1, n) + (1,) * (x.ndim - 3) + (-1,)
    cr, sr, cc, sc = [t.reshape(shp).astype(x.dtype) for t in rope]
    xr, xc = jnp.split(x, 2, axis=-1)
    return jnp.concatenate([_rotate(xr, cr, sr), _rotate(xc, cc, sc)], axis=-1)

def chunk_spatial_gating(p, w_s, b_s):
    bn, n, _ = p.shape
    z = jax.nn.gelu(p)
    u, v = jnp.split(z, 2, axis=-1)
    v = rms_norm(v.reshape(bn, n // CHUNK, CHUNK, HEADS_PER_GROUP, HEAD_DIM))
    sv = jnp.einsum('hpq,bnqhc->bnphc', w_s, v) + b_s.T[None, None, :, :, None]
    return u * sv.reshape(bn, n, GROUP_W)

def fourier_mix(p):
    bn, n, _ = p.shape
    z = p.astype(jnp.float32).reshape(bn, n, HEADS_PER_GROUP, HEAD_DIM)
    f = jnp.fft.fft2(z, axes=(1, 3), norm="ortho").real
    return f.reshape(bn, n, GROUP_W).astype(p.dtype)

def lambda_value(lam, lam_init):
    lf = lam.astype(jnp.float32)
    return jnp.exp(jnp.sum(lf[0] * lf[1])) - jnp.exp(jnp.sum(lf[2] * lf[3])) + lam_init

def diff_attn_core(q, k, v, lam):
    s = jnp.einsum('bqhmd,bkhmd->bhmqk', q, k).astype(jnp.float32) * (DIFF_D ** -0.5)
    a = jax.nn.softmax(s, axis=-1)
    w = a[:, :, 0] - lam * a[:, :, 1]
    return jnp.einsum('bhqk,bkhd->bqhd', w.astype(v.dtype), v)

def ctx_attention(q, k, v):
    s = jnp.einsum('bqhd,bkhd->bhqk', q, k).astype(jnp.float32) * (HEAD_DIM ** -0.5)
    p = jax.nn.softmax(s, axis=-1).astype(v.dtype)
    return jnp.einsum('bhqk,bkhd->bqhd', p, v)

def neighbourhood_attn_latent(q, k, v, kc, vc, rpb):
    bn, n, h, dh = q.shape
    rows = n // GRID_W
    kr = min(NA_ROWS, rows)
    n_cb = GRID_W // NA_QCOLS
    scale = HEAD_DIM ** -0.5
    qg = q.reshape(bn, rows, n_cb, NA_QCOLS, h, dh).transpose(1, 0, 2, 3, 4, 5)
    kg = k.reshape(bn, rows, GRID_W, h, dh)
    vg = v.reshape(bn, rows, GRID_W, h, dh)
    qcol = jnp.arange(GRID_W).reshape(n_cb, NA_QCOLS)
    kstart = jnp.clip(qcol[:, 0] - NA_COLS // 2, 0, GRID_W - NA_KCOLS)
    kcol = kstart[:, None] + jnp.arange(NA_KCOLS)
    wstart = jnp.clip(qcol - NA_COLS // 2, 0, GRID_W - NA_COLS)
    kc3 = kcol[:, None, :]
    valid = (kc3 >= wstart[..., None]) & (kc3 < wstart[..., None] + NA_COLS)
    coff = jnp.clip(kc3 - qcol[..., None], -(NA_COLS - 1), NA_COLS - 1) + NA_COLS - 1
    rpb_c = rpb[:, :, coff]
    n_loc = kr * NA_KCOLS

    def one_row(args):
        r, q_row = args
        rstart = jnp.clip(r - kr // 2, 0, rows - kr)
        k_rows = lax.dynamic_slice_in_dim(kg, rstart, kr, axis=1)
        v_rows = lax.dynamic_slice_in_dim(vg, rstart, kr, axis=1)
        k_blk = k_rows[:, :, kcol]
        v_blk = v_rows[:, :, kcol]
        roff = rstart + jnp.arange(kr) - r + NA_ROWS - 1
        bias = rpb_c[:, roff].transpose(0, 2, 3, 1, 4).astype(jnp.float32)
        s_loc = jnp.einsum('bjqhd,brjkhd->bhjqrk', q_row, k_blk).astype(jnp.float32) * scale + bias
        s_loc = jnp.where(valid[:, :, None, :], s_loc, -jnp.inf)
        s_loc = s_loc.reshape(bn, h, n_cb, NA_QCOLS, n_loc)
        s_ctx = jnp.einsum('bjqhd,bkhd->bhjqk', q_row, kc).astype(jnp.float32) * scale
        p = jax.nn.softmax(jnp.concatenate([s_loc, s_ctx], axis=-1), axis=-1).astype(v.dtype)
        p_loc = p[..., :n_loc].reshape(bn, h, n_cb, NA_QCOLS, kr, NA_KCOLS)
        p_ctx = p[..., n_loc:]
        o = (jnp.einsum('bhjqrk,brjkhd->bjqhd', p_loc, v_blk)
             + jnp.einsum('bhjqk,bkhd->bjqhd', p_ctx, vc))
        return o.reshape(bn, GRID_W, h * dh)

    out = lax.map(one_row, (jnp.arange(rows), qg))
    return out.transpose(1, 0, 2, 3).reshape(bn, n, h * dh)

def token_mixers(hx, hc, w_in, w_out, head_g, sgu_w, sgu_b, dqn, dkn, dlam,
                 nqn, nkn, rpb, rope, lam_init, ctx_out):
    bn, n, _ = hx.shape
    h = HEADS_PER_GROUP
    px = hx @ w_in
    pc = hc @ w_in
    lam = lambda_value(dlam, lam_init)
    head_scale = jnp.asarray(np.array([1.0] * (2 * h) + [1.0 - lam_init] * h + [1.0] * h,
                                      dtype=np.float32), dtype=hx.dtype)

    def groups(p):
        return p[..., :A_END], p[..., A_END:B_END], p[..., B_END:C_END], p[..., C_END:]

    def diff_qkv(p, use_rope):
        m = p.shape[1]
        q, k, v = jnp.split(p, 3, axis=-1)
        q = rms_norm(q.reshape(bn, m, h, 2, DIFF_D), dqn)
        k = rms_norm(k.reshape(bn, m, h, 2, DIFF_D), dkn)
        if use_rope:
            q = apply_axial_rope(q, rope)
            k = apply_axial_rope(k, rope)
        return q, k, v.reshape(bn, m, h, HEAD_DIM)

    def na_qkv(p):
        m = p.shape[1]
        q, k, v = jnp.split(p, 3, axis=-1)
        q = rms_norm(q.reshape(bn, m, h, HEAD_DIM), nqn)
        k = rms_norm(k.reshape(bn, m, h, HEAD_DIM), nkn)
        return q, k, v.reshape(bn, m, h, HEAD_DIM)

    def merge(ya, yb, yc, yd):
        y = jnp.concatenate([ya, yb, yc, yd], axis=-1)
        m = y.shape[1]
        y = rms_norm(y.reshape(bn, m, N_GROUPS * h, HEAD_DIM), head_g.reshape(N_GROUPS * h, HEAD_DIM))
        y = y * head_scale[:, None]
        return y.reshape(bn, m, MIX_W) @ w_out

    aX, bX, cX, dX = groups(px)
    aC, bC, cC, dC = groups(pc)

    cq_c, ck_c, cv_c = diff_qkv(cC, False)
    nq_c, nk_c, nv_c = na_qkv(dC)

    ya = chunk_spatial_gating(aX, sgu_w, sgu_b)
    yb = fourier_mix(bX)
    cq, ck, cv = diff_qkv(cX, True)
    k_all = jnp.concatenate([ck, ck_c], axis=1)
    v_all = jnp.concatenate([cv, cv_c], axis=1)
    qb = cq.reshape(bn, n // DIFF_Q_BLOCK, DIFF_Q_BLOCK, h, 2, DIFF_D).transpose(1, 0, 2, 3, 4, 5)
    yc = lax.map(lambda qblk: diff_attn_core(qblk, k_all, v_all, lam), qb)
    yc = yc.transpose(1, 0, 2, 3, 4).reshape(bn, n, GROUP_W)
    nq, nk, nv = na_qkv(dX)
    yd = neighbourhood_attn_latent(nq, nk, nv, nk_c, nv_c, rpb)
    y_lat = merge(ya, yb, yc, yd)

    if not ctx_out:
        return y_lat, None
    m = hc.shape[1]
    ya_c = chunk_spatial_gating(aC, sgu_w, sgu_b)
    yb_c = fourier_mix(bC)
    yc_c = diff_attn_core(cq_c, ck_c, cv_c, lam).reshape(bn, m, GROUP_W)
    yd_c = ctx_attention(nq_c, nk_c, nv_c).reshape(bn, m, GROUP_W)
    return y_lat, merge(ya_c, yb_c, yc_c, yd_c)

def expert_choice_ffn(x, router_w, wg, wu, wd):
    bn, n, _ = x.shape
    cap = CAPACITY_FACTOR * n // N_EXPERTS
    aff = jax.nn.softmax(jnp.einsum('bnd,de->bne', x, router_w).astype(jnp.float32), axis=-1)
    gate, idx = lax.top_k(aff.transpose(0, 2, 1), cap)
    bidx = jnp.arange(bn)[:, None, None]
    xg = x[bidx, idx]
    hid = jax.nn.silu(jnp.einsum('becd,edf->becf', xg, wg)) * jnp.einsum('becd,edf->becf', xg, wu)
    o = jnp.einsum('becf,efd->becd', hid, wd) * gate[..., None].astype(x.dtype)
    return jnp.zeros_like(x).at[bidx, idx].add(o)

def first_inputs(seed: int = 0) -> dict:
    key = jax.random.key(seed)
    ks = jax.random.split(key, 24)
    f32 = jnp.float32
    L, D, H = DEPTH, D_MODEL, HEADS_PER_GROUP

    def nrm(k, shape, s):
        return jax.random.normal(k, shape, f32) * s

    return {
        "x": nrm(ks[0], (BATCH, SEQ, D), 1.0),
        "c": nrm(ks[1], (BATCH, D), 1.0),
        "ctx": nrm(ks[2], (BATCH, CTX_LEN, D), 1.0),
        "c_ctx": nrm(ks[3], (D,), 1.0),
        "ada_w": nrm(ks[4], (L, D, 6 * D), 0.5 * D ** -0.5),
        "ada_b": nrm(ks[5], (L, 6 * D), 0.02),
        "norm1_g": 1.0 + nrm(ks[6], (L, D), 0.02),
        "norm2_g": 1.0 + nrm(ks[7], (L, D), 0.02),
        "w_in": nrm(ks[8], (L, D, IN_W), D ** -0.5),
        "w_out": nrm(ks[9], (L, MIX_W, D), MIX_W ** -0.5),
        "head_out_g": 1.0 + nrm(ks[10], (L, MIX_W), 0.02),
        "sgu_w": nrm(ks[11], (L, H, CHUNK, CHUNK), CHUNK ** -0.5),
        "sgu_b": 1.0 + nrm(ks[12], (L, H, CHUNK), 0.02),
        "diff_qn_g": 1.0 + nrm(ks[13], (L, DIFF_D), 0.02),
        "diff_kn_g": 1.0 + nrm(ks[14], (L, DIFF_D), 0.02),
        "diff_lambda": nrm(ks[15], (L, 4, DIFF_D), 0.1),
        "na_qn_g": 1.0 + nrm(ks[16], (L, HEAD_DIM), 0.02),
        "na_kn_g": 1.0 + nrm(ks[17], (L, HEAD_DIM), 0.02),
        "na_rpb": nrm(ks[18], (L, H, 2 * NA_ROWS - 1, 2 * NA_COLS - 1), 0.1),
        "router_w": nrm(ks[19], (L, D, N_EXPERTS), D ** -0.5),
        "exp_w_gate": nrm(ks[20], (L, N_EXPERTS, D, EXPERT_FF), D ** -0.5),
        "exp_w_up": nrm(ks[21], (L, N_EXPERTS, D, EXPERT_FF), D ** -0.5),
        "exp_w_down": nrm(ks[22], (L, N_EXPERTS, EXPERT_FF, D), EXPERT_FF ** -0.5),
    }

def first_block(x, c, ctx, c_ctx, ada_w, ada_b, norm1_g, norm2_g, w_in, w_out, head_out_g,
              sgu_w, sgu_b, diff_qn_g, diff_kn_g, diff_lambda, na_qn_g, na_kn_g, na_rpb,
              router_w, exp_w_gate, exp_w_up, exp_w_down):
    n = x.shape[1]
    rope = axial_rope_tables(n, DIFF_D)
    s_c = jax.nn.silu(c)
    s_cc = jax.nn.silu(c_ctx)
    xc = ctx
    for l in range(DEPTH):
        last = l == DEPTH - 1
        lam_init = 0.8 - 0.6 * math.exp(-0.3 * l)
        mod = (s_c @ ada_w[l] + ada_b[l])[:, None, :]
        mod_c = (s_cc @ ada_w[l] + ada_b[l])[None, None, :]
        sh1, sc1, g1, sh2, sc2, g2 = jnp.split(mod, 6, axis=-1)
        csh1, csc1, cg1, csh2, csc2, cg2 = jnp.split(mod_c, 6, axis=-1)
        hx = rms_norm(x, norm1_g[l]) * (1.0 + sc1) + sh1
        hc = rms_norm(xc, norm1_g[l]) * (1.0 + csc1) + csh1
        y_lat, y_ctx = token_mixers(hx, hc, w_in[l], w_out[l], head_out_g[l], sgu_w[l], sgu_b[l],
                                    diff_qn_g[l], diff_kn_g[l], diff_lambda[l],
                                    na_qn_g[l], na_kn_g[l], na_rpb[l], rope, lam_init,
                                    not last)
        x = x + g1 * y_lat
        x = x + g2 * expert_choice_ffn(rms_norm(x, norm2_g[l]) * (1.0 + sc2) + sh2,
                                       router_w[l], exp_w_gate[l], exp_w_up[l], exp_w_down[l])
        if not last:
            xc = xc + cg1 * y_ctx
            xc = xc + cg2 * expert_choice_ffn(rms_norm(xc, norm2_g[l]) * (1.0 + csc2) + csh2,
                                              router_w[l], exp_w_gate[l], exp_w_up[l], exp_w_down[l])
    return x


A_HEADS = 4
A_DK = 128
A_DV = 256
A_QK = A_HEADS * A_DK
A_V = A_HEADS * A_DV
GATE_SOFT_CAP = 15.0
B_HEADS = 8
B_DK = 128
B_DV = 128
B_WIDTH = B_HEADS * B_DK
CONV_K = 4
CHUNK_2 = 64
D_FF = ((8 * D_MODEL // 3 + 255) // 256) * 256
DEEPNORM_ALPHA = (2.0 * DEPTH) ** 0.25
DEEPNORM_BETA = (8.0 * DEPTH) ** -0.25
LN_EPS = 1e-5
RMS_EPS = 1e-6
IN_SIZES = (A_QK, A_QK, A_V, A_V, A_HEADS, A_HEADS, 3 * B_WIDTH, B_WIDTH, B_HEADS, B_HEADS, D_MODEL, D_MODEL)
N_IN = sum(IN_SIZES)
SPLIT_POINTS = tuple(int(v) for v in np.cumsum(IN_SIZES)[:-1])


def _layernorm(x, g, b):
    xf = x.astype(jnp.float32)
    mu = jnp.mean(xf, -1, keepdims=True)
    var = jnp.mean(jnp.square(xf - mu), -1, keepdims=True)
    y = (xf - mu) * lax.rsqrt(var + LN_EPS) * g.astype(jnp.float32) + b.astype(jnp.float32)
    return y.astype(x.dtype)

def _head_rmsnorm(h, g):
    return h * lax.rsqrt(jnp.mean(jnp.square(h), -1, keepdims=True) + RMS_EPS) * g.astype(jnp.float32)

def _soft_cap(x):
    return GATE_SOFT_CAP * jnp.tanh(x / GATE_SOFT_CAP)

def _to_chunks(t):
    bsz, s, h = t.shape[:3]
    t = t.reshape((bsz, s // CHUNK_2, CHUNK_2, h) + t.shape[3:])
    perm = (1, 0, 3, 2) + tuple(range(4, t.ndim))
    return t.transpose(perm)

def _from_chunks(t):
    nc, bsz, h, l, d = t.shape
    return t.transpose(1, 0, 3, 2, 4).reshape(bsz, nc * l, h, d)

def _causal_conv(u, w):
    k, c = w.shape
    return lax.conv_general_dilated(u, w.astype(u.dtype)[:, None, :], window_strides=(1,), padding=[(k - 1, 0)],
                                    dimension_numbers=('NWC', 'WIO', 'NWC'), feature_group_count=c)

def _mlstm_chunked(q, k, v, i_pre, f_pre):
    bsz, _, h, dk = q.shape
    dv = v.shape[-1]
    q = q * (dk ** -0.5)
    li = _soft_cap(i_pre)
    lf = jax.nn.log_sigmoid(_soft_cap(f_pre))
    xs = (_to_chunks(q), _to_chunks(k), _to_chunks(v), _to_chunks(li), _to_chunks(lf))
    causal = jnp.tril(jnp.ones((CHUNK_2, CHUNK_2), dtype=bool))

    def step(carry, chunk):
        c_st, n_st, m_st = carry
        qc, kc, vc, lic, lfc = chunk
        g = jnp.cumsum(lfc, -1)
        dmat = jnp.where(causal, g[..., :, None] - g[..., None, :] + lic[..., None, :], -jnp.inf)
        inter = g + m_st[..., None]
        m_t = jnp.maximum(inter, jnp.max(dmat, -1))
        w = jnp.exp(dmat - m_t[..., None])
        s = jnp.einsum('bhtd,bhsd->bhts', qc, kc) * w
        sc = jnp.exp(inter - m_t)
        num = jnp.einsum('bhts,bhsv->bhtv', s, vc) + sc[..., None] * jnp.einsum('bhtd,bhdv->bhtv', qc, c_st)
        den = jnp.sum(s, -1) + sc * jnp.einsum('bhtd,bhd->bht', qc, n_st)
        h_out = num / jnp.maximum(jnp.abs(den), jnp.exp(-m_t))[..., None]
        g_end = g[..., -1]
        dec = g_end[..., None] - g + lic
        m_new = jnp.maximum(g_end + m_st, jnp.max(dec, -1))
        wk = jnp.exp(dec - m_new[..., None])
        carry_scale = jnp.exp(g_end + m_st - m_new)
        c_new = carry_scale[..., None, None] * c_st + jnp.einsum('bhs,bhsd,bhsv->bhdv', wk, kc, vc)
        n_new = carry_scale[..., None] * n_st + jnp.einsum('bhs,bhsd->bhd', wk, kc)
        return (c_new, n_new, m_new), h_out

    init = (jnp.zeros((bsz, h, dk, dv), jnp.float32), jnp.zeros((bsz, h, dk), jnp.float32),
            jnp.zeros((bsz, h), jnp.float32))
    _, hs = lax.scan(step, init, xs)
    return _from_chunks(hs)

def _l2norm(t):
    return t * lax.rsqrt(jnp.sum(jnp.square(t), -1, keepdims=True) + RMS_EPS)

def _gated_delta_chunked(q, k, v, beta, g):
    bsz, _, h, dk = q.shape
    dv = v.shape[-1]
    q = _l2norm(q) * (dk ** -0.5)
    k = _l2norm(k)
    qc, kc, vc = _to_chunks(q), _to_chunks(k), _to_chunks(v)
    bc, gc = _to_chunks(beta), _to_chunks(g)
    gcum = jnp.cumsum(gc, -1)
    incl = jnp.tril(jnp.ones((CHUNK_2, CHUNK_2), dtype=bool))
    strict = jnp.tril(jnp.ones((CHUNK_2, CHUNK_2), dtype=bool), -1)
    diff = gcum[..., :, None] - gcum[..., None, :]
    decay_mat = jnp.where(incl, jnp.exp(jnp.where(incl, diff, 0.0)), 0.0)
    kk = jnp.einsum('nbhid,nbhjd->nbhij', kc, kc)
    a_low = jnp.where(strict, bc[..., :, None] * kk * decay_mat, 0.0)
    rhs = jnp.concatenate([vc * bc[..., None], kc * (bc * jnp.exp(gcum))[..., None]], -1)
    sol = lax.linalg.triangular_solve(jnp.eye(CHUNK_2, dtype=jnp.float32) + a_low, rhs, left_side=True, lower=True,
                                      transpose_a=False, conjugate_a=False, unit_diagonal=True)
    u, w = sol[..., :dv], sol[..., dv:]
    attn = jnp.einsum('nbhid,nbhjd->nbhij', qc, kc) * decay_mat
    qe = qc * jnp.exp(gcum)[..., None]
    kd = kc * jnp.exp(gcum[..., -1:] - gcum)[..., None]
    g_end = jnp.exp(gcum[..., -1])

    def step(s_st, chunk):
        uc, wc, ac, qec, kdc, gec = chunk
        v_new = uc - jnp.einsum('bhld,bhdv->bhlv', wc, s_st)
        o = jnp.einsum('bhld,bhdv->bhlv', qec, s_st) + jnp.einsum('bhij,bhjv->bhiv', ac, v_new)
        s_new = s_st * gec[..., None, None] + jnp.einsum('bhld,bhlv->bhdv', kdc, v_new)
        return s_new, o

    init = jnp.zeros((bsz, h, dk, dv), jnp.float32)
    _, os_ = lax.scan(step, init, (u, w, attn, qe, kd, g_end))
    return _from_chunks(os_)

def _layer(x, w_in, b_igate, b_fgate, g_mlstm_norm, conv_w, a_log, dt_bias, g_gdn_norm,
           w_branch_a, w_branch_b, w_out, ln1_g, ln1_b, w_ffn_up, w_ffn_down, ln2_g, ln2_b):
    bsz, s, _ = x.shape
    f32 = jnp.float32
    proj = jnp.einsum('bsd,dn->bsn', x, w_in)
    qa, ka, va, oa, ia, fa, qkv_b, zb, beta_b, a_b, gate_a, gate_b = jnp.split(proj, SPLIT_POINTS, axis=-1)

    ha = _mlstm_chunked(qa.reshape(bsz, s, A_HEADS, A_DK).astype(f32),
                        ka.reshape(bsz, s, A_HEADS, A_DK).astype(f32),
                        va.reshape(bsz, s, A_HEADS, A_DV).astype(f32),
                        ia.astype(f32) + b_igate.astype(f32),
                        fa.astype(f32) + b_fgate.astype(f32))
    ha = _head_rmsnorm(ha, g_mlstm_norm.reshape(A_HEADS, A_DV)).reshape(bsz, s, A_V)
    ha = (ha * jax.nn.sigmoid(oa.astype(f32))).astype(x.dtype)

    qkv = jax.nn.silu(_causal_conv(qkv_b, conv_w))
    qb, kb, vb = jnp.split(qkv, [B_WIDTH, 2 * B_WIDTH], axis=-1)
    beta = jax.nn.sigmoid(beta_b.astype(f32))
    g = -jnp.exp(a_log.astype(f32)) * jax.nn.softplus(a_b.astype(f32) + dt_bias.astype(f32))
    hb = _gated_delta_chunked(qb.reshape(bsz, s, B_HEADS, B_DK).astype(f32),
                              kb.reshape(bsz, s, B_HEADS, B_DK).astype(f32),
                              vb.reshape(bsz, s, B_HEADS, B_DV).astype(f32), beta, g)
    hb = _head_rmsnorm(hb, g_gdn_norm).reshape(bsz, s, B_WIDTH)
    hb = (hb * jax.nn.silu(zb.astype(f32))).astype(x.dtype)

    y = (jax.nn.sigmoid(gate_a) * jnp.einsum('bsc,cd->bsd', ha, w_branch_a)
         + jax.nn.sigmoid(gate_b) * jnp.einsum('bsc,cd->bsd', hb, w_branch_b))
    mix = jnp.einsum('bsd,de->bse', y, w_out)
    x = _layernorm(DEEPNORM_ALPHA * x + mix, ln1_g, ln1_b)

    gu = jnp.einsum('bsd,df->bsf', x, w_ffn_up)
    gt, up = jnp.split(gu, [D_FF], axis=-1)
    ffn = jnp.einsum('bsf,fd->bsd', jax.nn.silu(gt) * up, w_ffn_down)
    x = _layernorm(DEEPNORM_ALPHA * x + ffn, ln2_g, ln2_b)
    return x

def second_inputs(seed: int = 0) -> dict:
    key = jax.random.key(seed)
    ks = jax.random.split(key, 20)
    f32 = jnp.float32

    def nrm(k, shape, scale):
        return jax.random.normal(k, shape, f32) * scale

    x = nrm(ks[0], (BATCH, SEQ, D_MODEL), 1.0)
    w_in = nrm(ks[1], (DEPTH, D_MODEL, N_IN), D_MODEL ** -0.5)
    b_igate = -2.0 + nrm(ks[2], (DEPTH, A_HEADS), 0.3)
    b_fgate = 3.0 + jax.random.uniform(ks[3], (DEPTH, A_HEADS), f32, 0.0, 3.0)
    g_mlstm_norm = 1.0 + nrm(ks[4], (DEPTH, A_V), 0.02)
    conv_w = nrm(ks[5], (DEPTH, CONV_K, 3 * B_WIDTH), CONV_K ** -0.5)
    a_log = jnp.log(jax.random.uniform(ks[6], (DEPTH, B_HEADS), f32, 1.0, 16.0))
    dt = jnp.exp(jax.random.uniform(ks[7], (DEPTH, B_HEADS), f32, math.log(1e-3), math.log(1e-1)))
    dt_bias = dt + jnp.log(-jnp.expm1(-dt))
    g_gdn_norm = 1.0 + nrm(ks[8], (DEPTH, B_DV), 0.02)
    w_branch_a = nrm(ks[9], (DEPTH, A_V, D_MODEL), A_V ** -0.5)
    w_branch_b = nrm(ks[10], (DEPTH, B_WIDTH, D_MODEL), B_WIDTH ** -0.5)
    w_out = nrm(ks[11], (DEPTH, D_MODEL, D_MODEL), D_MODEL ** -0.5 * DEEPNORM_BETA)
    ln1_g = 1.0 + nrm(ks[12], (DEPTH, D_MODEL), 0.02)
    ln1_b = nrm(ks[13], (DEPTH, D_MODEL), 0.02)
    w_ffn_up = nrm(ks[14], (DEPTH, D_MODEL, 2 * D_FF), D_MODEL ** -0.5)
    w_ffn_down = nrm(ks[15], (DEPTH, D_FF, D_MODEL), D_FF ** -0.5 * DEEPNORM_BETA)
    ln2_g = 1.0 + nrm(ks[16], (DEPTH, D_MODEL), 0.02)
    ln2_b = nrm(ks[17], (DEPTH, D_MODEL), 0.02)
    return {'x': x, 'w_in': w_in, 'b_igate': b_igate, 'b_fgate': b_fgate, 'g_mlstm_norm': g_mlstm_norm,
            'conv_w': conv_w, 'a_log': a_log, 'dt_bias': dt_bias, 'g_gdn_norm': g_gdn_norm,
            'w_branch_a': w_branch_a, 'w_branch_b': w_branch_b, 'w_out': w_out, 'ln1_g': ln1_g, 'ln1_b': ln1_b,
            'w_ffn_up': w_ffn_up, 'w_ffn_down': w_ffn_down, 'ln2_g': ln2_g, 'ln2_b': ln2_b}

def second_block(x, w_in, b_igate, b_fgate, g_mlstm_norm, conv_w, a_log, dt_bias, g_gdn_norm,
              w_branch_a, w_branch_b, w_out, ln1_g, ln1_b, w_ffn_up, w_ffn_down, ln2_g, ln2_b):
    for l in range(DEPTH):
        x = _layer(x, w_in[l], b_igate[l], b_fgate[l], g_mlstm_norm[l], conv_w[l], a_log[l], dt_bias[l],
                   g_gdn_norm[l], w_branch_a[l], w_branch_b[l], w_out[l], ln1_g[l], ln1_b[l],
                   w_ffn_up[l], w_ffn_down[l], ln2_g[l], ln2_b[l])
    return x


def setup_inputs(seed=0):
    out = dict(first_inputs(seed))
    for name, value in second_inputs(seed + 1).items():
        if name != "x":
            out[name + "_2"] = value
    return out


def reference(
    x, c, ctx, c_ctx, ada_w, ada_b, norm1_g, norm2_g, w_in, w_out, head_out_g, sgu_w, sgu_b,
    diff_qn_g, diff_kn_g, diff_lambda, na_qn_g, na_kn_g, na_rpb, router_w, exp_w_gate, exp_w_up,
    exp_w_down, w_in_2, b_igate_2, b_fgate_2, g_mlstm_norm_2, conv_w_2, a_log_2, dt_bias_2,
    g_gdn_norm_2, w_branch_a_2, w_branch_b_2, w_out_2, ln1_g_2, ln1_b_2, w_ffn_up_2,
    w_ffn_down_2, ln2_g_2, ln2_b_2,
):
    x = first_block(
        x, c, ctx, c_ctx, ada_w, ada_b, norm1_g, norm2_g, w_in, w_out, head_out_g, sgu_w, sgu_b,
        diff_qn_g, diff_kn_g, diff_lambda, na_qn_g, na_kn_g, na_rpb, router_w, exp_w_gate,
        exp_w_up, exp_w_down,
    )
    return second_block(
        x, w_in_2, b_igate_2, b_fgate_2, g_mlstm_norm_2, conv_w_2, a_log_2, dt_bias_2,
        g_gdn_norm_2, w_branch_a_2, w_branch_b_2, w_out_2, ln1_g_2, ln1_b_2, w_ffn_up_2,
        w_ffn_down_2, ln2_g_2, ln2_b_2,
    )


_drawn_inputs = setup_inputs


def setup_inputs(seed=0):
    import zlib

    import numpy as np

    out = dict(_drawn_inputs(seed))
    spreads = {}
    factors = {'norm1_g': 6.06,
     'norm2_g': 5.556,
     'head_out_g': 5.506,
     'sgu_b': 8.0,
     'diff_qn_g': 8.0,
     'diff_kn_g': 8.0,
     'diff_lambda': 3.91,
     'na_qn_g': 8.0,
     'na_kn_g': 8.0,
     'na_rpb': 8.0,
     'b_igate_2': 200.0,
     'g_mlstm_norm_2': 200.0,
     'g_gdn_norm_2': 8.0,
     'b_fgate_2': 3.101}
    for name, (base, spread) in spreads.items():
        noise = np.random.default_rng([zlib.crc32(name.encode()), seed]).standard_normal(out[name].shape)
        drawn = base * np.exp(spread * noise) if base else spread * noise
        out[name] = jnp.asarray(drawn.astype(out[name].dtype))
    for name, factor in factors.items():
        out[name] = (out[name] * factor).astype(out[name].dtype)
    return out
```

```python
import math
from collections import Counter
from contextlib import ExitStack, contextmanager

import concourse.bass as bass
import numpy as np
from concourse import mybir

ALU = mybir.AluOpType
ACT = mybir.ActivationFunctionType
F32 = mybir.dt.float32
AXX = mybir.AxisListType.X

P = 128
D = 1024
KT = D // P
SEQ = 256
DEPTH = 2
GRID_W = 64
HEADS = 4
HD = 64
DIFF_D = 32
NA_COLS = 16
N_EXP = 16
CAP = 2 * SEQ // N_EXP
ROPE_BASE = 10000.0
EPS = 1e-6
LN_EPS = 1e-5
IN_W = 2304
BAND = 2 * GRID_W - 1
CN = 512
RING = 6
BANKS = 8
NEG = -1e30

A_U, A_V, B_Z, C_Q, C_K, C_V, D_Q, D_K, D_V = 0, 256, 512, 768, 1024, 1280, 1536, 1792, 2048

A_DK, A_DV = 128, 256
B_HEADS = 8
D_FF = 2816
FT = D_FF // P
N_IN = 9240
ALPHA = (2.0 * DEPTH) ** 0.25
W2_QA, W2_KA, W2_VA, W2_OA, W2_I, W2_F = 0, 512, 1024, 2048, 3072, 3076
W2_QKV, W2_Z, W2_BETA, W2_A, W2_GA, W2_GB = 3080, 6152, 7176, 7184, 7192, 8216


class Count:

    def __init__(self, name, eng):
        self.name, self.eng, self.per_turn = name, eng, {}
        self.base, self.local = Counter(), Counter()
        self.turn = None
        self.unit_base, self.unit_local = 0, 0

    def due(self, what, n=1):
        self.local[what] += n
        v = self.base[what] + self.local[what]
        return v if self.turn is None else self.turn * self.per_turn[what] + v

    def unit(self, k=1):
        self.unit_local += k
        return self.unit_base + self.unit_local - 1

    def uses(self, n):
        v = n // BANKS + 1
        return v if self.turn is None else self.turn * (self.per_turn["unit"] // BANKS) + v

    @contextmanager
    def loop(self, turns, per_turn):
        self.per_turn = per_turn
        self.base.update(self.local)
        self.local = Counter()
        self.unit_base += self.unit_local
        self.unit_local = 0
        with self.eng.Fori(0, turns) as turn:
            self.turn = turn
            yield turn
            self.turn = None
        for what, n in self.local.items():
            assert per_turn[what] == n, (self.name, what, n)
            self.base[what] += n * turns
        if self.unit_local:
            assert self.unit_local == per_turn["unit"], (self.name, self.unit_local)
        self.unit_base += self.unit_local * turns
        self.local, self.unit_local = Counter(), 0


def expert_turn(ns):
    turn = {"unit": 32, "chunk_used": 24, "xgc_ready": 4, "xg_used": 4, "vector_step": 8 * (ns - 1)}
    turn.update({f"chunk{s}": 64 for s in range(RING)})
    return turn


def bc(ap, axis, shape):
    return ap.unsqueeze(axis).broadcast_to(shape)


def constants():
    f = np.float32
    n, c = np.arange(SEQ), np.arange(HD)
    wn = 2 * np.pi * np.outer(n, n) % (2 * np.pi * SEQ) / SEQ
    wn = 2 * np.pi * (np.outer(n, n) % SEQ) / SEQ
    wc = 2 * np.pi * (np.outer(c, c) % HD) / HD
    scale = 1.0 / math.sqrt(SEQ * HD)
    seq_dft = np.concatenate([np.cos(wn), np.sin(wn)], 1)
    two = np.eye(2)
    head_dft = np.concatenate([np.kron(two, np.cos(wc)), -np.kron(two, np.sin(wc))], 1) * scale
    half = DIFF_D // 2
    inv = (1.0 / (f(ROPE_BASE) ** (np.arange(0, half, 2, dtype=f) / f(half)))).astype(f)
    row = ((n // GRID_W).astype(f)[:, None] * inv).astype(f)
    col = ((n % GRID_W).astype(f)[:, None] * inv).astype(f)
    cos = np.concatenate([np.cos(row), np.cos(row), np.cos(col), np.cos(col)], 1)
    sin = np.concatenate([-np.sin(row), np.sin(row), -np.sin(col), np.sin(col)], 1)
    rope = np.concatenate([cos, sin], 1)
    qc = np.arange(P) % GRID_W
    kc = np.arange(SEQ) % GRID_W
    w0 = np.clip(qc - NA_COLS // 2, 0, GRID_W - NA_COLS)[:, None]
    window = np.where((kc[None] >= w0) & (kc[None] < w0 + NA_COLS), 0.0, NEG)
    i, j = np.arange(P)[:, None], np.arange(P)[None]
    causal_t = np.where(i <= j, 0.0, NEG)
    strict_t = (i < j) * 1.0
    levels = []
    for s in (1, 2, 4, 8, 16, 32, 64):
        levels.append(((i // (2 * s) == j // (2 * s)) & (i % (2 * s) >= s) & (j % (2 * s) < s)) * 1.0)
    slots = np.broadcast_to(np.arange(1, CAP + 1), (P, CAP))
    pick = np.zeros((P, 31))
    pick[:, 15] = 1.0
    out = {
        "seq_dft": seq_dft, "head_dft": head_dft, "rope": rope, "window": window,
        "ident": np.eye(P), "ones": np.ones((P, P)), "slots": slots, "pick": pick,
        "causal_t": np.concatenate([causal_t, np.zeros((P, P))], 1), "strict_t": strict_t,
        "levels": np.concatenate(levels + [levels[0].T], 1),
    }
    return {k: np.ascontiguousarray(v.astype(f)) for k, v in out.items()}


def first_half_memory(view):
    m = {}
    at = 132
    def put(name, width, **parts):
        nonlocal at
        m[name] = view(at, width)
        m[name + "_at"] = at
        at += width
    put("rope", 128)
    put("window", 256)
    put("slots", CAP)
    put("seq_dft", 2 * CN)
    put("head_dft", 256)
    put("rows", P)
    put("cols", 44)
    put("silu_c", 16)
    put("mod", 96)
    put("gain1", 16)
    put("gain2", 16)
    put("gains_qk", 192)
    put("lam_rows", 128)
    put("lam", 4)
    put("router", 128)
    put("ss", 128)
    put("aff", 64)
    put("small", 96)
    put("pos", 64)
    put("sgu_t", 512)
    put("scratch", 1536)
    put("gate", 2048)
    put("x", 4096)
    put("ht", 4096)
    put("xn", 4096)
    put("proj", 4 * IN_W)
    m["end"] = at
    return m


def build(nc, A, out, gate_scratch, band):
    with ExitStack() as ctx:
        ring = ctx.enter_context(nc.sbuf_tensor("ring", [P, RING * KT * CN], F32))
        arena = ctx.enter_context(nc.sbuf_tensor("arena", [P, 28600], F32))
        bank = [ctx.enter_context(nc.psum_tensor(f"bank{b}", [P, CN], F32)) for b in range(BANKS)]
        names = [f"bank_full{b}" for b in range(BANKS)] + [f"bank_free{b}" for b in range(BANKS)]
        names += [f"chunk{s}" for s in range(RING)]
        names += ["chunk_used", "vector_step", "scalar_step", "consts", "smalls", "band_out", "bias_in",
                  "x_ready", "silu_c", "row_ready", "row_saved", "gate1_in", "gate2_in", "bias_used",
                  "stat", "root", "xn_ready", "vn_ready", "lam_dot", "lam_exp", "qk_ready", "row_max", "w_diff",
                  "logit", "logit_exp", "aff_ready", "rank_ready", "sel_ready", "selg_ready", "xg_ready",
                  "xg_used", "xgc_ready", "moe_done",
                  "smalls2", "vecs_ready", "mg_soft", "mg_rows", "mg_en", "mexp_in", "mexp", "ha_ready", "bg_exp", "bg_in",
                  "bg_ln", "bg_cum", "bg_rows", "conv_done", "sq_ready", "sq_used", "rn_ready", "e_in", "e_exp",
                  "at_ready", "x0_ready", "heads_done", "hb_ready", "y_ready", "ln_gains", "ln_ready", "out_done"]
        sem = {n: ctx.enter_context(nc.semaphore(n)) for n in names}

        def view(at, width):
            return arena[:, at:at + width]

        ident, ones = view(0, 128), view(128, 4)
        m = first_half_memory(view)
        assert m["end"] <= 28600, m["end"]
        slot = [ring[:, s * KT * CN:(s + 1) * KT * CN].rearrange("p (k n) -> p k n", k=KT) for s in range(RING)]
        U = lambda n: bank[n % BANKS]
        full = [sem[f"bank_full{b}"] for b in range(BANKS)]
        free = [sem[f"bank_free{b}"] for b in range(BANKS)]

        X = m["x"].rearrange("p (t n) -> p t n", t=4)
        HT = m["ht"].rearrange("p (k n) -> p k n", k=KT)
        XN = m["xn"].rearrange("p (t n) -> p t n", t=4)
        PROJ = m["proj"].rearrange("p (t n) -> p t n", t=4)
        ADAB = m["proj"][:, 0:6 * D]
        SGU = m["proj"][:, 6 * D:6 * D + 512].rearrange("p (h q) -> p h q", h=HEADS)
        SGUT = m["sgu_t"].rearrange("p (h q) -> p h q", h=HEADS)
        BIAS = m["gate"].rearrange("p (t h k) -> p t h k", t=2, h=HEADS)
        GATE1 = m["gate"].rearrange("p (s n) -> p s n", s=2)
        SELT = m["gate"].rearrange("p (s b t) -> p s b t", s=2, b=4)
        SCR = m["scratch"]
        ROWBUF = SCR.rearrange("p (j n) -> p j n", j=3)
        ROWS, COLS = m["rows"], m["cols"]
        SC = m["silu_c"].rearrange("p (k s) -> p k s", s=2)
        MOD = m["mod"].rearrange("p (j s) -> p j s", s=2)
        GAIN = [m["gain1"].rearrange("p (k s) -> p k s", s=2), m["gain2"].rearrange("p (k s) -> p k s", s=2)]
        SHIFT = [MOD[:, 0:8, :], MOD[:, 24:32, :]]
        RW = m["router"].rearrange("p (k e) -> p k e", k=KT)
        SS = m["ss"]
        SS28 = SS[:, 0:112].rearrange("p (t g) -> p t g", t=4)
        SST = SS[:, 112:116]
        ROPE = m["rope"].rearrange("p (t c) -> p t c", t=2)
        SEQDFT = m["seq_dft"].rearrange("p (k n) -> p k n", k=2)
        HDFT = m["head_dft"]
        QKT = [m["ht"][:, 2048 * i:2048 * i + 2048].rearrange("p (b n) -> p b n", b=4) for i in range(2)]
        EXPS = m["xn"][:, 0:2048].rearrange("p (j q n) -> p j q n", j=2, q=2)
        W = m["xn"][:, 2048:3072].rearrange("p (j n) -> p j n", j=2)
        WT = m["xn"][:, 3072:4096].rearrange("p (j n) -> p j n", j=2)
        PT = m["xn"][:, 0:2048].rearrange("p (s b n) -> p s b n", s=2, b=2)
        XG = m["proj"][:, 0:8192].rearrange("p (k e c) -> p k e c", k=KT, e=N_EXP)
        XGC = m["proj"][:, 8192:9216].rearrange("p (j k c) -> p j k c", j=2, k=KT)
        GATE2 = m["proj"][:, 0:2048].rearrange("p (s n) -> p s n", s=2)
        SEL = m["ht"][:, 0:2048].rearrange("p (t e c) -> p t e c", t=4, e=N_EXP)
        AFFT = m["ht"][:, 2048:2560]
        WORK = m["ht"][:, 2560:3072]
        RANK = m["ht"][:, 3072:3584]
        OEXP = [m["ht"].rearrange("p (b n) -> p b n", b=4), m["xn"].rearrange("p (b n) -> p b n", b=4)]
        HID = SCR[:, 0:1024].rearrange("p (j n) -> p j n", j=2)
        HIDT = SCR[:, 1024:1536].rearrange("p (k c) -> p k c", k=KT)
        AFF = m["aff"].rearrange("p (t e) -> p t e", t=4)
        POS = m["pos"].rearrange("p (t e) -> p t e", t=4)
        SMALL = m["small"]

        block = ctx.enter_context(nc.Block())
        pe = Count("tensor", nc.tensor)
        ac = Count("scalar", nc.scalar)
        dv = Count("vector", nc.vector)
        sp = Count("sync", nc.sync)
        gp = Count("gpsimd", nc.gpsimd)
        mm = nc.tensor.matmul

        def turn(o, i):
            k = i.shape[0]
            return nc.tensor.transpose(o, i, ident[0:k, 0:k])

        m2, at2 = {}, [132]

        def put2(name, width):
            m2[name] = view(at2[0], width)
            at2[0] += width

        for name, width in (("causal", 256), ("strict", 128), ("levels", 1024), ("pick", 32), ("rows", P),
                            ("cols", 112), ("w_gates", 192), ("gate_rows", 2048), ("gate_cols", 64), ("ss", 64),
                            ("root_rows", 256), ("vecs", 8), ("scratch", 2048)):
            put2(name, width)
        assert at2[0] <= m["x_at"]
        base2 = m["x_at"] + 2 * D
        up = lambda at, width: view(base2 + at, width)
        X2 = X[:, 0:2, :]
        COLS2, SS2, VEC, SCR2 = m2["cols"], m2["ss"], m2["vecs"], m2["scratch"]
        CONVW = COLS2[:, 0:96].rearrange("p (i t) -> p i t", i=4)
        WG = m2["w_gates"].rearrange("p (k n) -> p k n", k=KT)
        GR = m2["gate_rows"].rearrange("p (i n) -> p i n", i=8)
        GC = m2["gate_cols"]
        LEVEL = m2["levels"].rearrange("p (i n) -> p i n", i=8)
        CAUSAL, STRICT, PICK = m2["causal"], m2["strict"], m2["pick"]
        R16 = m2["root_rows"]
        XT2 = up(0, 2048).rearrange("p (k n) -> p k n", k=KT)
        HAT = up(2048, 2048).rearrange("p (k n) -> p k n", k=KT)
        QA = up(4096, 1024).rearrange("p (h n) -> p h n", h=4)
        KA = up(5120, 1024).rearrange("p (h n) -> p h n", h=4)
        VA = up(6144, 2056).rearrange("p (t h n) -> p t h n", t=2, h=4)
        OA = up(8200, 2048).rearrange("p (t n) -> p t n", t=2)
        HA = up(10248, 2048).rearrange("p (t n) -> p t n", t=2)
        EA = up(12296, 1536).rearrange("p (j n) -> p j n", j=4)
        PA = up(13832, 1536).rearrange("p (j n) -> p j n", j=4)
        QB = up(4096, 2048).rearrange("p (h n) -> p h n", h=8)
        KB = up(6144, 2048).rearrange("p (h n) -> p h n", h=8)
        VB = up(8192, 2048).rearrange("p (h n) -> p h n", h=8)
        quad = lambda at: up(at, 512).rearrange("p (m n) -> p m n", m=4)
        EB, ATTN, AT, XI, XIT, YI, VX, KX, UU = [quad(10240 + 512 * i) for i in range(9)]
        WTT, ST, EG, QE = [up(14848 + 256 * i, 256).rearrange("p (h n) -> p h n", h=2) for i in range(4)]
        ZB = up(6144, 2048).rearrange("p (t n) -> p t n", t=2)
        SGA = up(8192, 2048).rearrange("p (t n) -> p t n", t=2)
        SGB = up(10240, 2048).rearrange("p (t n) -> p t n", t=2)
        HBN = up(12288, 2048).rearrange("p (t n) -> p t n", t=2)
        LNG = up(14336, 4096).rearrange("p (i n) -> p i n", i=4)
        HFF = up(4096, FT * SEQ).rearrange("p (f n) -> p f n", f=FT)
        assert base2 + 14336 + 4096 <= 28600
        NEG_B1, SCALE_A = 15.0, A_DK ** -0.5
        FF_TILES = [4, 4, 4, 4, 4, 2]

        def turn_pairs(src):
            done = []
            for j in range(4):
                u = pe.unit()
                if u >= BANKS:
                    nc.tensor.wait_ge(free[u % BANKS], pe.uses(u - BANKS))
                for k in range(2):
                    for t in range(2):
                        last = turn(U(u)[:, k * SEQ + t * P:k * SEQ + (t + 1) * P],
                                    src[:, t, (2 * j + k) * P:(2 * j + k + 1) * P])
                last.then_inc(full[u % BANKS], 1)
                done.append(u)
            for n_out in done:
                nc.tensor.wait_ge(free[n_out % BANKS], pe.uses(n_out))

        def take_pairs(e, dst, gain=None):
            for j in range(4):
                if (j % 2 == 1) != (e is ac):
                    e.unit()
                    continue
                u = e.unit()
                e.eng.wait_ge(full[u % BANKS], e.uses(u))
                if gain is None:
                    o, i = dst[:, 2 * j:2 * j + 2, :].rearrange("p k n -> p (k n)"), U(u)[:, :]
                    (nc.scalar.copy(o, i) if e is ac else nc.vector.tensor_copy(o, i)).then_inc(free[u % BANKS], 1)
                    e.eng.wait_ge(free[u % BANKS], e.uses(u))
                    continue
                for k in range(2):
                    o, i, g = dst[:, 2 * j + k, :], U(u)[:, k * SEQ:(k + 1) * SEQ], gain(2 * j + k)
                    ins = (nc.scalar.activation(o, i, ACT.Copy, scale=g) if e is ac
                           else nc.vector.tensor_scalar(o, i, g, None, ALU.mult))
                    if k:
                        ins.then_inc(free[u % BANKS], 1)
                        e.eng.wait_ge(free[u % BANKS], e.uses(u))
                    else:
                        ins.then_inc(sem[e.name + "_step"], 1)
                        e.eng.wait_ge(sem[e.name + "_step"], e.due(e.name + "_step"))

        def tiles(l):
            return range(4) if l < DEPTH - 1 else range(2)

        def streams(l):
            return range(2) if l < DEPTH - 1 else range(1)

        def jobs(l):
            return [(kind, t, h) for t in tiles(l) for kind in "CD" for h in range(HEADS)]

        PROJ_CHUNKS = [(0, 512), (512, 512), (1024, 512), (1536, 512), (2048, 256)]

        def proj_tiles(l, c):
            return tiles(l) if c == 0 else range(4)

        @block.sync
        def _(eng):
            count = [0]

            def load(src, kt=KT, n=CN):
                q = count[0]
                count[0] += 1
                if q >= RING:
                    nc.sync.wait_ge(sem["chunk_used"], sp.due("chunk_used"))
                eng.dma_start(slot[q % RING][:, 0:kt, 0:n], src.rearrange("(k p) n -> p k n", p=P)
                              ).then_inc(sem[f"chunk{q % RING}"], 16)

            for l in range(DEPTH):
                for j in range(12):
                    load(A["ada_w"][l, :, j * CN:(j + 1) * CN])
                for at, n in PROJ_CHUNKS:
                    load(A["w_in"][l, :, at:at + n], n=n)
                for c in range(2):
                    load(A["w_out"][l, :, c * CN:(c + 1) * CN])
                with sp.loop(4, expert_turn(len(streams(l)))) as g:
                    for e in range(4):
                        for c in range(2):
                            for w in ("exp_w_gate", "exp_w_up"):
                                load(A[w][l, g * 4 + e, :, c * CN:(c + 1) * CN])
                        for c in range(2):
                            load(A["exp_w_down"][l, g * 4 + e, :, c * CN:(c + 1) * CN])
            with_2 = A["w_in_2"]
            for l in range(DEPTH):
                for at in (W2_QA, W2_KA, W2_VA, W2_VA + CN, W2_OA, W2_OA + CN):
                    load(with_2[l, :, at:at + CN])
                for i in range(6):
                    load(with_2[l, :, W2_QKV + i * CN:W2_QKV + (i + 1) * CN])
                for first in (W2_Z, W2_GA):
                    for c in range(2):
                        load(with_2[l, :, first + c * CN:first + (c + 1) * CN])
                for c in range(2):
                    load(A["w_branch_a_2"][l, :, c * CN:(c + 1) * CN])
                for c in range(2):
                    load(with_2[l, :, W2_GB + c * CN:W2_GB + (c + 1) * CN])
                for c in range(2):
                    load(A["w_branch_b_2"][l, :, c * CN:(c + 1) * CN])
                for c in range(2):
                    load(A["w_out_2"][l, :, c * CN:(c + 1) * CN])
                for i, n in enumerate(FF_TILES):
                    for half in range(2):
                        at = half * D_FF + i * CN
                        load(A["w_ffn_up_2"][l, :, at:at + n * P], n=n * P)
                for c in range(2):
                    for i in range(3):
                        k1 = min(FT, 8 * i + 8)
                        load(A["w_ffn_down_2"][l, 8 * i * P:k1 * P, c * CN:(c + 1) * CN], kt=k1 - 8 * i)

        @block.gpsimd
        def _(eng):
            def get(dst, src, what):
                eng.dma_start(dst, src).then_inc(sem[what], 16)

            get(ident, A["c_ident"], "consts")
            get(ones, A["c_ones"][:, 0:4], "consts")
            get(m["rope"].rearrange("p (t c) -> p t c", t=2), A["c_rope"].rearrange("(t p) c -> p t c", p=P), "consts")
            get(m["window"], A["c_window"], "consts")
            get(m["slots"], A["c_slots"], "consts")
            get(SEQDFT, A["c_seq_dft"].rearrange("(k p) n -> p k n", p=P), "consts")
            get(HDFT, A["c_head_dft"], "consts")
            get(X[:, 0:2, :], A["x"][0].rearrange("(t p) n -> p t n", p=P), "consts")
            get(X[:, 2:4, :], A["ctx"][0].rearrange("(t p) n -> p t n", p=P), "consts")
            rpb = A["na_rpb"]
            for l in range(DEPTH):
                for h in range(HEADS):
                    at = ((l * HEADS + h) * 15 + 4) * 31 + 15 - (GRID_W - 1)
                    src = bass.AP(rpb.tensor, at, [[31, 7], [0, GRID_W], [1, BAND]])
                    get(band[l, h], src, "band_out")
            for l in range(DEPTH):
                if l:
                    nc.gpsimd.wait_ge(sem["x_ready"], gp.due("x_ready", 2))
                def rows(at, src):
                    get(ROWS[at:at + src.shape[0], :], src, "smalls")
                rows(0, A["norm1_g"][l].rearrange("(k p) -> k p", p=P))
                rows(8, A["norm2_g"][l].rearrange("(k p) -> k p", p=P))
                rows(16, A["head_out_g"][l].rearrange("(k p) -> k p", p=P))
                rows(24, A["sgu_b"][l])
                rows(28, A["c"][0].rearrange("(k p) -> k p", p=P))
                rows(36, A["c_ctx"].rearrange("(k p) -> k p", p=P))
                get(ADAB[0:2, :], A["ada_b"][l].partition_broadcast(2), "smalls")
                get(SGU, A["sgu_w"][l].rearrange("h p q -> p h q"), "smalls")
                at = 0
                for name in ("diff_qn_g", "diff_kn_g", "na_qn_g", "na_kn_g"):
                    w = A[name].shape[1]
                    get(m["gains_qk"][:, at:at + w], A[name][l].partition_broadcast(P), "smalls")
                    at += w
                get(m["lam_rows"], A["diff_lambda"][l].rearrange("a b -> (a b)").partition_broadcast(P), "smalls")
                get(RW, A["router_w"][l].rearrange("(k p) e -> p k e", p=P), "smalls")
                if l == 0:
                    nc.gpsimd.wait_ge(sem["band_out"], gp.due("band_out", 16 * DEPTH * HEADS))
                for h in range(HEADS):
                    for r in range(4):
                        at = ((l * HEADS + h) * 7 + 3 - r) * GRID_W * BAND + GRID_W - 1
                        src = bass.AP(band.tensor, at, [[BAND - 1, GRID_W], [GRID_W * BAND, 4], [1, GRID_W]])
                        p0 = (r % 2) * GRID_W
                        dst = BIAS[p0:p0 + GRID_W, r // 2, h, :].rearrange("p (a b) -> p a b", a=4)
                        get(dst, src, "bias_in")
                for j in (4, 5, 10, 11):
                    nc.gpsimd.wait_ge(sem["row_ready"], gp.due("row_ready"))
                    g, c = (0 if j < 6 else 1), j % 2
                    eng.dma_start(gate_scratch[l, g, :, c * CN:(c + 1) * CN], ROWBUF[0:2, j % 3, :]
                                  ).then_inc(sem["row_saved"], 16)
                gp.local["row_saved"] += 48
                nc.gpsimd.wait_ge(sem["row_saved"], gp.due("row_saved", 16))
                nc.gpsimd.wait_ge(sem["bias_used"], gp.due("bias_used"))
                for s in streams(l):
                    get(GATE1[:, s, :], gate_scratch[l, 0, s, :].partition_broadcast(P), "gate1_in")
                ns = len(streams(l))
                nc.gpsimd.wait_ge(sem["xg_ready"], gp.due("xg_ready"))
                if l == 0:
                    for j in range(2):
                        eng.memset(XGC[:, j, :, :], 0.0).then_inc(sem["xg_used"], 1)
                        nc.gpsimd.wait_ge(sem["xg_used"], gp.due("xg_used"))
                    gp.local["xg_used"] -= 2
                with gp.loop(4, expert_turn(ns)) as g:
                    for e in range(4):
                        nc.gpsimd.wait_ge(sem["xg_used"], gp.due("xg_used"))
                        eng.tensor_copy(
                            XGC[:, e % 2, :, 0:32 * ns],
                            m["proj"][:, 0:8192].rearrange("p (k e c) -> p k (e c)", k=KT, e=N_EXP)
                            [:, :, bass.ds(g * (4 * 64) + e * 64, 32 * ns)]).then_inc(sem["xgc_ready"], 1)
                        nc.gpsimd.wait_ge(sem["xgc_ready"], gp.due("xgc_ready"))
                nc.gpsimd.wait_ge(sem["moe_done"], gp.due("moe_done"))
                for s in streams(l):
                    get(GATE2[:, s, :], gate_scratch[l, 1, s, :].partition_broadcast(P), "gate2_in")
            for l in range(DEPTH):
                nc.gpsimd.wait_ge(sem["x_ready"], gp.due("x_ready", 2 if l == 0 else 1))
                if l == 0:
                    get(CAUSAL, A["c_causal_t"], "smalls2")
                    get(STRICT, A["c_strict_t"], "smalls2")
                    get(m2["levels"], A["c_levels"], "smalls2")
                    get(PICK[:, 0:31], A["c_pick"], "smalls2")
                get(m2["rows"][0:96, :], A["conv_w_2"][l].rearrange("i (t p) -> (i t) p", p=P), "smalls2")
                get(m2["rows"][96:104, :], A["g_mlstm_norm_2"][l].rearrange("(k p) -> k p", p=P), "smalls2")
                get(m2["rows"][104:105, :], A["g_gdn_norm_2"][l:l + 1, :], "smalls2")
                get(WG[:, :, 0:8], A["w_in_2"][l, :, W2_I:W2_I + 8].rearrange("(k p) n -> p k n", p=P), "smalls2")
                get(WG[:, :, 8:24], A["w_in_2"][l, :, W2_BETA:W2_BETA + 16].rearrange("(k p) n -> p k n", p=P), "smalls2")
                for i, (name, n) in enumerate((("b_igate_2", 4), ("b_fgate_2", 4), ("dt_bias_2", 8), ("a_log_2", 8))):
                    get(VEC[0:n, i:i + 1], A[name][l].rearrange("(n a) -> n a", a=1), "smalls2")
                nc.gpsimd.wait_ge(sem["heads_done"], gp.due("heads_done"))
                for i, name in enumerate(("ln1_g_2", "ln1_b_2", "ln2_g_2", "ln2_b_2")):
                    get(LNG[:, i, :], A[name][l].partition_broadcast(P), "ln_gains")
            nc.gpsimd.wait_ge(sem["x_ready"], gp.due("x_ready"))
            eng.dma_start(out[0].rearrange("(t p) n -> p t n", p=P), X2).then_inc(sem["out_done"], 16)
            nc.gpsimd.wait_ge(sem["out_done"], gp.due("out_done", 16))

        chunks, held, pending = [0], [0], [0]

        def next_chunk():
            q = chunks[0]
            chunks[0] += 1
            nc.tensor.wait_ge(sem[f"chunk{q % RING}"], pe.due(f"chunk{q % RING}", 16))
            pending[0] = held[0]
            held[0] = 1
            return slot[q % RING]

        def release(ins):
            ins.then_inc(sem["chunk_used"], 1)
            held[0] = pending[0] = 0

        def product(o, lhs, rhs, kt, start=True, stop=True):
            for k in range(kt):
                last = mm(o, lhs(k), rhs(k), start=start and k == 0, stop=stop and k == kt - 1)
                if pending[0]:
                    last.then_inc(sem["chunk_used"], 1)
                    pending[0] = 0
            return last

        def pe_turn_tiles(src, nt):
            done = []
            for k in range(KT):
                u = pe.unit()
                if u >= BANKS:
                    nc.tensor.wait_ge(free[u % BANKS], pe.uses(u - BANKS))
                for t in range(nt):
                    last = turn(U(u)[:, t * P:(t + 1) * P], src[:, t, k * P:(k + 1) * P])
                last.then_inc(full[u % BANKS], 1)
                done.append(u)
            return done

        @block.tensor
        def _(eng):
            nc.tensor.wait_ge(sem["consts"], pe.due("consts", 16 * 9))
            for l in range(DEPTH):
                ns, nt = len(streams(l)), len(tiles(l))
                nc.tensor.wait_ge(sem["smalls"], pe.due("smalls", 16 * 14))
                u = pe.unit()
                if u >= BANKS:
                    nc.tensor.wait_ge(free[u % BANKS], pe.uses(u - BANKS))
                turn(U(u)[:, 0:44], ROWS[0:44, :]).then_inc(full[u % BANKS], 1)
                u = pe.unit()
                if u >= BANKS:
                    nc.tensor.wait_ge(free[u % BANKS], pe.uses(u - BANKS))
                for h in range(HEADS):
                    last = turn(U(u)[:, h * P:(h + 1) * P], SGU[:, h, :])
                last.then_inc(full[u % BANKS], 1)
                nc.tensor.wait_ge(sem["silu_c"], pe.due("silu_c"))

                def ada(j):
                    w = next_chunk()
                    u = pe.unit()
                    if u >= BANKS:
                        nc.tensor.wait_ge(free[u % BANKS], pe.uses(u - BANKS))
                    product(U(u)[0:2, :], lambda k: SC[:, k, :], lambda k: w[:, k, :], KT).then_inc(full[u % BANKS], 1)
                    return u

                def ada_turn(j):
                    nc.tensor.wait_ge(free[rows_of[j] % BANKS], pe.uses(rows_of[j]))
                    if j // 2 not in (2, 5):
                        u = pe.unit()
                        if u >= BANKS:
                            nc.tensor.wait_ge(free[u % BANKS], pe.uses(u - BANKS))
                        for i in range(4):
                            last = turn(U(u)[:, 2 * i:2 * i + 2], ROWBUF[0:2, j % 3, i * P:(i + 1) * P])
                        last.then_inc(full[u % BANKS], 1)

                rows_of = {0: ada(0)}
                for j in range(12):
                    if j < 11:
                        rows_of[j + 1] = ada(j + 1)
                    ada_turn(j)
                nc.tensor.wait_ge(sem["xn_ready"], pe.due("xn_ready", 4))
                ht = pe_turn_tiles(XN, 4)
                for n_out in ht:
                    nc.tensor.wait_ge(free[n_out % BANKS], pe.uses(n_out))
                proj = {}
                for c, (at, n) in enumerate(PROJ_CHUNKS):
                    w = next_chunk()
                    for t in proj_tiles(l, c):
                        u = pe.unit()
                        if u >= BANKS:
                            nc.tensor.wait_ge(free[u % BANKS], pe.uses(u - BANKS))
                        product(U(u)[:, 0:n], lambda k: HT[:, k, t * P:(t + 1) * P],
                                                 lambda k: w[:, k, 0:n], KT).then_inc(full[u % BANKS], 1)
                        proj[c, t] = u
                for n_out in [u for (c, t), u in proj.items() if c == 1]:
                    nc.tensor.wait_ge(free[n_out % BANKS], pe.uses(n_out))
                first = {}
                for s in streams(l):
                    for b in range(2):
                        u = pe.unit()
                        if u >= BANKS:
                            nc.tensor.wait_ge(free[u % BANKS], pe.uses(u - BANKS))
                        for t in range(2):
                            last = mm(U(u)[:, :], PROJ[:, 2 * s + t, B_Z + b * P:B_Z + (b + 1) * P],
                                      SEQDFT[:, t, :], start=(t == 0), stop=(t == 1))
                            if held[0]:
                                release(last)
                        last.then_inc(full[u % BANKS], 1)
                        first[s, b] = u
                for s in streams(l):
                    for n_out in (first[s, 0], first[s, 1]):
                        nc.tensor.wait_ge(free[n_out % BANKS], pe.uses(n_out))
                    for t in range(2):
                        u = pe.unit()
                        if u >= BANKS:
                            nc.tensor.wait_ge(free[u % BANKS], pe.uses(u - BANKS))
                        for b in range(2):
                            for part in range(2):
                                last = mm(U(u)[:, b * P:(b + 1) * P],
                                          PT[:, s, b, part * SEQ + t * P:part * SEQ + (t + 1) * P],
                                          HDFT[:, part * P:(part + 1) * P], start=(part == 0), stop=(part == 1))
                        last.then_inc(full[u % BANKS], 1)
                for t in tiles(l):
                    nc.tensor.wait_ge(sem["vn_ready"], pe.due("vn_ready"))
                    u = pe.unit()
                    if u >= BANKS:
                        nc.tensor.wait_ge(free[u % BANKS], pe.uses(u - BANKS))
                    for h in range(HEADS):
                        last = mm(U(u)[:, h * HD:(h + 1) * HD], SGUT[:, h, :],
                                  PROJ[:, t, A_V + h * HD:A_V + (h + 1) * HD], start=True, stop=True)
                    last.then_inc(full[u % BANKS], 1)
                last_proj = [u for (c, t), u in proj.items()]
                qk = []
                for t in range(4):
                    nc.tensor.wait_ge(sem["qk_ready"], pe.due("qk_ready"))
                    for at in (C_Q, D_Q):
                        u = pe.unit()
                        if u >= BANKS:
                            nc.tensor.wait_ge(free[u % BANKS], pe.uses(u - BANKS))
                        for b in range(4):
                            last = turn(U(u)[:, b * P:(b + 1) * P], PROJ[:, t, at + b * P:at + (b + 1) * P])
                        last.then_inc(full[u % BANKS], 1)
                        qk.append(u)
                for n_out in qk:
                    nc.tensor.wait_ge(free[n_out % BANKS], pe.uses(n_out))

                todo = jobs(l)

                def keys(t):
                    return (0, 512) if t < 2 else (SEQ, SEQ)

                def scores(i):
                    kind, t, h = todo[i]
                    k0, nk = keys(t)
                    for q in range(2 if kind == "C" else 1):
                        w = DIFF_D if kind == "C" else HD
                        r = (h % 2) * HD + q * DIFF_D
                        T = QKT[0 if kind == "C" else 1]
                        u = pe.unit()
                        if u >= BANKS:
                            nc.tensor.wait_ge(free[u % BANKS], pe.uses(u - BANKS))
                        score_of[i] = u
                        mm(U(u)[:, 0:nk], T[r:r + w, h // 2, t * P:(t + 1) * P],
                                            T[r:r + w, 2 + h // 2, k0:k0 + nk], start=True, stop=True).then_inc(full[u % BANKS], 1)

                wt_of, score_of = {}, {}

                def turn_weights(i):
                    kind, t, h = todo[i]
                    k0, nk = keys(t)
                    if kind == "C":
                        nc.tensor.wait_ge(sem["w_diff"], pe.due("w_diff"))
                    else:
                        nc.tensor.wait_ge(free[score_of[i] % BANKS], pe.uses(score_of[i]))
                    u = pe.unit()
                    if u >= BANKS:
                        nc.tensor.wait_ge(free[u % BANKS], pe.uses(u - BANKS))
                    for b in range(nk // P):
                        last = turn(U(u)[:, b * P:(b + 1) * P], W[:, i % 2, b * P:(b + 1) * P])
                    last.then_inc(full[u % BANKS], 1)
                    wt_of[i] = u

                def values(i):
                    kind, t, h = todo[i]
                    k0, nk = keys(t)
                    v = (C_V if kind == "C" else D_V) + h * HD
                    nc.tensor.wait_ge(free[wt_of[i] % BANKS], pe.uses(wt_of[i]))
                    u = pe.unit()
                    if u >= BANKS:
                        nc.tensor.wait_ge(free[u % BANKS], pe.uses(u - BANKS))
                    for b in range(nk // P):
                        last = mm(U(u)[:, 0:HD], WT[:, i % 2, b * P:(b + 1) * P],
                                  PROJ[:, k0 // P + b, v:v + HD], start=(b == 0), stop=(b == nk // P - 1))
                    last.then_inc(full[u % BANKS], 1)

                n = len(todo)
                scores(0)
                for i in range(n):
                    if i + 1 < n:
                        scores(i + 1)
                    turn_weights(i)
                    if i:
                        values(i - 1)
                values(n - 1)
                nc.tensor.wait_ge(sem["xn_ready"], pe.due("xn_ready", nt))
                ht = pe_turn_tiles(XN, nt)
                for n_out in ht:
                    nc.tensor.wait_ge(free[n_out % BANKS], pe.uses(n_out))
                for c in range(2):
                    w = next_chunk()
                    for t in tiles(l):
                        u = pe.unit()
                        if u >= BANKS:
                            nc.tensor.wait_ge(free[u % BANKS], pe.uses(u - BANKS))
                        product(U(u)[:, :], lambda k: HT[:, k, t * P:(t + 1) * P],
                                                 lambda k: w[:, k, :], KT).then_inc(full[u % BANKS], 1)
                nc.tensor.wait_ge(sem["xn_ready"], pe.due("xn_ready", nt))
                ht = pe_turn_tiles(XN, nt)
                for n_out in ht:
                    nc.tensor.wait_ge(free[n_out % BANKS], pe.uses(n_out))
                u = pe.unit()
                if u >= BANKS:
                    nc.tensor.wait_ge(free[u % BANKS], pe.uses(u - BANKS))
                for t in tiles(l):
                    for k in range(KT):
                        last = mm(U(u)[:, t * N_EXP:(t + 1) * N_EXP], HT[:, k, t * P:(t + 1) * P], RW[:, k, :],
                                  start=(k == 0), stop=(k == KT - 1))
                last.then_inc(full[u % BANKS], 1)
                nc.tensor.wait_ge(sem["aff_ready"], pe.due("aff_ready"))
                u = pe.unit()
                if u >= BANKS:
                    nc.tensor.wait_ge(free[u % BANKS], pe.uses(u - BANKS))
                for t in tiles(l):
                    last = turn(U(u)[0:N_EXP, t * P:(t + 1) * P], AFF[:, t, :])
                last.then_inc(full[u % BANKS], 1)
                nc.tensor.wait_ge(sem["rank_ready"], pe.due("rank_ready"))
                u = pe.unit()
                if u >= BANKS:
                    nc.tensor.wait_ge(free[u % BANKS], pe.uses(u - BANKS))
                for t in tiles(l):
                    last = turn(U(u)[:, t * N_EXP:(t + 1) * N_EXP], RANK[0:N_EXP, t * P:(t + 1) * P])
                last.then_inc(full[u % BANKS], 1)
                nc.tensor.wait_ge(sem["sel_ready"], pe.due("sel_ready", nt))
                for k in range(KT):
                    for s in streams(l):
                        u = pe.unit()
                        if u >= BANKS:
                            nc.tensor.wait_ge(free[u % BANKS], pe.uses(u - BANKS))
                        for t in range(2):
                            last = mm(U(u)[:, :], XN[:, 2 * s + t, k * P:(k + 1) * P],
                                      SEL[:, 2 * s + t, :, :].rearrange("p e c -> p (e c)"),
                                      start=(t == 0), stop=(t == 1))
                        last.then_inc(full[u % BANKS], 1)
                for t in tiles(l):
                    nc.tensor.wait_ge(sem["selg_ready"], pe.due("selg_ready"))
                    u = pe.unit()
                    if u >= BANKS:
                        nc.tensor.wait_ge(free[u % BANKS], pe.uses(u - BANKS))
                    for b in range(4):
                        last = turn(U(u)[:, b * P:(b + 1) * P],
                                    SEL[:, t, 4 * b:4 * b + 4, :].rearrange("p e c -> p (e c)"))
                    last.then_inc(full[u % BANKS], 1)
                M = 32 * ns
                with pe.loop(4, expert_turn(ns)) as g:
                    for e in range(4):
                        nc.tensor.wait_ge(sem["xgc_ready"], pe.due("xgc_ready"))
                        ups, halves = [], []
                        for c in range(2):
                            for w_i in range(2):
                                w = next_chunk()
                                u = pe.unit()
                                if u >= BANKS:
                                    nc.tensor.wait_ge(free[u % BANKS], pe.uses(u - BANKS))
                                product(U(u)[0:M, :], lambda k: XGC[:, e % 2, k, 0:M],
                                                         lambda k: w[:, k, :], KT).then_inc(full[u % BANKS], 1)
                            ups.append(u)
                        for c in range(2):
                            nc.tensor.wait_ge(free[ups[c] % BANKS], pe.uses(ups[c]))
                            u = pe.unit()
                            if u >= BANKS:
                                nc.tensor.wait_ge(free[u % BANKS], pe.uses(u - BANKS))
                            for i in range(4):
                                last = mm(U(u)[:, i * M:(i + 1) * M], HID[0:M, c, i * P:(i + 1) * P],
                                          ident[0:M, 0:M], start=True, stop=True)
                                if c == 0 and i == 0:
                                    last.then_inc(sem["xg_used"], 1)
                            last.then_inc(full[u % BANKS], 1)
                            halves.append(u)
                        for n_out in halves:
                            nc.tensor.wait_ge(free[n_out % BANKS], pe.uses(n_out))
                        for c in range(2):
                            w = next_chunk()
                            u = pe.unit()
                            if u >= BANKS:
                                nc.tensor.wait_ge(free[u % BANKS], pe.uses(u - BANKS))
                            product(U(u)[0:M, :], lambda k: HIDT[:, k, 0:M],
                                                     lambda k: w[:, k, :], KT).then_inc(full[u % BANKS], 1)
                nc.tensor.wait_ge(sem["moe_done"], pe.due("moe_done"))
                for c in range(2):
                    for t in tiles(l):
                        s = t // 2
                        u = pe.unit()
                        if u >= BANKS:
                            nc.tensor.wait_ge(free[u % BANKS], pe.uses(u - BANKS))
                        for b in range(4):
                            last = mm(U(u)[:, :], SELT[:, s, b, (t % 2) * P:(t % 2 + 1) * P],
                                      OEXP[s][:, b, c * CN:(c + 1) * CN], start=(b == 0), stop=(b == 3))
                            if held[0]:
                                release(last)
                        last.then_inc(full[u % BANKS], 1)
            def across(row, n):
                return ident[0:n, row:row + 1].broadcast_to([n, P])

            def by_features(tiles_n):
                w = next_chunk()
                us = []
                for j in range(0, tiles_n, 2):
                    u = pe.unit()
                    if u >= BANKS:
                        nc.tensor.wait_ge(free[u % BANKS], pe.uses(u - BANKS))
                    for c in range(2):
                        last = product(U(u)[:, c * SEQ:(c + 1) * SEQ], lambda k: w[:, k, (j + c) * P:(j + c + 1) * P],
                                       lambda k: XT2[:, k, :], KT)
                    last.then_inc(full[u % BANKS], 1)
                    us.append(u)
                return us

            def by_tokens(T, n_chunks=2):
                us = []
                for c in range(n_chunks):
                    w = next_chunk()
                    for t in range(2):
                        u = pe.unit()
                        if u >= BANKS:
                            nc.tensor.wait_ge(free[u % BANKS], pe.uses(u - BANKS))
                        product(U(u)[:, :], lambda k: T[:, k, t * P:(t + 1) * P],
                                                 lambda k: w[:, k, :], KT).then_inc(full[u % BANKS], 1)
                        us.append(u)
                return us

            for l in range(DEPTH):
                nc.tensor.wait_ge(sem["smalls2"], pe.due("smalls2", 16 * (13 if l == 0 else 9)))
                u = pe.unit()
                if u >= BANKS:
                    nc.tensor.wait_ge(free[u % BANKS], pe.uses(u - BANKS))
                turn(U(u)[:, 0:105], m2["rows"][0:105, :]).then_inc(full[u % BANKS], 1)
                if l:
                    nc.tensor.wait_ge(sem["x_ready"], pe.due("x_ready", 1))
                else:
                    nc.tensor.wait_ge(sem["x_ready"], pe.due("x_ready", 4))
                turn_pairs(X2)
                u = pe.unit()
                if u >= BANKS:
                    nc.tensor.wait_ge(free[u % BANKS], pe.uses(u - BANKS))
                for i in range(2):
                    last = product(U(u)[0:4, i * SEQ:(i + 1) * SEQ], lambda k: WG[:, k, 4 * i:4 * i + 4],
                                   lambda k: XT2[:, k, :], KT)
                last.then_inc(full[u % BANKS], 1)
                qk = by_features(4) + by_features(4)
                va = by_tokens(XT2) 
                by_tokens(XT2)
                nc.tensor.wait_ge(sem["mg_rows"], pe.due("mg_rows"))
                nc.tensor.wait_ge(sem["mg_en"], pe.due("mg_en"))
                u = pe.unit()
                if u >= BANKS:
                    nc.tensor.wait_ge(free[u % BANKS], pe.uses(u - BANKS))
                for i, r in enumerate((4, 6)):
                    for t in range(2):
                        last = turn(U(u)[:, 8 * i + 4 * t:8 * i + 4 * t + 4], GR[0:4, r, t * P:(t + 1) * P])
                last.then_inc(full[u % BANKS], 1)
                for n_out in qk:
                    nc.tensor.wait_ge(free[n_out % BANKS], pe.uses(n_out))
                for pair in range(2):
                    u = pe.unit()
                    if u >= BANKS:
                        nc.tensor.wait_ge(free[u % BANKS], pe.uses(u - BANKS))
                    for j in range(2):
                        last = mm(U(u)[:, j * SEQ:(j + 1) * SEQ], across(2 * pair + j, 4), GR[0:4, 5, :],
                                  start=True, stop=True)
                    last.then_inc(full[u % BANKS], 1)
                    scored = []
                    for j in range(2):
                        h = 2 * pair + j
                        u = pe.unit()
                        if u >= BANKS:
                            nc.tensor.wait_ge(free[u % BANKS], pe.uses(u - BANKS))
                        mm(U(u)[:, 0:SEQ], KA[:, h, 0:P], QA[:, h, :], start=True, stop=True)
                        mm(U(u)[:, SEQ:SEQ + P], KA[:, h, P:SEQ], QA[:, h, P:SEQ], start=True, stop=True).then_inc(full[u % BANKS], 1)
                        scored.append(u)
                    for n_out in va:
                        nc.tensor.wait_ge(free[n_out % BANKS], pe.uses(n_out))
                    for j in range(2):
                        h = 2 * pair + j
                        nc.tensor.wait_ge(free[scored[j] % BANKS], pe.uses(scored[j]))
                        u = pe.unit()
                        if u >= BANKS:
                            nc.tensor.wait_ge(free[u % BANKS], pe.uses(u - BANKS))
                        mm(U(u)[:, 0:257], PA[:, h, 0:P], VA[:, 0, h, :], start=True, stop=True).then_inc(full[u % BANKS], 1)
                        u = pe.unit()
                        if u >= BANKS:
                            nc.tensor.wait_ge(free[u % BANKS], pe.uses(u - BANKS))
                        mm(U(u)[:, 0:257], PA[:, h, P:SEQ], VA[:, 0, h, :], start=True, stop=False)
                        mm(U(u)[:, 0:257], PA[:, h, SEQ:SEQ + P], VA[:, 1, h, :], start=False, stop=True).then_inc(full[u % BANKS], 1)
                nc.tensor.wait_ge(sem["ha_ready"], pe.due("ha_ready", 2))
                turn_pairs(HA)
                u = pe.unit()
                if u >= BANKS:
                    nc.tensor.wait_ge(free[u % BANKS], pe.uses(u - BANKS))
                for i in range(2):
                    last = product(U(u)[0:8, i * SEQ:(i + 1) * SEQ], lambda k: WG[:, k, 8 + 8 * i:16 + 8 * i],
                                   lambda k: XT2[:, k, :], KT)
                last.then_inc(full[u % BANKS], 1)
                for i in range(6):
                    by_features(4)
                u = pe.unit()
                if u >= BANKS:
                    nc.tensor.wait_ge(free[u % BANKS], pe.uses(u - BANKS))
                for r in range(16):
                    if r % 2 == 0:
                        nc.tensor.wait_ge(sem["sq_ready"], pe.due("sq_ready"))
                    last = mm(U(u)[0:16, 0:SEQ], PICK[:, 15 - r:31 - r],
                              SCR2[:, 1024 + 512 * (r // 2 % 2) + SEQ * (r % 2):1024 + 512 * (r // 2 % 2) + SEQ * (r % 2) + SEQ],
                              start=(r == 0), stop=(r == 15))
                    if r % 2 and r < 15:
                        last.then_inc(sem["sq_used"], 1)
                last.then_inc(full[u % BANKS], 1)
                nc.tensor.wait_ge(sem["rn_ready"], pe.due("rn_ready"))
                units = []
                for r in range(0, 16, 2):
                    u = pe.unit()
                    if u >= BANKS:
                        nc.tensor.wait_ge(free[u % BANKS], pe.uses(u - BANKS))
                    for j in range(2):
                        last = mm(U(u)[:, j * SEQ:(j + 1) * SEQ], across(r + j, 16), R16[0:16, :], start=True, stop=True)
                    last.then_inc(full[u % BANKS], 1)
                    units.append(u)
                for n_out in units:
                    nc.tensor.wait_ge(free[n_out % BANKS], pe.uses(n_out))
                nc.tensor.wait_ge(sem["bg_rows"], pe.due("bg_rows"))
                u = pe.unit()
                if u >= BANKS:
                    nc.tensor.wait_ge(free[u % BANKS], pe.uses(u - BANKS))
                for i, (r, t) in enumerate(((0, 0), (0, 1), (1, 0), (1, 1), (2, 1), (3, 0))):
                    last = turn(U(u)[:, 8 * i:8 * i + 8], GR[0:8, r, t * P:(t + 1) * P])
                last.then_inc(full[u % BANKS], 1)
                nc.tensor.wait_ge(free[u % BANKS], pe.uses(u))

                for b in range(4):
                    hs = (2 * b, 2 * b + 1)
                    quad_of = [(h, c) for h in hs for c in range(2)]

                    def four(lhs, rhs, op=mm):
                        u = pe.unit()
                        if u >= BANKS:
                            nc.tensor.wait_ge(free[u % BANKS], pe.uses(u - BANKS))
                        for i in range(4):
                            last = mm(U(u)[:, i * P:(i + 1) * P], lhs(i), rhs(i), start=True, stop=True)
                        last.then_inc(full[u % BANKS], 1)
                        return u

                    def four_turned(src):
                        u = pe.unit()
                        if u >= BANKS:
                            nc.tensor.wait_ge(free[u % BANKS], pe.uses(u - BANKS))
                        for i in range(4):
                            last = turn(U(u)[:, i * P:(i + 1) * P], src(i))
                        last.then_inc(full[u % BANKS], 1)
                        return u

                    tok = lambda T: (lambda i: T[:, quad_of[i][0], quad_of[i][1] * P:(quad_of[i][1] + 1) * P])
                    for r in (4, 0):
                        u = pe.unit()
                        if u >= BANKS:
                            nc.tensor.wait_ge(free[u % BANKS], pe.uses(u - BANKS))
                        for j in range(2):
                            last = mm(U(u)[:, j * SEQ:(j + 1) * SEQ], across(hs[j], 8), GR[0:8, r, :],
                                      start=True, stop=True)
                        last.then_inc(full[u % BANKS], 1)
                    four(tok(KB), tok(QB))
                    four(tok(KB), tok(KB))
                    k_unit = four_turned(tok(KB))
                    v_unit = four_turned(tok(VB))
                    nc.tensor.wait_ge(sem["at_ready"], pe.due("at_ready"))
                    four_turned(lambda i: AT[:, i, :])
                    nc.tensor.wait_ge(sem["x0_ready"], pe.due("x0_ready"))
                    for s in range(1, 7):
                        y = four(lambda i: AT[:, i, :], lambda i: XI[:, i, :])
                        nc.tensor.wait_ge(free[y % BANKS], pe.uses(y))
                        ups = []
                        if s < 6:
                            ups.append(four(lambda i: XIT[:, i, :], lambda i: YI[:, i, :]))
                        ups.append(four(lambda i: YI[:, i, :], lambda i: XIT[:, i, :]))
                        for n_out in ups:
                            nc.tensor.wait_ge(free[n_out % BANKS], pe.uses(n_out))
                    for n_out in (k_unit, v_unit):
                        nc.tensor.wait_ge(free[n_out % BANKS], pe.uses(n_out))
                    uu = four(lambda i: XIT[:, i, :], lambda i: VX[:, i, :])
                    wt = pe.unit()
                    if wt >= BANKS:
                        nc.tensor.wait_ge(free[wt % BANKS], pe.uses(wt - BANKS))
                    for j in range(2):
                        last = mm(U(wt)[:, j * P:(j + 1) * P], KX[:, 2 * j + 1, :], XIT[:, 2 * j + 1, :], start=True, stop=True)
                    last.then_inc(full[wt % BANKS], 1)
                    nc.tensor.wait_ge(free[uu % BANKS], pe.uses(uu))
                    st = pe.unit()
                    if st >= BANKS:
                        nc.tensor.wait_ge(free[st % BANKS], pe.uses(st - BANKS))
                    for j in range(2):
                        last = mm(U(st)[:, j * P:(j + 1) * P], KX[:, 2 * j, :], UU[:, 2 * j, :], start=True, stop=True)
                    last.then_inc(full[st % BANKS], 1)
                    for n_out in (wt, st):
                        nc.tensor.wait_ge(free[n_out % BANKS], pe.uses(n_out))
                    ws = pe.unit()
                    if ws >= BANKS:
                        nc.tensor.wait_ge(free[ws % BANKS], pe.uses(ws - BANKS))
                    for j in range(2):
                        last = mm(U(ws)[:, j * P:(j + 1) * P], WTT[:, j, :], ST[:, j, :], start=True, stop=True)
                    last.then_inc(full[ws % BANKS], 1)
                    nc.tensor.wait_ge(free[ws % BANKS], pe.uses(ws))
                    u = pe.unit()
                    if u >= BANKS:
                        nc.tensor.wait_ge(free[u % BANKS], pe.uses(u - BANKS))
                    for i in range(4):
                        second = i % 2 == 1
                        last = mm(U(u)[:, i * P:(i + 1) * P], ATTN[:, i, :], UU[:, i, :], start=True, stop=not second)
                        if second:
                            last = mm(U(u)[:, i * P:(i + 1) * P], QE[:, i // 2, :], ST[:, i // 2, :], start=False, stop=True)
                    last.then_inc(full[u % BANKS], 1)
                by_tokens(XT2)
                by_tokens(XT2)
                by_tokens(HAT)
                by_tokens(XT2)
                nc.tensor.wait_ge(sem["hb_ready"], pe.due("hb_ready", 2))
                turn_pairs(HBN)
                by_tokens(XT2)
                nc.tensor.wait_ge(sem["y_ready"], pe.due("y_ready"))
                turn_pairs(SGA)
                by_tokens(HAT)
                nc.tensor.wait_ge(sem["ln_ready"], pe.due("ln_ready", 2))
                turn_pairs(X2)
                for n in FF_TILES:
                    by_features(n)
                    ffn = by_features(n)
                for n_out in ffn:
                    nc.tensor.wait_ge(free[n_out % BANKS], pe.uses(n_out))
                for c in range(2):
                    us = [pe.unit(), pe.unit()]
                    for n_out in us:
                        nc.tensor.wait_ge(free[n_out % BANKS], pe.uses(n_out - BANKS))
                    for i in range(3):
                        w = next_chunk()
                        k1 = min(FT, 8 * i + 8)
                        for t in range(2):
                            last = product(U(us[t])[:, :], lambda k: HFF[:, 8 * i + k, t * P:(t + 1) * P],
                                           lambda k: w[:, k, :], k1 - 8 * i, start=(i == 0), stop=(i == 2))
                            if i == 2:
                                last.then_inc(full[us[t] % BANKS], 1)

        def ac_roots(src, n_terms):
            return nc.scalar.activation(src, src, ACT.Sqrt, scale=1.0 / n_terms, bias=EPS)

        def ac_square_sums(nt):
            for t in range(nt):
                nc.scalar.activation(SCR[:, 0:D], X[:, t, :], ACT.Square, accum_out=SST[:, t:t + 1]).then_inc(sem["scalar_step"], 1)
                nc.scalar.wait_ge(sem["scalar_step"], ac.due("scalar_step"))
            ac_roots(SST[:, 0:nt], D).then_inc(sem["root"], 1)
            nc.scalar.wait_ge(sem["root"], ac.due("root"))

        def modulated(e, k, n, nt, gain, shift):
            u = e.unit()
            e.eng.wait_ge(full[u % BANKS], e.uses(u))
            for s in range(nt // 2):
                o, i = HT[:, k, s * SEQ:(s + 1) * SEQ], U(u)[:, s * SEQ:(s + 1) * SEQ]
                g, b = gain[:, k, s:s + 1], shift[:, k, s:s + 1]
                if e is ac:
                    ins = nc.scalar.activation(o, i, ACT.Identity, scale=g, bias=b)
                else:
                    ins = nc.vector.tensor_scalar(o, i, g, b, ALU.mult, ALU.add)
                if s == nt // 2 - 1:
                    ins.then_inc(free[u % BANKS], 1)
                    e.eng.wait_ge(free[u % BANKS], e.uses(u))
            return u

        def gathered(e, k, s):
            u = e.unit()
            e.eng.wait_ge(full[u % BANKS], e.uses(u))
            o = XG[:, k, :, 32 * s:32 * s + 32]
            i = U(u)[:, :].rearrange("p (e c) -> p e c", e=N_EXP)
            g, b = GAIN[1][:, k, s:s + 1], SHIFT[1][:, k, s:s + 1]
            if e is ac:
                nc.scalar.activation(o, i, ACT.Identity, scale=g, bias=b).then_inc(free[u % BANKS], 1)
                e.eng.wait_ge(free[u % BANKS], e.uses(u))
            else:
                nc.vector.tensor_scalar(o, i, g, b, ALU.mult, ALU.add).then_inc(free[u % BANKS], 1)
                e.eng.wait_ge(free[u % BANKS], e.uses(u))
            return u

        @block.scalar
        def _(eng):
            act = nc.scalar.activation
            nc.scalar.wait_ge(sem["consts"], ac.due("consts", 16 * 9))
            for l in range(DEPTH):
                ns, nt = len(streams(l)), len(tiles(l))
                u_cols = ac.unit()
                ac.unit()
                nc.scalar.wait_ge(free[u_cols % BANKS], ac.uses(u_cols))
                act(SC, COLS[:, 28:44].rearrange("p (s k) -> p k s", s=2), ACT.Silu).then_inc(sem["silu_c"], 1)
                nc.scalar.wait_ge(sem["silu_c"], ac.due("silu_c"))
                ac.unit(12 + 8)
                if l:
                    nc.scalar.wait_ge(sem["x_ready"], ac.due("x_ready"))
                nc.scalar.wait_ge(sem["row_saved"], ac.due("row_saved", 64))
                ac_square_sums(4)
                for k in range(KT):
                    if k % 2:
                        if k == 1:
                            nc.scalar.wait_ge(sem["lam_dot"], ac.due("lam_dot"))
                        modulated(ac, k, 4, 4, GAIN[0], SHIFT[0])
                    else:
                        ac.unit()
                for c, (at, n) in enumerate(PROJ_CHUNKS):
                    for t in proj_tiles(l, c):
                        if c == 0:
                            u = ac.unit()
                            nc.scalar.wait_ge(full[u % BANKS], ac.uses(u))
                            act(PROJ[:, t, at:at + n], U(u)[:, 0:n], ACT.Gelu_apprx_tanh).then_inc(free[u % BANKS], 1)
                            nc.scalar.wait_ge(free[u % BANKS], ac.uses(u))
                        elif t % 2:
                            u = ac.unit()
                            nc.scalar.wait_ge(full[u % BANKS], ac.uses(u))
                            nc.scalar.copy(PROJ[:, t, at:at + n], U(u)[:, 0:n]).then_inc(free[u % BANKS], 1)
                            nc.scalar.wait_ge(free[u % BANKS], ac.uses(u))
                        else:
                            ac.unit()
                act(m["lam"][:, 0:2], m["lam"][:, 0:2], ACT.Exp).then_inc(sem["lam_exp"], 1)
                nc.scalar.wait_ge(sem["lam_exp"], ac.due("lam_exp"))
                for s in streams(l):
                    for b in range(2):
                        u = ac.unit()
                        nc.scalar.wait_ge(full[u % BANKS], ac.uses(u))
                        nc.scalar.copy(PT[:, s, b, :], U(u)[:, :]).then_inc(free[u % BANKS], 1)
                        nc.scalar.wait_ge(free[u % BANKS], ac.uses(u))
                for t in tiles(l):
                    u = ac.unit()
                    nc.scalar.wait_ge(full[u % BANKS], ac.uses(u))
                    nc.scalar.copy(PROJ[:, t, B_Z:B_Z + 256], U(u)[:, 0:256]).then_inc(free[u % BANKS], 1)
                    nc.scalar.wait_ge(free[u % BANKS], ac.uses(u))
                nc.scalar.wait_ge(sem["stat"], ac.due("stat"))
                ac_roots(SS28[:, 0:nt, 0:4], HD).then_inc(sem["scalar_step"], 1)
                nc.scalar.wait_ge(sem["scalar_step"], ac.due("scalar_step"))
                ac_roots(SS28[:, :, 4:20], DIFF_D).then_inc(sem["scalar_step"], 1)
                nc.scalar.wait_ge(sem["scalar_step"], ac.due("scalar_step"))
                ac_roots(SS28[:, :, 20:28], HD).then_inc(sem["root"], 1)
                nc.scalar.wait_ge(sem["root"], ac.due("root"))
                ac.unit(nt)
                for t in range(4):
                    for T in QKT:
                        u = ac.unit()
                        nc.scalar.wait_ge(full[u % BANKS], ac.uses(u))
                        nc.scalar.copy(T[:, :, t * P:(t + 1) * P],
                                                       U(u)[:, :].rearrange("p (b n) -> p b n", b=4)).then_inc(free[u % BANKS], 1)
                        nc.scalar.wait_ge(free[u % BANKS], ac.uses(u))
                todo = jobs(l)
                n = len(todo)

                def exps(i):
                    kind, t, h = todo[i]
                    nk = 512 if t < 2 else SEQ
                    scale = (DIFF_D if kind == "C" else HD) ** -0.5
                    for q in range(2 if kind == "C" else 1):
                        u = ac.unit()
                        nc.scalar.wait_ge(full[u % BANKS], ac.uses(u))
                        nc.scalar.wait_ge(sem["row_max"], ac.due("row_max"))
                        o = EXPS[:, i % 2, q, 0:nk] if kind == "C" else W[:, i % 2, 0:nk]
                        col = 2 * (i % 2) + q
                        act(o, U(u)[:, 0:nk], ACT.Exp, scale=scale, bias=SMALL[:, col:col + 1],
                                            accum_out=SMALL[:, 4 + col:5 + col]).then_inc(free[u % BANKS], 1)
                        nc.scalar.wait_ge(free[u % BANKS], ac.uses(u))

                exps(0)
                for i in range(n):
                    if i + 1 < n:
                        exps(i + 1)
                    nk = 512 if todo[i][1] < 2 else SEQ
                    u = ac.unit()
                    nc.scalar.wait_ge(full[u % BANKS], ac.uses(u))
                    nc.scalar.copy(WT[:, i % 2, 0:nk], U(u)[:, 0:nk]).then_inc(free[u % BANKS], 1)
                    nc.scalar.wait_ge(free[u % BANKS], ac.uses(u))
                    if i:
                        ac.unit()
                ac.unit()
                nc.scalar.wait_ge(sem["stat"], ac.due("stat"))
                ac_roots(SS[:, 0:16 * nt], HD).then_inc(sem["root"], 1)
                nc.scalar.wait_ge(sem["root"], ac.due("root"))
                for k in range(KT):
                    if k % 2:
                        u = ac.unit()
                        nc.scalar.wait_ge(full[u % BANKS], ac.uses(u))
                        act(HT[:, k, 0:nt * P], U(u)[:, 0:nt * P], ACT.Copy, scale=COLS[:, 16 + k:17 + k]).then_inc(free[u % BANKS], 1)
                        nc.scalar.wait_ge(free[u % BANKS], ac.uses(u))
                    else:
                        ac.unit()
                ac.unit(2 * nt)
                nc.scalar.wait_ge(sem["x_ready"], ac.due("x_ready", 1))
                ac_square_sums(nt)
                for k in range(KT):
                    if k % 2:
                        modulated(ac, k, 4, nt, GAIN[1], SHIFT[1])
                    else:
                        ac.unit()
                ac.unit()
                nc.scalar.wait_ge(sem["logit"], ac.due("logit"))
                act(AFF[:, 0:nt, :], AFF[:, 0:nt, :], ACT.Exp).then_inc(sem["logit_exp"], 1)
                nc.scalar.wait_ge(sem["logit_exp"], ac.due("logit_exp"))
                ac.unit(2)
                for k in range(KT):
                    for s in streams(l):
                        if k % 2:
                            gathered(ac, k, s)
                        else:
                            ac.unit()
                for t in tiles(l):
                    u = ac.unit()
                    nc.scalar.wait_ge(full[u % BANKS], ac.uses(u))
                    nc.scalar.copy(SELT[:, t // 2, :, (t % 2) * P:(t % 2 + 1) * P],
                                                   U(u)[:, :].rearrange("p (b n) -> p b n", b=4)).then_inc(free[u % BANKS], 1)
                    nc.scalar.wait_ge(free[u % BANKS], ac.uses(u))
                M = 32 * ns
                with ac.loop(4, expert_turn(ns)) as g:
                    for e in range(4):
                        for c in range(2):
                            u = ac.unit()
                            nc.scalar.wait_ge(full[u % BANKS], ac.uses(u))
                            act(HID[0:M, c, :], U(u)[0:M, :], ACT.Silu).then_inc(free[u % BANKS], 1)
                            nc.scalar.wait_ge(free[u % BANKS], ac.uses(u))
                            ac.unit()
                        for c in range(2):
                            u = ac.unit()
                            nc.scalar.wait_ge(full[u % BANKS], ac.uses(u))
                            nc.scalar.copy(HIDT[:, 4 * c:4 * c + 4, 0:M],
                                                           U(u)[:, 0:4 * M].rearrange("p (k c) -> p k c", k=4)).then_inc(free[u % BANKS], 1)
                            nc.scalar.wait_ge(free[u % BANKS], ac.uses(u))
                        ac.unit(2)
                ac.unit(2 * nt)
            for l in range(DEPTH):
                u = ac.unit()
                nc.scalar.wait_ge(free[u % BANKS], ac.uses(u))
                take_pairs(ac, XT2)
                nc.scalar.wait_ge(sem["vecs_ready"], ac.due("vecs_ready"))
                u = ac.unit()
                nc.scalar.wait_ge(full[u % BANKS], ac.uses(u))
                act(GR[0:4, 0, :], U(u)[0:4, 0:SEQ], ACT.Tanh, scale=1 / NEG_B1, bias=VEC[0:4, 4:5]).then_inc(sem["scalar_step"], 1)
                nc.scalar.wait_ge(sem["scalar_step"], ac.due("scalar_step"))
                act(GR[0:4, 1, :], U(u)[0:4, SEQ:2 * SEQ], ACT.Tanh, scale=1 / NEG_B1, bias=VEC[0:4, 5:6]).then_inc(free[u % BANKS], 1)
                nc.scalar.wait_ge(free[u % BANKS], ac.uses(u))
                act(GR[0:4, 1, :], GR[0:4, 1, :], ACT.Exp, scale=-NEG_B1).then_inc(sem["scalar_step"], 1)
                nc.scalar.wait_ge(sem["scalar_step"], ac.due("scalar_step"))
                act(GR[0:4, 2, :], GR[0:4, 1, :], ACT.Ln, bias=1.0).then_inc(sem["mg_soft"], 1)
                nc.scalar.wait_ge(sem["mg_soft"], ac.due("mg_soft"))
                for T in (QA, KA):
                    for j in range(2):
                        if j:
                            u = ac.unit()
                            nc.scalar.wait_ge(full[u % BANKS], ac.uses(u))
                            nc.scalar.copy(T[:, 2 * j:2 * j + 2, :].rearrange("p h n -> p (h n)"), U(u)[:, :]).then_inc(free[u % BANKS], 1)
                            nc.scalar.wait_ge(free[u % BANKS], ac.uses(u))
                        else:
                            ac.unit()
                for c in range(2):
                    for t in range(2):
                        if t:
                            u = ac.unit()
                            nc.scalar.wait_ge(full[u % BANKS], ac.uses(u))
                            nc.scalar.copy(VA[:, t, 2 * c:2 * c + 2, 0:256],
                                                           U(u)[:, :].rearrange("p (h n) -> p h n", h=2)).then_inc(free[u % BANKS], 1)
                            nc.scalar.wait_ge(free[u % BANKS], ac.uses(u))
                        else:
                            ac.unit()
                for c in range(2):
                    for t in range(2):
                        u = ac.unit()
                        nc.scalar.wait_ge(full[u % BANKS], ac.uses(u))
                        act(OA[:, t, c * CN:(c + 1) * CN], U(u)[:, :], ACT.Sigmoid).then_inc(free[u % BANKS], 1)
                        nc.scalar.wait_ge(free[u % BANKS], ac.uses(u))
                nc.scalar.wait_ge(sem["mg_rows"], ac.due("mg_rows"))
                act(GR[0:4, 6, :], GR[0:4, 6, :], ACT.Exp, scale=-1.0).then_inc(sem["mg_en"], 1)
                nc.scalar.wait_ge(sem["mg_en"], ac.due("mg_en"))
                u = ac.unit()
                nc.scalar.wait_ge(free[u % BANKS], ac.uses(u))
                for pair in range(2):
                    ac.unit(3)
                    for j in range(2):
                        h = 2 * pair + j
                        nc.scalar.wait_ge(sem["mexp_in"], ac.due("mexp_in"))
                        act(EA[:, h, 0:SEQ], EA[:, h, 0:SEQ], ACT.Exp, bias=GC[:, h:h + 1]).then_inc(sem["scalar_step"], 1)
                        nc.scalar.wait_ge(sem["scalar_step"], ac.due("scalar_step"))
                        act(EA[:, h, SEQ:SEQ + P], EA[:, h, SEQ:SEQ + P], ACT.Exp, bias=GC[:, 4 + h:5 + h]).then_inc(sem["mexp"], 1)
                        nc.scalar.wait_ge(sem["mexp"], ac.due("mexp"))
                    ac.unit(4)
                nc.scalar.wait_ge(sem["stat"], ac.due("stat"))
                ac_roots(SS2[:, 0:8], A_DV).then_inc(sem["root"], 1)
                nc.scalar.wait_ge(sem["root"], ac.due("root"))
                take_pairs(ac, HAT, lambda k: COLS2[:, 96 + k:97 + k])
                u = ac.unit()
                nc.scalar.wait_ge(full[u % BANKS], ac.uses(u))
                act(GR[0:8, 0, :], U(u)[0:8, 0:SEQ], ACT.Exp, scale=-1.0).then_inc(sem["bg_exp"], 1)
                nc.scalar.wait_ge(sem["bg_exp"], ac.due("bg_exp"))
                nc.scalar.wait_ge(sem["bg_in"], ac.due("bg_in"))
                act(GR[0:8, 5, :], GR[0:8, 5, :], ACT.Exp, scale=-1.0).then_inc(sem["scalar_step"], 1)
                nc.scalar.wait_ge(sem["scalar_step"], ac.due("scalar_step"))
                act(GR[0:8, 5, :], GR[0:8, 5, :], ACT.Ln, bias=1.0).then_inc(sem["scalar_step"], 1)
                nc.scalar.wait_ge(sem["scalar_step"], ac.due("scalar_step"))
                act(VEC[0:8, 3:4], VEC[0:8, 3:4], ACT.Exp).then_inc(sem["bg_ln"], 1)
                nc.scalar.wait_ge(sem["bg_ln"], ac.due("bg_ln"))
                nc.scalar.wait_ge(sem["bg_cum"], ac.due("bg_cum"))
                act(GR[0:8, 2, P:SEQ], GR[0:8, 4, P:SEQ], ACT.Exp).then_inc(sem["scalar_step"], 1)
                nc.scalar.wait_ge(sem["scalar_step"], ac.due("scalar_step"))
                act(GR[0:8, 3, 0:P], GR[0:8, 4, 0:P], ACT.Exp, scale=-1.0, bias=GR[0:8, 4, P - 1:P]).then_inc(sem["bg_exp"], 1)
                nc.scalar.wait_ge(sem["bg_exp"], ac.due("bg_exp"))
                for i in range(6):
                    T = (QB, KB, VB)[i // 2]
                    for j in range(2):
                        u = ac.unit()
                        nc.scalar.wait_ge(free[u % BANKS], ac.uses(u))
                        acc = SCR2[:, 512 * (j % 2):512 * (j % 2) + 512]
                        h = 4 * (i % 2) + 2 * j
                        o = T[:, h:h + 2, :].rearrange("p h n -> p (h n)")
                        act(o, acc, ACT.Silu).then_inc(sem["conv_done"], 1)
                        nc.scalar.wait_ge(sem["conv_done"], ac.due("conv_done"))
                for j in range(8):
                    T = QB if j < 4 else KB
                    if j >= 2:
                        nc.scalar.wait_ge(sem["sq_used"], ac.due("sq_used"))
                    h = 2 * (j % 4)
                    act(SCR2[:, 1024 + 512 * (j % 2):1536 + 512 * (j % 2)],
                                            T[:, h:h + 2, :].rearrange("p h n -> p (h n)"), ACT.Square).then_inc(sem["sq_ready"], 1)
                    nc.scalar.wait_ge(sem["sq_ready"], ac.due("sq_ready"))
                ac.local["sq_used"] += 2 - 1
                u = ac.unit()
                nc.scalar.wait_ge(full[u % BANKS], ac.uses(u))
                act(R16[0:16, :], U(u)[0:16, 0:SEQ], ACT.Sqrt, bias=EPS).then_inc(free[u % BANKS], 1)
                nc.scalar.wait_ge(free[u % BANKS], ac.uses(u))
                ac.unit(8)
                u = ac.unit()
                nc.scalar.wait_ge(free[u % BANKS], ac.uses(u))
                for b in range(4):
                    u_decay = ac.unit()
                    nc.scalar.wait_ge(full[u_decay % BANKS], ac.uses(u_decay))
                    ac.unit(3)
                    nc.scalar.wait_ge(sem["e_in"], ac.due("e_in"))
                    act(EG, U(u_decay)[:, :].rearrange("p (h c n) -> p h c n", h=2, c=2)[:, :, 1, :], ACT.Exp).then_inc(free[u_decay % BANKS], 1)
                    nc.scalar.wait_ge(free[u_decay % BANKS], ac.uses(u_decay))
                    for i in range(4):
                        h, c = 2 * b + i // 2, i % 2
                        ins = act(EB[:, i, :], EB[:, i, :], ACT.Exp, bias=GC[:, 16 + 8 * c + h:17 + 8 * c + h])
                        if i == 3:
                            ins.then_inc(sem["e_exp"], 1)
                            nc.scalar.wait_ge(sem["e_exp"], ac.due("e_exp"))
                        else:
                            ins.then_inc(sem["scalar_step"], 1)
                            nc.scalar.wait_ge(sem["scalar_step"], ac.due("scalar_step"))
                    ac.unit()
                    u = ac.unit()
                    nc.scalar.wait_ge(full[u % BANKS], ac.uses(u))
                    for i in range(4):
                        h, c = 2 * b + i // 2, i % 2
                        ins = act(VX[:, i, :], U(u)[:, i * P:(i + 1) * P], ACT.Copy, scale=GC[:, 8 * c + h:8 * c + h + 1])
                        if i == 3:
                            ins.then_inc(free[u % BANKS], 1)
                            nc.scalar.wait_ge(free[u % BANKS], ac.uses(u))
                        else:
                            ins.then_inc(sem["scalar_step"], 1)
                            nc.scalar.wait_ge(sem["scalar_step"], ac.due("scalar_step"))
                    ac.unit(1 + 5 * 3 + 2)
                    u = ac.unit()
                    nc.scalar.wait_ge(full[u % BANKS], ac.uses(u))
                    nc.scalar.copy(UU, U(u)[:, :].rearrange("p (m n) -> p m n", m=4)).then_inc(free[u % BANKS], 1)
                    nc.scalar.wait_ge(free[u % BANKS], ac.uses(u))
                    for T in (WTT, ST):
                        u = ac.unit()
                        nc.scalar.wait_ge(full[u % BANKS], ac.uses(u))
                        nc.scalar.copy(T, U(u)[:, 0:SEQ].rearrange("p (m n) -> p m n", m=2)).then_inc(free[u % BANKS], 1)
                        nc.scalar.wait_ge(free[u % BANKS], ac.uses(u))
                    ac.unit(2)
                nc.scalar.wait_ge(sem["stat"], ac.due("stat"))
                ac_roots(SS2[:, 0:16], P).then_inc(sem["root"], 1)
                nc.scalar.wait_ge(sem["root"], ac.due("root"))

                def gate_units(T, func):
                    for c in range(2):
                        for t in range(2):
                            u = ac.unit()
                            nc.scalar.wait_ge(full[u % BANKS], ac.uses(u))
                            act(T[:, t, c * CN:(c + 1) * CN], U(u)[:, :], func).then_inc(free[u % BANKS], 1)
                            nc.scalar.wait_ge(free[u % BANKS], ac.uses(u))

                gate_units(ZB, ACT.Silu)
                gate_units(SGA, ACT.Sigmoid)
                ac.unit(4)
                gate_units(SGB, ACT.Sigmoid)
                take_pairs(ac, XT2, lambda k: COLS2[:, 104:105])
                ac.unit(4)
                take_pairs(ac, HAT)
                ac.unit(4)
                nc.scalar.wait_ge(sem["stat"], ac.due("stat"))
                nc.scalar.activation(SS2[:, 32:34], SS2[:, 32:34], ACT.Sqrt, bias=LN_EPS).then_inc(sem["root"], 1)
                nc.scalar.wait_ge(sem["root"], ac.due("root"))
                take_pairs(ac, XT2)
                ups = []
                for n in FF_TILES:
                    gs = []
                    for j in range(0, n, 2):
                        u = ac.unit()
                        nc.scalar.wait_ge(full[u % BANKS], ac.uses(u))
                        p = len(ups) + len(gs)
                        if p >= 4:
                            nc.scalar.wait_ge(free[ups[p - 4] % BANKS], ac.uses(ups[p - 4]))
                        gs.append(u)
                        act(SCR2[:, 512 * (p % 4):512 * (p % 4) + 512], U(u)[:, :], ACT.Silu).then_inc(free[u % BANKS], 1)
                        nc.scalar.wait_ge(free[u % BANKS], ac.uses(u))
                    for j in range(0, n, 2):
                        ups.append(ac.unit())
                ac.unit(4)
                nc.scalar.wait_ge(sem["stat"], ac.due("stat"))
                nc.scalar.activation(SS2[:, 32:34], SS2[:, 32:34], ACT.Sqrt, bias=LN_EPS).then_inc(sem["root"], 1)
                nc.scalar.wait_ge(sem["root"], ac.due("root"))

        @block.vector
        def _(eng):
            v = nc.vector
            tt, ts, stt, red = v.tensor_tensor, v.tensor_scalar, v.scalar_tensor_tensor, v.tensor_reduce
            nc.vector.wait_ge(sem["consts"], dv.due("consts", 16 * 9))

            def normed(nt):
                nc.vector.wait_ge(sem["root"], dv.due("root"))
                v.reciprocal(SST[:, 0:nt], SST[:, 0:nt]).then_inc(sem["vector_step"], 1)
                nc.vector.wait_ge(sem["vector_step"], dv.due("vector_step"))
                for t in range(nt):
                    ts(XN[:, t, :], X[:, t, :], SST[:, t:t + 1], None, ALU.mult).then_inc(sem["xn_ready"], 1)
                    nc.vector.wait_ge(sem["xn_ready"], dv.due("xn_ready"))

            def added(l, gate):
                for c in range(2):
                    for t in tiles(l):
                        cols = slice(c * CN, (c + 1) * CN)
                        u = dv.unit()
                        nc.vector.wait_ge(full[u % BANKS], dv.uses(u))
                        tt(SCR[:, 0:CN], U(u)[:, :], gate[:, t // 2, cols], ALU.mult).then_inc(free[u % BANKS], 1)
                        nc.vector.wait_ge(free[u % BANKS], dv.uses(u))
                        add = tt(X[:, t, cols], X[:, t, cols], SCR[:, 0:CN], ALU.add)
                        if c == 1 and t == tiles(l)[-1]:
                            add.then_inc(sem["x_ready"], 1)
                            nc.vector.wait_ge(sem["x_ready"], dv.due("x_ready"))
                        else:
                            add.then_inc(sem["vector_step"], 1)
                            nc.vector.wait_ge(sem["vector_step"], dv.due("vector_step"))

            for l in range(DEPTH):
                lam_init = 0.8 - 0.6 * math.exp(-0.3 * l)
                ns, nt = len(streams(l)), len(tiles(l))
                nc.vector.wait_ge(sem["smalls"], dv.due("smalls", 16 * 14))
                u = dv.unit()
                nc.vector.wait_ge(full[u % BANKS], dv.uses(u))
                v.tensor_copy(COLS, U(u)[:, 0:44]).then_inc(free[u % BANKS], 1)
                nc.vector.wait_ge(free[u % BANKS], dv.uses(u))
                u = dv.unit()
                nc.vector.wait_ge(full[u % BANKS], dv.uses(u))
                v.tensor_copy(m["sgu_t"], U(u)[:, :]).then_inc(free[u % BANKS], 1)
                nc.vector.wait_ge(free[u % BANKS], dv.uses(u))
                ts(COLS[:, 20:22], COLS[:, 20:22], 1.0 - lam_init, None, ALU.mult).then_inc(sem["vector_step"], 1)
                nc.vector.wait_ge(sem["vector_step"], dv.due("vector_step"))

                def row(j):
                    u = dv.unit()
                    nc.vector.wait_ge(full[u % BANKS], dv.uses(u))
                    if j == 7:
                        nc.vector.wait_ge(sem["row_saved"], dv.due("row_saved", 32))
                    o, b = ROWBUF[0:2, j % 3, :], ADAB[0:2, j * CN:(j + 1) * CN]
                    if j // 2 in (2, 5):
                        v.tensor_copy(o, U(u)[0:2, :]).then_inc(free[u % BANKS], 1)
                        nc.vector.wait_ge(free[u % BANKS], dv.uses(u))
                        tt(o, o, b, ALU.add).then_inc(sem["row_ready"], 1)
                        nc.vector.wait_ge(sem["row_ready"], dv.due("row_ready"))
                    else:
                        tt(o, U(u)[0:2, :], b, ALU.add).then_inc(free[u % BANKS], 1)
                        nc.vector.wait_ge(free[u % BANKS], dv.uses(u))

                row(0)
                for j in range(12):
                    if j < 11:
                        row(j + 1)
                    if j // 2 not in (2, 5):
                        u = dv.unit()
                        nc.vector.wait_ge(full[u % BANKS], dv.uses(u))
                        v.tensor_copy(MOD[:, 4 * j:4 * j + 4, :].rearrange("p j s -> p (j s)"),
                                                      U(u)[:, 0:8]).then_inc(free[u % BANKS], 1)
                        nc.vector.wait_ge(free[u % BANKS], dv.uses(u))
                for i, part in enumerate((1, 4)):
                    g = COLS[:, 8 * i:8 * i + 8]
                    stt(GAIN[i], MOD[:, part * 8:part * 8 + 8, :], 1.0, bc(g, 2, [P, KT, 2]),
                                ALU.add, ALU.mult).then_inc(sem["vector_step"], 1)
                    nc.vector.wait_ge(sem["vector_step"], dv.due("vector_step"))
                lr = m["lam_rows"].rearrange("p (a b c) -> p a b c", a=2, b=2)
                nc.vector.wait_ge(sem["row_saved"], dv.due("row_saved", 32))
                tt(SCR[:, 1400:1464].rearrange("p (a c) -> p a c", a=2), lr[:, :, 0, :], lr[:, :, 1, :], ALU.mult).then_inc(sem["vector_step"], 1)
                nc.vector.wait_ge(sem["vector_step"], dv.due("vector_step"))
                red(m["lam"][:, 0:2], SCR[:, 1400:1464].rearrange("p (a c) -> p a c", a=2), AXX, ALU.add).then_inc(sem["lam_dot"], 1)
                nc.vector.wait_ge(sem["lam_dot"], dv.due("lam_dot"))
                normed(4)
                ht = []
                for k in range(KT):
                    ht.append(dv.unit() if k % 2 else modulated(dv, k, 4, 4, GAIN[0], SHIFT[0]))
                proj = []
                for c, (at, n) in enumerate(PROJ_CHUNKS):
                    for t in proj_tiles(l, c):
                        if c == 0 or t % 2:
                            proj.append(dv.unit())
                        else:
                            u = dv.unit()
                            nc.vector.wait_ge(full[u % BANKS], dv.uses(u))
                            v.tensor_copy(PROJ[:, t, at:at + n], U(u)[:, 0:n]).then_inc(free[u % BANKS], 1)
                            nc.vector.wait_ge(free[u % BANKS], dv.uses(u))
                for n_out in proj:
                    nc.vector.wait_ge(free[n_out % BANKS], dv.uses(n_out))
                nc.vector.wait_ge(sem["lam_exp"], dv.due("lam_exp"))
                tt(m["lam"][:, 2:3], m["lam"][:, 0:1], m["lam"][:, 1:2], ALU.subtract).then_inc(sem["vector_step"], 1)
                nc.vector.wait_ge(sem["vector_step"], dv.due("vector_step"))
                ts(m["lam"][:, 2:3], m["lam"][:, 2:3], lam_init, None, ALU.add).then_inc(sem["vector_step"], 1)
                nc.vector.wait_ge(sem["vector_step"], dv.due("vector_step"))
                nc.vector.wait_ge(sem["bias_in"], dv.due("bias_in", 256))
                bias = m["gate"].rearrange("p (a k) -> p a k", a=8)
                stt(bias, bias, float(HD ** 0.5), bc(m["window"], 1, [P, 8, SEQ]), ALU.mult, ALU.add).then_inc(sem["vector_step"], 1)
                nc.vector.wait_ge(sem["vector_step"], dv.due("vector_step"))
                u_four = dv.unit(2 * ns)
                four = [dv.unit() for t in tiles(l)]
                for t in range(4):
                    todo = [(C_Q, 512, 16, DIFF_D, 4), (D_Q, 512, 8, HD, 20)]
                    if t < nt:
                        todo.append((A_V, 256, 4, HD, 0))
                    for at, n, g, w, o in todo:
                        src = PROJ[:, t, at:at + n]
                        tt(SCR[:, 0:n], src, src, ALU.mult).then_inc(sem["vector_step"], 1)
                        nc.vector.wait_ge(sem["vector_step"], dv.due("vector_step"))
                        ins = red(SS28[:, t, o:o + g], SCR[:, 0:n].rearrange("p (g w) -> p g w", g=g), AXX, ALU.add)
                        if t == 3 and (at, n) == todo[-1][:2]:
                            ins.then_inc(sem["stat"], 1)
                            nc.vector.wait_ge(sem["stat"], dv.due("stat"))
                        else:
                            ins.then_inc(sem["vector_step"], 1)
                            nc.vector.wait_ge(sem["vector_step"], dv.due("vector_step"))
                nc.vector.wait_ge(sem["root"], dv.due("root"))
                v.reciprocal(SS28[:, 0:nt, 0:4], SS28[:, 0:nt, 0:4]).then_inc(sem["vector_step"], 1)
                nc.vector.wait_ge(sem["vector_step"], dv.due("vector_step"))
                v.reciprocal(SS28[:, :, 4:28], SS28[:, :, 4:28]).then_inc(sem["vector_step"], 1)
                nc.vector.wait_ge(sem["vector_step"], dv.due("vector_step"))
                for t in tiles(l):
                    x = PROJ[:, t, A_V:A_V + 256].rearrange("p (g w) -> p g w", g=4)
                    tt(x, x, bc(SS28[:, t, 0:4], 2, [P, 4, HD]), ALU.mult).then_inc(sem["vn_ready"], 1)
                    nc.vector.wait_ge(sem["vn_ready"], dv.due("vn_ready"))
                for t in range(4):
                    for at, g, w, o, go in ((C_Q, 16, DIFF_D, 4, 0), (D_Q, 8, HD, 20, 64)):
                        x = PROJ[:, t, at:at + 512].rearrange("p (g w) -> p g w", g=g)
                        tt(x, x, bc(SS28[:, t, o:o + g], 2, [P, g, w]), ALU.mult).then_inc(sem["vector_step"], 1)
                        nc.vector.wait_ge(sem["vector_step"], dv.due("vector_step"))
                        x4 = PROJ[:, t, at:at + 512].rearrange("p (j g w) -> p j g w", j=2, w=w)
                        gains = m["gains_qk"][:, go:go + 2 * w].rearrange("p (j w) -> p j w", j=2)
                        last = tt(x4, x4, bc(gains, 2, [P, 2, g // 2, w]), ALU.mult)
                        if at == D_Q:
                            last.then_inc(sem["qk_ready"], 1)
                            nc.vector.wait_ge(sem["qk_ready"], dv.due("qk_ready"))
                            continue
                        last.then_inc(sem["vector_step"], 1)
                        nc.vector.wait_ge(sem["vector_step"], dv.due("vector_step"))
                        if t < 2:
                            xr = PROJ[:, t, at:at + 512].rearrange("p (g r h e) -> p g r h e", g=16, r=2, h=2)
                            sr = SCR[:, 0:512].rearrange("p (g r h e) -> p g r h e", g=16, r=2, h=2)
                            sin = ROPE[:, t, 32:64].rearrange("p (r h e) -> p r h e", r=2, h=2)
                            for h in range(2):
                                tt(sr[:, :, :, h, :], xr[:, :, :, 1 - h, :],
                                           bc(sin[:, :, h, :], 1, [P, 16, 2, 8]), ALU.mult).then_inc(sem["vector_step"], 1)
                                nc.vector.wait_ge(sem["vector_step"], dv.due("vector_step"))
                            tt(x, x, bc(ROPE[:, t, 0:32], 1, [P, 16, 32]), ALU.mult).then_inc(sem["vector_step"], 1)
                            nc.vector.wait_ge(sem["vector_step"], dv.due("vector_step"))
                            tt(PROJ[:, t, at:at + 512], PROJ[:, t, at:at + 512], SCR[:, 0:512], ALU.add).then_inc(sem["vector_step"], 1)
                            nc.vector.wait_ge(sem["vector_step"], dv.due("vector_step"))
                for t in tiles(l):
                    u = dv.unit()
                    nc.vector.wait_ge(full[u % BANKS], dv.uses(u))
                    sv = SCR[:, 0:256].rearrange("p (h w) -> p h w", h=4)
                    tt(sv, U(u)[:, 0:256].rearrange("p (h w) -> p h w", h=4),
                                       bc(COLS[:, 24:28], 2, [P, 4, HD]), ALU.add).then_inc(free[u % BANKS], 1)
                    nc.vector.wait_ge(free[u % BANKS], dv.uses(u))
                    tt(PROJ[:, t, 0:256], PROJ[:, t, 0:256], SCR[:, 0:256], ALU.mult).then_inc(sem["vector_step"], 1)
                    nc.vector.wait_ge(sem["vector_step"], dv.due("vector_step"))
                dv.unit(8)
                todo = jobs(l)
                n = len(todo)
                score_of = {}

                def maxima(i):
                    kind, t, h = todo[i]
                    nk = 512 if t < 2 else SEQ
                    scale = (DIFF_D if kind == "C" else HD) ** -0.5
                    for q in range(2 if kind == "C" else 1):
                        u = dv.unit()
                        nc.vector.wait_ge(full[u % BANKS], dv.uses(u))
                        score_of[i, q] = u
                        if kind == "D" and t < 2:
                            tt(U(u)[:, 0:SEQ], U(u)[:, 0:SEQ], BIAS[:, t, h, :], ALU.add).then_inc(sem["vector_step"], 1)
                            nc.vector.wait_ge(sem["vector_step"], dv.due("vector_step"))
                        col = 2 * (i % 2) + q
                        red(SMALL[:, 8 + col:9 + col], U(u)[:, 0:nk], AXX, ALU.max).then_inc(sem["vector_step"], 1)
                        nc.vector.wait_ge(sem["vector_step"], dv.due("vector_step"))
                        ts(SMALL[:, col:col + 1], SMALL[:, 8 + col:9 + col], -scale, None, ALU.mult).then_inc(sem["row_max"], 1)
                        nc.vector.wait_ge(sem["row_max"], dv.due("row_max"))

                def weights(i):
                    kind, t, h = todo[i]
                    nk = 512 if t < 2 else SEQ
                    r = SMALL[:, 12 + 2 * (i % 3):14 + 2 * (i % 3)]
                    s = SMALL[:, 4 + 2 * (i % 2):6 + 2 * (i % 2)]
                    if kind == "D":
                        nc.vector.wait_ge(free[score_of[i, 0] % BANKS], dv.uses(score_of[i, 0]))
                        v.reciprocal(r[:, 0:1], s[:, 0:1]).then_inc(sem["vector_step"], 1)
                        nc.vector.wait_ge(sem["vector_step"], dv.due("vector_step"))
                        return
                    for n_out in (score_of[i, 0], score_of[i, 1]):
                        nc.vector.wait_ge(free[n_out % BANKS], dv.uses(n_out))
                    v.reciprocal(r, s).then_inc(sem["vector_step"], 1)
                    nc.vector.wait_ge(sem["vector_step"], dv.due("vector_step"))
                    tt(r[:, 1:2], r[:, 1:2], m["lam"][:, 2:3], ALU.mult).then_inc(sem["vector_step"], 1)
                    nc.vector.wait_ge(sem["vector_step"], dv.due("vector_step"))
                    e = EXPS[:, i % 2, :, 0:nk]
                    ts(e[:, 1, :], e[:, 1, :], r[:, 1:2], None, ALU.mult).then_inc(sem["vector_step"], 1)
                    nc.vector.wait_ge(sem["vector_step"], dv.due("vector_step"))
                    stt(W[:, i % 2, 0:nk], e[:, 0, :], r[:, 0:1], e[:, 1, :], ALU.mult, ALU.subtract).then_inc(sem["w_diff"], 1)
                    nc.vector.wait_ge(sem["w_diff"], dv.due("w_diff"))

                def values(i):
                    kind, t, h = todo[i]
                    r = SMALL[:, 12 + 2 * (i % 3):13 + 2 * (i % 3)]
                    u = dv.unit()
                    nc.vector.wait_ge(full[u % BANKS], dv.uses(u))
                    at = (C_Q if kind == "C" else D_Q) + h * HD
                    o = PROJ[:, t, at:at + HD]
                    (v.tensor_copy(o, U(u)[:, 0:HD]) if kind == "C" else
                                 ts(o, U(u)[:, 0:HD], r, None, ALU.mult)).then_inc(free[u % BANKS], 1)
                    nc.vector.wait_ge(free[u % BANKS], dv.uses(u))

                maxima(0)
                for i in range(n):
                    if i + 1 < n:
                        maxima(i + 1)
                    weights(i)
                    dv.unit()
                    if i:
                        values(i - 1)
                values(n - 1)
                v.memset(SMALL[:, 90:91], 0.0).then_inc(sem["bias_used"], 1)
                nc.vector.wait_ge(sem["bias_used"], dv.due("bias_used"))
                for n_out in four:
                    nc.vector.wait_ge(free[n_out % BANKS], dv.uses(n_out))
                segs = ((0, 0, 256), (B_Z, 256, 512), (D_Q, 768, 256))
                for t in tiles(l):
                    for at, o, w in segs:
                        src = PROJ[:, t, at:at + w]
                        tt(SCR[:, o:o + w], src, src, ALU.mult).then_inc(sem["vector_step"], 1)
                        nc.vector.wait_ge(sem["vector_step"], dv.due("vector_step"))
                    ins = red(SS[:, 16 * t:16 * t + 16], SCR[:, 0:D].rearrange("p (g w) -> p g w", g=16), AXX, ALU.add)
                    if t == nt - 1:
                        ins.then_inc(sem["stat"], 1)
                        nc.vector.wait_ge(sem["stat"], dv.due("stat"))
                    else:
                        ins.then_inc(sem["vector_step"], 1)
                        nc.vector.wait_ge(sem["vector_step"], dv.due("vector_step"))
                nc.vector.wait_ge(sem["root"], dv.due("root"))
                v.reciprocal(SS[:, 0:16 * nt], SS[:, 0:16 * nt]).then_inc(sem["vector_step"], 1)
                nc.vector.wait_ge(sem["vector_step"], dv.due("vector_step"))
                for t in tiles(l):
                    for at, o, w in segs:
                        g = w // HD
                        r = SS[:, 16 * t + o // HD:16 * t + o // HD + g]
                        ins = tt(XN[:, t, o:o + w].rearrange("p (g w) -> p g w", g=g),
                                 PROJ[:, t, at:at + w].rearrange("p (g w) -> p g w", g=g), bc(r, 2, [P, g, HD]), ALU.mult)
                        if at == D_Q:
                            ins.then_inc(sem["xn_ready"], 1)
                            nc.vector.wait_ge(sem["xn_ready"], dv.due("xn_ready"))
                        else:
                            ins.then_inc(sem["vector_step"], 1)
                            nc.vector.wait_ge(sem["vector_step"], dv.due("vector_step"))
                for k in range(KT):
                    if k % 2:
                        dv.unit()
                    else:
                        u = dv.unit()
                        nc.vector.wait_ge(full[u % BANKS], dv.uses(u))
                        ts(HT[:, k, 0:nt * P], U(u)[:, 0:nt * P], COLS[:, 16 + k:17 + k], None, ALU.mult).then_inc(free[u % BANKS], 1)
                        nc.vector.wait_ge(free[u % BANKS], dv.uses(u))
                nc.vector.wait_ge(sem["gate1_in"], dv.due("gate1_in", 16 * ns))
                added(l, GATE1)
                normed(nt)
                for k in range(KT):
                    if k % 2:
                        dv.unit()
                    else:
                        modulated(dv, k, 4, nt, GAIN[1], SHIFT[1])
                u = dv.unit()
                nc.vector.wait_ge(full[u % BANKS], dv.uses(u))
                lg = U(u)[:, 0:nt * N_EXP].rearrange("p (t e) -> p t e", t=nt)
                aff = AFF[:, 0:nt, :]
                mx = SMALL[:, 0:nt]
                red(mx, lg, AXX, ALU.max).then_inc(sem["vector_step"], 1)
                nc.vector.wait_ge(sem["vector_step"], dv.due("vector_step"))
                tt(aff, lg, bc(mx, 2, [P, nt, N_EXP]), ALU.subtract).then_inc(free[u % BANKS], 1)
                nc.vector.wait_ge(free[u % BANKS], dv.uses(u))
                v.memset(SMALL[:, 90:91], 0.0).then_inc(sem["logit"], 1)
                nc.vector.wait_ge(sem["logit"], dv.due("logit"))
                nc.vector.wait_ge(sem["logit_exp"], dv.due("logit_exp"))
                red(mx, aff, AXX, ALU.add).then_inc(sem["vector_step"], 1)
                nc.vector.wait_ge(sem["vector_step"], dv.due("vector_step"))
                v.reciprocal(mx, mx).then_inc(sem["vector_step"], 1)
                nc.vector.wait_ge(sem["vector_step"], dv.due("vector_step"))
                tt(aff, aff, bc(mx, 2, [P, nt, N_EXP]), ALU.mult).then_inc(sem["aff_ready"], 1)
                nc.vector.wait_ge(sem["aff_ready"], dv.due("aff_ready"))
                u = dv.unit()
                nc.vector.wait_ge(full[u % BANKS], dv.uses(u))
                n = nt * P
                v.tensor_copy(AFFT[0:N_EXP, 0:n], U(u)[0:N_EXP, 0:n]).then_inc(sem["vector_step"], 1)
                nc.vector.wait_ge(sem["vector_step"], dv.due("vector_step"))
                v.tensor_copy(WORK[0:N_EXP, 0:n], U(u)[0:N_EXP, 0:n]).then_inc(free[u % BANKS], 1)
                nc.vector.wait_ge(free[u % BANKS], dv.uses(u))
                for s in streams(l):
                    wk = WORK[0:N_EXP, s * SEQ:(s + 1) * SEQ]
                    top = SMALL[0:N_EXP, 16:24]
                    for i in range(CAP // 8):
                        v.max(top, wk).then_inc(sem["vector_step"], 1)
                        nc.vector.wait_ge(sem["vector_step"], dv.due("vector_step"))
                        v.match_replace(wk, top, wk, -1.0).then_inc(sem["vector_step"], 1)
                        nc.vector.wait_ge(sem["vector_step"], dv.due("vector_step"))
                wk = WORK[0:N_EXP, 0:n]
                tt(wk, wk, AFFT[0:N_EXP, 0:n], ALU.not_equal).then_inc(sem["vector_step"], 1)
                nc.vector.wait_ge(sem["vector_step"], dv.due("vector_step"))
                for s in streams(l):
                    cols = slice(s * SEQ, (s + 1) * SEQ)
                    v.tensor_tensor_scan(RANK[0:N_EXP, cols], ones[0:N_EXP, 0:1].broadcast_to([N_EXP, SEQ]),
                                                 WORK[0:N_EXP, cols], 0.0, ALU.mult, ALU.add).then_inc(sem["vector_step"], 1)
                    nc.vector.wait_ge(sem["vector_step"], dv.due("vector_step"))
                tt(RANK[0:N_EXP, 0:n], RANK[0:N_EXP, 0:n], wk, ALU.mult).then_inc(sem["rank_ready"], 1)
                nc.vector.wait_ge(sem["rank_ready"], dv.due("rank_ready"))
                u = dv.unit()
                nc.vector.wait_ge(full[u % BANKS], dv.uses(u))
                v.tensor_copy(POS[:, 0:nt, :], U(u)[:, 0:nt * N_EXP].rearrange("p (t e) -> p t e", t=nt)).then_inc(free[u % BANKS], 1)
                nc.vector.wait_ge(free[u % BANKS], dv.uses(u))
                for t in tiles(l):
                    tt(SEL[:, t, :, :], bc(m["slots"], 1, [P, N_EXP, CAP]),
                                            bc(POS[:, t, :], 2, [P, N_EXP, CAP]), ALU.is_equal).then_inc(sem["sel_ready"], 1)
                    nc.vector.wait_ge(sem["sel_ready"], dv.due("sel_ready"))
                gat = []
                for k in range(KT):
                    for s in streams(l):
                        gat.append(dv.unit() if k % 2 else gathered(dv, k, s))
                for n_out in gat:
                    nc.vector.wait_ge(free[n_out % BANKS], dv.uses(n_out))
                v.memset(SMALL[:, 90:91], 0.0).then_inc(sem["xg_ready"], 1)
                nc.vector.wait_ge(sem["xg_ready"], dv.due("xg_ready"))
                for t in tiles(l):
                    tt(SEL[:, t, :, :], SEL[:, t, :, :], bc(AFF[:, t, :], 2, [P, N_EXP, CAP]), ALU.mult).then_inc(sem["selg_ready"], 1)
                    nc.vector.wait_ge(sem["selg_ready"], dv.due("selg_ready"))
                selt = [dv.unit() for t in tiles(l)]
                for n_out in selt:
                    nc.vector.wait_ge(free[n_out % BANKS], dv.uses(n_out))
                M = 32 * ns
                with dv.loop(4, expert_turn(ns)) as g:
                    for e in range(4):
                        for c in range(2):
                            gate_unit = dv.unit()
                            u = dv.unit()
                            nc.vector.wait_ge(full[u % BANKS], dv.uses(u))
                            nc.vector.wait_ge(free[gate_unit % BANKS], dv.uses(gate_unit))
                            tt(HID[0:M, c, :], U(u)[0:M, :], HID[0:M, c, :], ALU.mult).then_inc(free[u % BANKS], 1)
                            nc.vector.wait_ge(free[u % BANKS], dv.uses(u))
                        dv.unit(2)
                        for c in range(2):
                            u = dv.unit()
                            nc.vector.wait_ge(full[u % BANKS], dv.uses(u))
                            for s in streams(l):
                                o = [m["ht"], m["xn"]][s][32 * e:32 * e + 32, bass.ds(g * D + c * CN, CN)]
                                ins = v.tensor_copy(o, U(u)[32 * s:32 * s + 32, :])
                                if s == ns - 1:
                                    ins.then_inc(free[u % BANKS], 1)
                                    nc.vector.wait_ge(free[u % BANKS], dv.uses(u))
                                else:
                                    ins.then_inc(sem["vector_step"], 1)
                                    nc.vector.wait_ge(sem["vector_step"], dv.due("vector_step"))
                v.memset(SMALL[:, 90:91], 0.0).then_inc(sem["moe_done"], 1)
                nc.vector.wait_ge(sem["moe_done"], dv.due("moe_done"))
                nc.vector.wait_ge(sem["gate2_in"], dv.due("gate2_in", 16 * ns))
                added(l, GATE2)

            def layer_norm(first):
                for t in range(2):
                    for c in range(2):
                        v.bn_stats(SS2[:, 40 + 6 * c:46 + 6 * c], X2[:, t, c * CN:(c + 1) * CN]).then_inc(sem["vector_step"], 1)
                        nc.vector.wait_ge(sem["vector_step"], dv.due("vector_step"))
                    v.bn_aggr(SS2[:, 34 + 2 * t:36 + 2 * t], SS2[:, 40:52]).then_inc(sem["vector_step"], 1)
                    nc.vector.wait_ge(sem["vector_step"], dv.due("vector_step"))
                    ins = v.tensor_copy(SS2[:, 32 + t:33 + t], SS2[:, 35 + 2 * t:36 + 2 * t])
                    if t:
                        ins.then_inc(sem["stat"], 1)
                        nc.vector.wait_ge(sem["stat"], dv.due("stat"))
                    else:
                        ins.then_inc(sem["vector_step"], 1)
                        nc.vector.wait_ge(sem["vector_step"], dv.due("vector_step"))
                nc.vector.wait_ge(sem["root"], dv.due("root"))
                v.reciprocal(SS2[:, 32:34], SS2[:, 32:34]).then_inc(sem["vector_step"], 1)
                nc.vector.wait_ge(sem["vector_step"], dv.due("vector_step"))
                for t in range(2):
                    ts(X2[:, t, :], X2[:, t, :], SS2[:, 34 + 2 * t:35 + 2 * t], SS2[:, 32 + t:33 + t],
                               ALU.subtract, ALU.mult).then_inc(sem["vector_step"], 1)
                    nc.vector.wait_ge(sem["vector_step"], dv.due("vector_step"))
                    tt(X2[:, t, :], X2[:, t, :], LNG[:, 0 if first else 2, :], ALU.mult).then_inc(sem["vector_step"], 1)
                    nc.vector.wait_ge(sem["vector_step"], dv.due("vector_step"))
                    ins = tt(X2[:, t, :], X2[:, t, :], LNG[:, 1 if first else 3, :], ALU.add)
                    if first:
                        ins.then_inc(sem["ln_ready"], 1)
                        nc.vector.wait_ge(sem["ln_ready"], dv.due("ln_ready"))
                    elif t:
                        ins.then_inc(sem["x_ready"], 1)
                        nc.vector.wait_ge(sem["x_ready"], dv.due("x_ready"))
                    else:
                        ins.then_inc(sem["vector_step"], 1)
                        nc.vector.wait_ge(sem["vector_step"], dv.due("vector_step"))

            def residual(u, t, c):
                cols = slice(c * CN, (c + 1) * CN)
                stt(X2[:, t, cols], X2[:, t, cols], ALPHA, U(u)[:, :], ALU.mult, ALU.add).then_inc(free[u % BANKS], 1)
                nc.vector.wait_ge(free[u % BANKS], dv.uses(u))

            for l in range(DEPTH):
                nc.vector.wait_ge(sem["smalls2"], dv.due("smalls2", 16 * (13 if l == 0 else 9)))
                u = dv.unit()
                nc.vector.wait_ge(full[u % BANKS], dv.uses(u))
                v.tensor_copy(COLS2[:, 0:105], U(u)[:, 0:105]).then_inc(free[u % BANKS], 1)
                nc.vector.wait_ge(free[u % BANKS], dv.uses(u))
                v.memset(VA[:, :, :, 256:257], 1.0).then_inc(sem["vector_step"], 1)
                nc.vector.wait_ge(sem["vector_step"], dv.due("vector_step"))
                ts(VEC[0:4, 4:6], VEC[0:4, 0:2], 1 / NEG_B1, None, ALU.mult).then_inc(sem["vecs_ready"], 1)
                nc.vector.wait_ge(sem["vecs_ready"], dv.due("vecs_ready"))
                take_pairs(dv, XT2)
                dv.unit()
                nc.vector.wait_ge(sem["mg_soft"], dv.due("mg_soft"))
                one = ones[:, 0:1]
                v.tensor_tensor_scan(GR[0:4, 3, :], one[0:4].broadcast_to([4, SEQ]), GR[0:4, 2, :], 0.0,
                                             ALU.mult, ALU.subtract).then_inc(sem["vector_step"], 1)
                nc.vector.wait_ge(sem["vector_step"], dv.due("vector_step"))
                stt(GR[0:4, 4, :], GR[0:4, 0, :], NEG_B1, GR[0:4, 3, :], ALU.mult, ALU.subtract).then_inc(sem["vector_step"], 1)
                nc.vector.wait_ge(sem["vector_step"], dv.due("vector_step"))
                v.tensor_tensor_scan(GR[0:4, 5, :], one[0:4].broadcast_to([4, SEQ]), GR[0:4, 4, :], 0.0,
                                             ALU.mult, ALU.max).then_inc(sem["vector_step"], 1)
                nc.vector.wait_ge(sem["vector_step"], dv.due("vector_step"))
                tt(GR[0:4, 6, :], GR[0:4, 3, :], GR[0:4, 5, :], ALU.add).then_inc(sem["vector_step"], 1)
                nc.vector.wait_ge(sem["vector_step"], dv.due("vector_step"))
                ts(GR[0:4, 6, :], GR[0:4, 6, :], -80.0, None, ALU.max).then_inc(sem["vector_step"], 1)
                nc.vector.wait_ge(sem["vector_step"], dv.due("vector_step"))
                ts(GR[0:4, 5, :], GR[0:4, 5, :], -1.0, None, ALU.mult).then_inc(sem["mg_rows"], 1)
                nc.vector.wait_ge(sem["mg_rows"], dv.due("mg_rows"))
                for T in (QA, KA):
                    for j in range(2):
                        if j:
                            dv.unit()
                        else:
                            u = dv.unit()
                            nc.vector.wait_ge(full[u % BANKS], dv.uses(u))
                            v.tensor_copy(T[:, 0:2, :].rearrange("p h n -> p (h n)"), U(u)[:, :]).then_inc(free[u % BANKS], 1)
                            nc.vector.wait_ge(free[u % BANKS], dv.uses(u))
                for c in range(2):
                    for t in range(2):
                        if t:
                            dv.unit()
                        else:
                            u = dv.unit()
                            nc.vector.wait_ge(full[u % BANKS], dv.uses(u))
                            v.tensor_copy(VA[:, 0, 2 * c:2 * c + 2, 0:256],
                                                          U(u)[:, :].rearrange("p (h n) -> p h n", h=2)).then_inc(free[u % BANKS], 1)
                            nc.vector.wait_ge(free[u % BANKS], dv.uses(u))
                oa = [dv.unit() for i in range(4)]
                u = dv.unit()
                nc.vector.wait_ge(full[u % BANKS], dv.uses(u))
                v.tensor_copy(GC[:, 0:16], U(u)[:, 0:16]).then_inc(free[u % BANKS], 1)
                nc.vector.wait_ge(free[u % BANKS], dv.uses(u))
                for pair in range(2):
                    u = dv.unit()
                    nc.vector.wait_ge(full[u % BANKS], dv.uses(u))
                    for j in range(2):
                        h = 2 * pair + j
                        b = U(u)[:, j * SEQ:(j + 1) * SEQ]
                        tt(EA[:, h, 0:SEQ], b, CAUSAL, ALU.add).then_inc(sem["vector_step"], 1)
                        nc.vector.wait_ge(sem["vector_step"], dv.due("vector_step"))
                        ins = tt(EA[:, h, SEQ:SEQ + P], b[:, P:SEQ], CAUSAL[:, 0:P], ALU.add)
                        if j == 0:
                            ins.then_inc(sem["vector_step"], 1)
                            nc.vector.wait_ge(sem["vector_step"], dv.due("vector_step"))
                        else:
                            ins.then_inc(free[u % BANKS], 1)
                            nc.vector.wait_ge(free[u % BANKS], dv.uses(u))
                        v.memset(SS2[:, 63:64], 0.0).then_inc(sem["mexp_in"], 1)
                        nc.vector.wait_ge(sem["mexp_in"], dv.due("mexp_in"))
                    for j in range(2):
                        h = 2 * pair + j
                        nc.vector.wait_ge(sem["mexp"], dv.due("mexp"))
                        u = dv.unit()
                        nc.vector.wait_ge(full[u % BANKS], dv.uses(u))
                        stt(PA[:, h, :], U(u)[:, 0:384], SCALE_A, EA[:, h, :], ALU.mult, ALU.mult).then_inc(free[u % BANKS], 1)
                        nc.vector.wait_ge(free[u % BANKS], dv.uses(u))
                    for j in range(2):
                        h = 2 * pair + j
                        for t in range(2):
                            u = dv.unit()
                            nc.vector.wait_ge(full[u % BANKS], dv.uses(u))
                            den = SS2[:, 60:61]
                            v.tensor_copy(den, U(u)[:, 256:257]).then_inc(sem["vector_step"], 1)
                            nc.vector.wait_ge(sem["vector_step"], dv.due("vector_step"))
                            stt(SS2[:, 61:62], den, -1.0, den, ALU.mult, ALU.max).then_inc(sem["vector_step"], 1)
                            nc.vector.wait_ge(sem["vector_step"], dv.due("vector_step"))
                            tt(SS2[:, 61:62], SS2[:, 61:62], GC[:, 8 + 4 * t + h:9 + 4 * t + h], ALU.max).then_inc(sem["vector_step"], 1)
                            nc.vector.wait_ge(sem["vector_step"], dv.due("vector_step"))
                            v.reciprocal(SS2[:, 61:62], SS2[:, 61:62]).then_inc(sem["vector_step"], 1)
                            nc.vector.wait_ge(sem["vector_step"], dv.due("vector_step"))
                            ts(HA[:, t, h * 256:(h + 1) * 256], U(u)[:, 0:256], SS2[:, 61:62], None, ALU.mult).then_inc(free[u % BANKS], 1)
                            nc.vector.wait_ge(free[u % BANKS], dv.uses(u))
                for n_out in oa:
                    nc.vector.wait_ge(free[n_out % BANKS], dv.uses(n_out))
                for t in range(2):
                    tt(SCR2[:, 0:D], HA[:, t, :], HA[:, t, :], ALU.mult).then_inc(sem["vector_step"], 1)
                    nc.vector.wait_ge(sem["vector_step"], dv.due("vector_step"))
                    ins = red(SS2[:, 4 * t:4 * t + 4], SCR2[:, 0:D].rearrange("p (h n) -> p h n", h=4), AXX, ALU.add)
                    if t:
                        ins.then_inc(sem["stat"], 1)
                        nc.vector.wait_ge(sem["stat"], dv.due("stat"))
                    else:
                        ins.then_inc(sem["vector_step"], 1)
                        nc.vector.wait_ge(sem["vector_step"], dv.due("vector_step"))
                nc.vector.wait_ge(sem["root"], dv.due("root"))
                v.reciprocal(SS2[:, 0:8], SS2[:, 0:8]).then_inc(sem["vector_step"], 1)
                nc.vector.wait_ge(sem["vector_step"], dv.due("vector_step"))
                for t in range(2):
                    x = HA[:, t, :].rearrange("p (h n) -> p h n", h=4)
                    tt(x, x, bc(SS2[:, 4 * t:4 * t + 4], 2, [P, 4, 256]), ALU.mult).then_inc(sem["vector_step"], 1)
                    nc.vector.wait_ge(sem["vector_step"], dv.due("vector_step"))
                    tt(HA[:, t, :], HA[:, t, :], OA[:, t, :], ALU.mult).then_inc(sem["ha_ready"], 1)
                    nc.vector.wait_ge(sem["ha_ready"], dv.due("ha_ready"))
                take_pairs(dv, HAT, lambda k: COLS2[:, 96 + k:97 + k])
                nc.vector.wait_ge(sem["bg_exp"], dv.due("bg_exp"))
                u = dv.unit()
                nc.vector.wait_ge(full[u % BANKS], dv.uses(u))
                ts(GR[0:8, 0, :], GR[0:8, 0, :], 1.0, None, ALU.add).then_inc(sem["vector_step"], 1)
                nc.vector.wait_ge(sem["vector_step"], dv.due("vector_step"))
                v.reciprocal(GR[0:8, 0, :], GR[0:8, 0, :]).then_inc(sem["vector_step"], 1)
                nc.vector.wait_ge(sem["vector_step"], dv.due("vector_step"))
                ts(GR[0:8, 4, :], U(u)[0:8, SEQ:2 * SEQ], VEC[0:8, 2:3], None, ALU.add).then_inc(free[u % BANKS], 1)
                nc.vector.wait_ge(free[u % BANKS], dv.uses(u))
                stt(GR[0:8, 5, :], GR[0:8, 4, :], -1.0, GR[0:8, 4, :], ALU.mult, ALU.max).then_inc(sem["bg_in"], 1)
                nc.vector.wait_ge(sem["bg_in"], dv.due("bg_in"))
                nc.vector.wait_ge(sem["bg_ln"], dv.due("bg_ln"))
                stt(GR[0:8, 6, :], GR[0:8, 4, :], 0.0, GR[0:8, 5, :], ALU.max, ALU.add).then_inc(sem["vector_step"], 1)
                nc.vector.wait_ge(sem["vector_step"], dv.due("vector_step"))
                ts(GR[0:8, 6, :], GR[0:8, 6, :], VEC[0:8, 3:4], None, ALU.mult).then_inc(sem["vector_step"], 1)
                nc.vector.wait_ge(sem["vector_step"], dv.due("vector_step"))
                for c in range(2):
                    cols = slice(c * P, (c + 1) * P)
                    ins = v.tensor_tensor_scan(GR[0:8, 4, cols], one[0:8].broadcast_to([8, P]), GR[0:8, 6, cols], 0.0,
                                               ALU.mult, ALU.subtract)
                    if c:
                        ins.then_inc(sem["bg_cum"], 1)
                        nc.vector.wait_ge(sem["bg_cum"], dv.due("bg_cum"))
                    else:
                        ins.then_inc(sem["vector_step"], 1)
                        nc.vector.wait_ge(sem["vector_step"], dv.due("vector_step"))
                ts(GR[0:8, 1, :], GR[0:8, 4, :], -1.0, None, ALU.mult).then_inc(sem["vector_step"], 1)
                nc.vector.wait_ge(sem["vector_step"], dv.due("vector_step"))
                nc.vector.wait_ge(sem["bg_exp"], dv.due("bg_exp"))
                tt(GR[0:8, 2, P:SEQ], GR[0:8, 2, P:SEQ], GR[0:8, 0, P:SEQ], ALU.mult).then_inc(sem["bg_rows"], 1)
                nc.vector.wait_ge(sem["bg_rows"], dv.due("bg_rows"))
                for i in range(6):
                    for j in range(2):
                        u = dv.unit()
                        nc.vector.wait_ge(full[u % BANKS], dv.uses(u))
                        if 2 * i + j >= 2:
                            nc.vector.wait_ge(sem["conv_done"], dv.due("conv_done"))
                        for c in range(2):
                            tile = 4 * i + 2 * j + c
                            acc = SCR2[:, 512 * (j % 2) + SEQ * c:512 * (j % 2) + SEQ * (c + 1)]
                            src = U(u)[:, c * SEQ:(c + 1) * SEQ]
                            ts(acc, src, CONVW[:, 3, tile:tile + 1], None, ALU.mult).then_inc(sem["vector_step"], 1)
                            nc.vector.wait_ge(sem["vector_step"], dv.due("vector_step"))
                            for d in range(1, 4):
                                ins = stt(acc[:, d:SEQ], src[:, 0:SEQ - d], CONVW[:, 3 - d, tile:tile + 1],
                                          acc[:, d:SEQ], ALU.mult, ALU.add)
                                if (c, d) == (1, 3):
                                    ins.then_inc(free[u % BANKS], 1)
                                    nc.vector.wait_ge(free[u % BANKS], dv.uses(u))
                                else:
                                    ins.then_inc(sem["vector_step"], 1)
                                    nc.vector.wait_ge(sem["vector_step"], dv.due("vector_step"))
                nc.vector.wait_ge(sem["conv_done"], dv.due("conv_done", 2))
                u = dv.unit()
                nc.vector.wait_ge(free[u % BANKS], dv.uses(u))
                v.reciprocal(R16[0:16, :], R16[0:16, :]).then_inc(sem["vector_step"], 1)
                nc.vector.wait_ge(sem["vector_step"], dv.due("vector_step"))
                ts(R16[0:8, :], R16[0:8, :], SCALE_A, None, ALU.mult).then_inc(sem["rn_ready"], 1)
                nc.vector.wait_ge(sem["rn_ready"], dv.due("rn_ready"))
                for r in range(0, 16, 2):
                    T = QB if r < 8 else KB
                    h = r % 8
                    x = T[:, h:h + 2, :].rearrange("p h n -> p (h n)")
                    u = dv.unit()
                    nc.vector.wait_ge(full[u % BANKS], dv.uses(u))
                    tt(x, x, U(u)[:, :], ALU.mult).then_inc(free[u % BANKS], 1)
                    nc.vector.wait_ge(free[u % BANKS], dv.uses(u))
                u = dv.unit()
                nc.vector.wait_ge(full[u % BANKS], dv.uses(u))
                v.tensor_copy(GC[:, 0:48], U(u)[:, 0:48]).then_inc(free[u % BANKS], 1)
                nc.vector.wait_ge(free[u % BANKS], dv.uses(u))
                flat = lambda T: T.rearrange("p m n -> p (m n)")
                for b in range(4):
                    u_decay, u_beta, u_kq, u_kk = dv.unit(), dv.unit(), dv.unit(), dv.unit()
                    for n_in in (u_decay, u_beta, u_kq, u_kk):
                        nc.vector.wait_ge(full[n_in % BANKS], dv.uses(n_in))
                    tt(EB, U(u_decay)[:, :].rearrange("p (m n) -> p m n", m=4),
                                       bc(CAUSAL[:, 0:P], 1, [P, 4, P]), ALU.add).then_inc(sem["e_in"], 1)
                    nc.vector.wait_ge(sem["e_in"], dv.due("e_in"))
                    u = dv.unit()
                    nc.vector.wait_ge(full[u % BANKS], dv.uses(u))
                    for i in range(4):
                        h, c = 2 * b + i // 2, i % 2
                        g = GC[:, 32 + h:33 + h] if c else GC[:, 40 + h:41 + h]
                        ins = ts(KX[:, i, :], U(u)[:, i * P:(i + 1) * P], g, None, ALU.mult)
                        if i == 3:
                            ins.then_inc(free[u % BANKS], 1)
                            nc.vector.wait_ge(free[u % BANKS], dv.uses(u))
                        else:
                            ins.then_inc(sem["vector_step"], 1)
                            nc.vector.wait_ge(sem["vector_step"], dv.due("vector_step"))
                    dv.unit()
                    nc.vector.wait_ge(sem["e_exp"], dv.due("e_exp"))
                    tt(flat(ATTN), U(u_kq)[:, :], flat(EB), ALU.mult).then_inc(free[u_kq % BANKS], 1)
                    nc.vector.wait_ge(free[u_kq % BANKS], dv.uses(u_kq))
                    tt(EB, EB, bc(STRICT, 1, [P, 4, P]), ALU.mult).then_inc(sem["vector_step"], 1)
                    nc.vector.wait_ge(sem["vector_step"], dv.due("vector_step"))
                    tt(flat(EB), flat(EB), U(u_kk)[:, :], ALU.mult).then_inc(free[u_kk % BANKS], 1)
                    nc.vector.wait_ge(free[u_kk % BANKS], dv.uses(u_kk))
                    tt(flat(AT), flat(EB), U(u_beta)[:, :], ALU.mult).then_inc(free[u_beta % BANKS], 1)
                    nc.vector.wait_ge(free[u_beta % BANKS], dv.uses(u_beta))
                    q2 = QB[:, 2 * b:2 * b + 2, P:SEQ]
                    tt(QE, q2, EG, ALU.mult).then_inc(sem["at_ready"], 1)
                    nc.vector.wait_ge(sem["at_ready"], dv.due("at_ready"))
                    u = dv.unit()
                    nc.vector.wait_ge(full[u % BANKS], dv.uses(u))
                    tt(XI, U(u)[:, :].rearrange("p (m n) -> p m n", m=4), bc(LEVEL[:, 0, :], 1, [P, 4, P]), ALU.mult).then_inc(free[u % BANKS], 1)
                    nc.vector.wait_ge(free[u % BANKS], dv.uses(u))
                    tt(XI, bc(ident, 1, [P, 4, P]), XI, ALU.subtract).then_inc(sem["vector_step"], 1)
                    nc.vector.wait_ge(sem["vector_step"], dv.due("vector_step"))
                    tt(XIT, AT, bc(LEVEL[:, 7, :], 1, [P, 4, P]), ALU.mult).then_inc(sem["vector_step"], 1)
                    nc.vector.wait_ge(sem["vector_step"], dv.due("vector_step"))
                    tt(XIT, bc(ident, 1, [P, 4, P]), XIT, ALU.subtract).then_inc(sem["x0_ready"], 1)
                    nc.vector.wait_ge(sem["x0_ready"], dv.due("x0_ready"))
                    for s in range(1, 7):
                        u = dv.unit()
                        nc.vector.wait_ge(full[u % BANKS], dv.uses(u))
                        tt(YI, U(u)[:, :].rearrange("p (m n) -> p m n", m=4), bc(LEVEL[:, s, :], 1, [P, 4, P]), ALU.mult).then_inc(free[u % BANKS], 1)
                        nc.vector.wait_ge(free[u % BANKS], dv.uses(u))
                        for T in ((XI, XIT) if s < 6 else (XIT,)):
                            u = dv.unit()
                            nc.vector.wait_ge(full[u % BANKS], dv.uses(u))
                            tt(flat(T), flat(T), U(u)[:, :], ALU.subtract).then_inc(free[u % BANKS], 1)
                            nc.vector.wait_ge(free[u % BANKS], dv.uses(u))
                    u_u = dv.unit()
                    dv.unit(2)
                    u = dv.unit()
                    nc.vector.wait_ge(full[u % BANKS], dv.uses(u))
                    tt(UU[:, 1::2, :], UU[:, 1::2, :], U(u)[:, 0:SEQ].rearrange("p (m n) -> p m n", m=2), ALU.subtract).then_inc(free[u % BANKS], 1)
                    nc.vector.wait_ge(free[u % BANKS], dv.uses(u))
                    u = dv.unit()
                    nc.vector.wait_ge(full[u % BANKS], dv.uses(u))
                    v.tensor_copy(QB[:, 2 * b:2 * b + 2, :].rearrange("p h n -> p (h n)"), U(u)[:, :]).then_inc(free[u % BANKS], 1)
                    nc.vector.wait_ge(free[u % BANKS], dv.uses(u))
                v.memset(SS2[:, 63:64], 0.0).then_inc(sem["heads_done"], 1)
                nc.vector.wait_ge(sem["heads_done"], dv.due("heads_done"))
                o = up(4096, 2048)
                tt(SCR2, o, o, ALU.mult).then_inc(sem["vector_step"], 1)
                nc.vector.wait_ge(sem["vector_step"], dv.due("vector_step"))
                red(SS2[:, 0:16], SCR2.rearrange("p (g n) -> p g n", g=16), AXX, ALU.add).then_inc(sem["stat"], 1)
                nc.vector.wait_ge(sem["stat"], dv.due("stat"))
                nc.vector.wait_ge(sem["root"], dv.due("root"))
                v.reciprocal(SS2[:, 0:16], SS2[:, 0:16]).then_inc(sem["vector_step"], 1)
                nc.vector.wait_ge(sem["vector_step"], dv.due("vector_step"))
                og = o.rearrange("p (g n) -> p g n", g=16)
                tt(og, og, bc(SS2[:, 0:16], 2, [P, 16, P]), ALU.mult).then_inc(sem["vector_step"], 1)
                nc.vector.wait_ge(sem["vector_step"], dv.due("vector_step"))
                z = [dv.unit() for i in range(4)]
                for n_out in z:
                    nc.vector.wait_ge(free[n_out % BANKS], dv.uses(n_out))
                for t in range(2):
                    tt(HBN[:, t, :].rearrange("p (h n) -> p h n", h=8), QB[:, :, t * P:(t + 1) * P],
                                           ZB[:, t, :].rearrange("p (h n) -> p h n", h=8), ALU.mult).then_inc(sem["hb_ready"], 1)
                    nc.vector.wait_ge(sem["hb_ready"], dv.due("hb_ready"))
                ga = [dv.unit() for i in range(4)]
                for n_out in ga:
                    nc.vector.wait_ge(free[n_out % BANKS], dv.uses(n_out))
                for c in range(2):
                    for t in range(2):
                        x = SGA[:, t, c * CN:(c + 1) * CN]
                        u = dv.unit()
                        nc.vector.wait_ge(full[u % BANKS], dv.uses(u))
                        tt(x, x, U(u)[:, :], ALU.mult).then_inc(free[u % BANKS], 1)
                        nc.vector.wait_ge(free[u % BANKS], dv.uses(u))
                gb = [dv.unit() for i in range(4)]
                for n_out in gb:
                    nc.vector.wait_ge(free[n_out % BANKS], dv.uses(n_out))
                take_pairs(dv, XT2, lambda k: COLS2[:, 104:105])
                for c in range(2):
                    for t in range(2):
                        x, g = SGA[:, t, c * CN:(c + 1) * CN], SGB[:, t, c * CN:(c + 1) * CN]
                        u = dv.unit()
                        nc.vector.wait_ge(full[u % BANKS], dv.uses(u))
                        tt(SCR2[:, 0:CN], g, U(u)[:, :], ALU.mult).then_inc(free[u % BANKS], 1)
                        nc.vector.wait_ge(free[u % BANKS], dv.uses(u))
                        ins = tt(x, x, SCR2[:, 0:CN], ALU.add)
                        if (c, t) == (1, 1):
                            ins.then_inc(sem["y_ready"], 1)
                            nc.vector.wait_ge(sem["y_ready"], dv.due("y_ready"))
                        else:
                            ins.then_inc(sem["vector_step"], 1)
                            nc.vector.wait_ge(sem["vector_step"], dv.due("vector_step"))
                take_pairs(dv, HAT)
                for c in range(2):
                    for t in range(2):
                        u = dv.unit()
                        nc.vector.wait_ge(full[u % BANKS], dv.uses(u))
                        residual(u, t, c)
                nc.vector.wait_ge(sem["ln_gains"], dv.due("ln_gains", 64))
                layer_norm(True)
                take_pairs(dv, XT2)
                tile = 0
                for n in FF_TILES:
                    gs = [dv.unit() for j in range(0, n, 2)]
                    for j in range(0, n, 2):
                        u = dv.unit()
                        nc.vector.wait_ge(full[u % BANKS], dv.uses(u))
                        nc.vector.wait_ge(free[gs[j // 2] % BANKS], dv.uses(gs[j // 2]))
                        p = (tile // 2) % 4
                        tt(HFF[:, tile:tile + 2, :].rearrange("p f n -> p (f n)"),
                                           SCR2[:, 512 * p:512 * p + 512], U(u)[:, :], ALU.mult).then_inc(free[u % BANKS], 1)
                        nc.vector.wait_ge(free[u % BANKS], dv.uses(u))
                        tile += 2
                for c in range(2):
                    for t in range(2):
                        u = dv.unit()
                        nc.vector.wait_ge(full[u % BANKS], dv.uses(u))
                        residual(u, t, c)
                layer_norm(False)

_INS = [
    "x", "c", "ctx", "c_ctx", "ada_w", "ada_b", "norm1_g", "norm2_g", "w_in", "w_out", "head_out_g", "sgu_w", "sgu_b",
    "diff_qn_g", "diff_kn_g", "diff_lambda", "na_qn_g", "na_kn_g", "na_rpb", "router_w", "exp_w_gate", "exp_w_up",
    "exp_w_down", "w_in_2", "b_igate_2", "b_fgate_2", "g_mlstm_norm_2", "conv_w_2", "a_log_2", "dt_bias_2",
    "g_gdn_norm_2", "w_branch_a_2", "w_branch_b_2", "w_out_2", "ln1_g_2", "ln1_b_2", "w_ffn_up_2",
    "w_ffn_down_2", "ln2_g_2", "ln2_b_2",
]


def kernel(**inputs):
    import numpy as _np
    import concourse.bacc as _bacc
    from concourse import mybir as _mybir
    from concourse.bass_utils import run_bass_kernel_spmd as _run

    nc = _bacc.Bacc("TRN2", target_bir_lowering=False, num_devices=1)
    arrays, args = {}, {}
    for name in _INS:
        arrays[f"in_{name}_dram"] = _np.ascontiguousarray(inputs[name])
    for name, a in constants().items():
        arrays[f"in_c_{name}_dram"] = a
    for key, a in arrays.items():
        args[key[3:-5]] = nc.dram_tensor(key, a.shape, _mybir.dt.from_np(a.dtype), kind="ExternalInput").ap()
    out = nc.dram_tensor("out_0_dram", (1, SEQ, D), F32, kind="ExternalOutput").ap()
    gate_scratch = nc.dram_tensor("gate_scratch", (DEPTH, 2, 2, D), F32, kind="Internal").ap()
    band = nc.dram_tensor("band", (DEPTH, HEADS, 7, GRID_W, BAND), F32, kind="Internal").ap()
    build(nc, args, out, gate_scratch, band)
    r = _run(nc, [arrays], core_ids=[0])
    return r.results[0]["out_0_dram"]
```

```python
import math
from collections import Counter
from contextlib import ExitStack, contextmanager

import concourse.bass as bass
import numpy as np
from concourse import mybir

ALU = mybir.AluOpType
ACT = mybir.ActivationFunctionType
F32 = mybir.dt.float32
AXX = mybir.AxisListType.X

P = 128
D = 1024
KT = D // P
SEQ = 256
DEPTH = 2
GRID_W = 64
HEADS = 4
HD = 64
DIFF_D = 32
NA_COLS = 16
N_EXP = 16
CAP = 2 * SEQ // N_EXP
ROPE_BASE = 10000.0
EPS = 1e-6
LN_EPS = 1e-5
IN_W = 2304
BAND = 2 * GRID_W - 1
CN = 512
RING = 6
BANKS = 8
ARENA = 28632
NEG = -1e30

A_U, A_V, B_Z, C_Q, C_K, C_V, D_Q, D_K, D_V = 0, 256, 512, 768, 1024, 1280, 1536, 1792, 2048

A_DK, A_DV = 128, 256
B_HEADS = 8
D_FF = 2816
FT = D_FF // P
N_IN = 9240
ALPHA = (2.0 * DEPTH) ** 0.25
W2_QA, W2_KA, W2_VA, W2_OA, W2_I, W2_F = 0, 512, 1024, 2048, 3072, 3076
W2_QKV, W2_Z, W2_BETA, W2_A, W2_GA, W2_GB = 3080, 6152, 7176, 7184, 7192, 8216


class Count:

    def __init__(self, name, eng):
        self.name, self.eng, self.per_turn = name, eng, {}
        self.base, self.local = Counter(), Counter()
        self.turn = None
        self.unit_base, self.unit_local = 0, 0

    def due(self, what, n=1):
        self.local[what] += n
        v = self.base[what] + self.local[what]
        return v if self.turn is None else self.turn * self.per_turn[what] + v

    def unit(self, k=1):
        self.unit_local += k
        return self.unit_base + self.unit_local - 1

    def uses(self, n):
        v = n // BANKS + 1
        return v if self.turn is None else self.turn * (self.per_turn["unit"] // BANKS) + v

    @contextmanager
    def loop(self, turns, per_turn):
        self.per_turn = per_turn
        self.base.update(self.local)
        self.local = Counter()
        self.unit_base += self.unit_local
        self.unit_local = 0
        with self.eng.Fori(0, turns) as turn:
            self.turn = turn
            yield turn
            self.turn = None
        for what, n in self.local.items():
            assert per_turn[what] == n, (self.name, what, n)
            self.base[what] += n * turns
        if self.unit_local:
            assert self.unit_local == per_turn["unit"], (self.name, self.unit_local)
        self.unit_base += self.unit_local * turns
        self.local, self.unit_local = Counter(), 0


def expert_turn(ns):
    turn = {"unit": 32, "chunk_used": 24, "xgc_ready": 4, "xg_used": 4, "vector_step": 8 * (ns - 1),
            "hid_silu": 8, "down_part": 8}
    turn.update({f"chunk{s}": 64 for s in range(RING)})
    return turn


def bc(ap, axis, shape):
    return ap.unsqueeze(axis).broadcast_to(shape)


def constants():
    f = np.float32
    n, c = np.arange(SEQ), np.arange(HD)
    wn = 2 * np.pi * np.outer(n, n) % (2 * np.pi * SEQ) / SEQ
    wn = 2 * np.pi * (np.outer(n, n) % SEQ) / SEQ
    wc = 2 * np.pi * (np.outer(c, c) % HD) / HD
    scale = 1.0 / math.sqrt(SEQ * HD)
    seq_dft = np.concatenate([np.cos(wn), np.sin(wn)], 1)
    two = np.eye(2)
    head_dft = np.concatenate([np.kron(two, np.cos(wc)), -np.kron(two, np.sin(wc))], 1) * scale
    half = DIFF_D // 2
    inv = (1.0 / (f(ROPE_BASE) ** (np.arange(0, half, 2, dtype=f) / f(half)))).astype(f)
    row = ((n // GRID_W).astype(f)[:, None] * inv).astype(f)
    col = ((n % GRID_W).astype(f)[:, None] * inv).astype(f)
    cos = np.concatenate([np.cos(row), np.cos(row), np.cos(col), np.cos(col)], 1)
    sin = np.concatenate([-np.sin(row), np.sin(row), -np.sin(col), np.sin(col)], 1)
    rope = np.concatenate([cos, sin], 1)
    qc = np.arange(P) % GRID_W
    kc = np.arange(SEQ) % GRID_W
    w0 = np.clip(qc - NA_COLS // 2, 0, GRID_W - NA_COLS)[:, None]
    window = np.where((kc[None] >= w0) & (kc[None] < w0 + NA_COLS), 0.0, NEG)
    i, j = np.arange(P)[:, None], np.arange(P)[None]
    causal_t = np.where(i <= j, 0.0, NEG)
    strict_t = (i < j) * 1.0
    levels = []
    for s in (1, 2, 4, 8, 16, 32, 64):
        levels.append(((i // (2 * s) == j // (2 * s)) & (i % (2 * s) >= s) & (j % (2 * s) < s)) * 1.0)
    slots = np.broadcast_to(np.arange(1, CAP + 1), (P, CAP))
    pick = np.zeros((P, 31))
    pick[:, 15] = 1.0
    fold = lambda w: np.pad(np.tile(np.eye(w), (2, 1)), ((0, P - 2 * w), (0, 0)))
    out = {
        "fold": np.concatenate([fold(64), fold(32), np.tile(np.eye(32), (4, 1))[:, 0:2]], 1),
        "seq_dft": seq_dft, "head_dft": head_dft, "rope": rope, "window": window,
        "ident": np.eye(P), "ones": np.ones((P, P)), "slots": slots, "pick": pick,
        "causal_t": np.concatenate([causal_t, np.zeros((P, P))], 1), "strict_t": strict_t,
        "levels": np.concatenate(levels + [levels[0].T], 1),
    }
    return {k: np.ascontiguousarray(v.astype(f)) for k, v in out.items()}


def first_half_memory(view):
    m = {}
    at = 132
    def put(name, width, **parts):
        nonlocal at
        m[name] = view(at, width)
        m[name + "_at"] = at
        at += width
    put("rope", 128)
    put("window", 256)
    put("slots", CAP)
    put("seq_dft", 2 * CN)
    put("head_dft", 256)
    put("rows", P)
    put("cols", 44)
    put("silu_c", 48)
    put("mod", 96)
    put("gain1", 16)
    put("gain2", 16)
    put("gains_qk", 192)
    put("lam_rows", 128)
    put("lam", 4)
    put("router", 128)
    put("fold", 98)
    put("ss", 116)
    put("aff", 64)
    put("small", 96)
    put("sgu_t", 512)
    put("scratch", 1536)
    put("gate", 2048)
    put("x", 4096)
    put("ht", 4096)
    put("xn", 4096)
    put("proj", 4 * IN_W)
    m["end"] = at
    return m


def build(nc, A, out, gate_scratch, band):
    with ExitStack() as ctx:
        ring = ctx.enter_context(nc.sbuf_tensor("ring", [P, RING * KT * CN], F32))
        arena = ctx.enter_context(nc.sbuf_tensor("arena", [P, ARENA], F32))
        bank = [ctx.enter_context(nc.psum_tensor(f"bank{b}", [P, CN], F32)) for b in range(BANKS)]
        names = [f"bank_full{b}" for b in range(BANKS)] + [f"bank_free{b}" for b in range(BANKS)]
        names += [f"chunk{s}" for s in range(RING)]
        names += ["chunk_used", "vector_step", "scalar_step", "rows_in", "tokens_in", "consts", "smalls", "band_out", "bias_in",
                  "x_ready", "silu_c", "mod_ready", "row_ready", "row_saved", "gate1_in", "gate2_in", "bias_used",
                  "stat", "root", "xn_ready", "vn_ready", "lam_dot", "lam_exp", "qk_ready", "row_max", "w_diff",
                  "logit", "logit_exp", "aff_ready", "rank_ready", "sel_ready", "selg_ready", "xg_ready",
                  "hid_silu", "down_part", "xg_used", "xgc_ready", "moe_done",
                  "smalls2", "vecs_ready", "mg_soft", "mg_rows", "mg_en", "mexp_in", "mexp", "ha_ready", "bg_exp", "bg_in",
                  "bg_ln", "bg_cum", "bg_rows", "conv_done", "sq_ready", "sq_used", "rn_ready", "e_in", "e_exp",
                  "at_ready", "x0_ready", "heads_done", "hb_ready", "y_ready", "ln_gains", "ln_ready", "out_done"]
        sem = {n: ctx.enter_context(nc.semaphore(n)) for n in names}

        def view(at, width):
            return arena[:, at:at + width]

        ident, ones = view(0, 128), view(128, 4)
        m = first_half_memory(view)
        assert m["end"] <= ARENA, m["end"]
        slot = [ring[:, s * KT * CN:(s + 1) * KT * CN].rearrange("p (k n) -> p k n", k=KT) for s in range(RING)]
        U = lambda n: bank[n % BANKS]
        full = [sem[f"bank_full{b}"] for b in range(BANKS)]
        free = [sem[f"bank_free{b}"] for b in range(BANKS)]

        X = m["x"].rearrange("p (t n) -> p t n", t=4)
        HT = m["ht"].rearrange("p (k n) -> p k n", k=KT)
        XN = m["xn"].rearrange("p (t n) -> p t n", t=4)
        PROJ = m["proj"].rearrange("p (t n) -> p t n", t=4)
        SGU = m["proj"][:, 6 * D:6 * D + 512].rearrange("p (h q) -> p h q", h=HEADS)
        SGUT = m["sgu_t"].rearrange("p (h q) -> p h q", h=HEADS)
        BIAS = m["gate"].rearrange("p (t h k) -> p t h k", t=2, h=HEADS)
        GATE1 = m["gate"].rearrange("p (s n) -> p s n", s=2)
        SELT = m["gate"].rearrange("p (s b t) -> p s b t", s=2, b=4)
        SCR = m["scratch"]
        ROWBUF = SCR[:, 0:1024].rearrange("p (j n) -> p j n", j=2)
        GATE_ROWS = SCR[0:8, 1024:1536]
        ROWS, COLS = m["rows"], m["cols"]
        SC = m["silu_c"][:, 0:16].rearrange("p (k s) -> p k s", s=2)
        MOD = m["mod"].rearrange("p (j s) -> p j s", s=2)
        GAIN = [m["gain1"].rearrange("p (k s) -> p k s", s=2), m["gain2"].rearrange("p (k s) -> p k s", s=2)]
        SHIFT = [MOD[:, 0:8, :], MOD[:, 24:32, :]]
        RW = m["router"].rearrange("p (k e) -> p k e", k=KT)
        SS = m["ss"]
        SS28 = SS[:, 0:112].rearrange("p (t g) -> p t g", t=4)
        SST = SS[:, 112:116]
        ROPE = m["rope"].rearrange("p (t c) -> p t c", t=2)
        SEQDFT = m["seq_dft"].rearrange("p (k n) -> p k n", k=2)
        HDFT = m["head_dft"]
        QKT = [m["ht"][:, 2048 * i:2048 * i + 2048].rearrange("p (b n) -> p b n", b=4) for i in range(2)]
        EXPS = m["xn"][:, 0:2048].rearrange("p (j q n) -> p j q n", j=2, q=2)
        W = m["xn"][:, 2048:3072].rearrange("p (j n) -> p j n", j=2)
        WT = m["xn"][:, 3072:4096].rearrange("p (j n) -> p j n", j=2)
        PT = m["xn"][:, 0:2048].rearrange("p (s b n) -> p s b n", s=2, b=2)
        XG = m["proj"][:, 0:8192].rearrange("p (k e c) -> p k e c", k=KT, e=N_EXP)
        XGC = m["proj"][:, 8192:9216].rearrange("p (j k c) -> p j k c", j=2, k=KT)
        GATE2 = [m["proj"][:, 6656:8704].rearrange("p (s n) -> p s n", s=2),
                 m["xn"][:, 0:2048].rearrange("p (s n) -> p s n", s=2)]
        SEL = m["ht"][:, 0:2048].rearrange("p (t e c) -> p t e c", t=4, e=N_EXP)
        AFFT = SCR[:, 0:512]
        WORK = m["ht"][:, 2560:3072]
        RANK = m["ht"][:, 3072:3584]
        OEXP = [m["ht"].rearrange("p (b n) -> p b n", b=4), m["xn"].rearrange("p (b n) -> p b n", b=4)]
        GATE_PARTS = m["seq_dft"].rearrange("p (j n) -> p j n", j=2)
        UP_PARTS = SCR[:, 0:1024].rearrange("p (j n) -> p j n", j=2)
        DOWN_PART = m["sgu_t"]
        FOLD = {64: m["fold"][:, 0:64], 32: m["fold"][0:64, 64:96]}
        FOLD_ROWS = m["fold"][:, 96:98]
        HIDT = SCR[:, 1024:1536].rearrange("p (k c) -> p k c", k=KT)
        AFF = m["aff"].rearrange("p (t e) -> p t e", t=4)
        POS = m["lam_rows"][:, 0:64].rearrange("p (t e) -> p t e", t=4)
        SMALL = m["small"]

        block = ctx.enter_context(nc.Block())
        pe = Count("tensor", nc.tensor)
        ac = Count("scalar", nc.scalar)
        dv = Count("vector", nc.vector)
        sp = Count("sync", nc.sync)
        gp = Count("gpsimd", nc.gpsimd)
        mm = nc.tensor.matmul

        def turn(o, i):
            k = i.shape[0]
            return nc.tensor.transpose(o, i, ident[0:k, 0:k])

        m2, at2 = {}, [132]

        def put2(name, width):
            m2[name] = view(at2[0], width)
            at2[0] += width

        for name, width in (("causal", 256), ("strict", 128), ("levels", 1024), ("pick", 32), ("rows", P),
                            ("cols", 112), ("w_gates", 192), ("vecs", 8), ("gate_rows", 2048), ("gate_cols", 64), ("ss", 64),
                            ("root_rows", 256), ("scratch", 2048)):
            put2(name, width)
        assert at2[0] <= m["x_at"]
        base2 = m["x_at"] + 2 * D
        up = lambda at, width: view(base2 + at, width)
        X2 = X[:, 0:2, :]
        COLS2, SS2, VEC, SCR2 = m2["cols"], m2["ss"], m2["vecs"], m2["scratch"]
        CONVW = COLS2[:, 0:96].rearrange("p (i t) -> p i t", i=4)
        WG = m2["w_gates"].rearrange("p (k n) -> p k n", k=KT)
        GR = m2["gate_rows"].rearrange("p (i n) -> p i n", i=8)
        GC = m2["gate_cols"]
        LEVEL = m2["levels"].rearrange("p (i n) -> p i n", i=8)
        CAUSAL, STRICT, PICK = m2["causal"], m2["strict"], m2["pick"]
        R16 = m2["root_rows"]
        XT2 = up(0, 2048).rearrange("p (k n) -> p k n", k=KT)
        HAT = up(2048, 2048).rearrange("p (k n) -> p k n", k=KT)
        QA = up(4096, 1024).rearrange("p (h n) -> p h n", h=4)
        KA = up(5120, 1024).rearrange("p (h n) -> p h n", h=4)
        VA = up(6144, 2056).rearrange("p (t h n) -> p t h n", t=2, h=4)
        OA = up(8200, 2048).rearrange("p (t n) -> p t n", t=2)
        HA = up(10248, 2048).rearrange("p (t n) -> p t n", t=2)
        EA = up(12296, 1536).rearrange("p (j n) -> p j n", j=4)
        PA = up(13832, 1536).rearrange("p (j n) -> p j n", j=4)
        QB = up(4096, 2048).rearrange("p (h n) -> p h n", h=8)
        KB = up(6144, 2048).rearrange("p (h n) -> p h n", h=8)
        VB = up(8192, 2048).rearrange("p (h n) -> p h n", h=8)

        class Delta:

            def __init__(self, at):
                quad = lambda i: up(at + 512 * i, 512).rearrange("p (m n) -> p m n", m=4)
                two = lambda at: up(at, 256).rearrange("p (h n) -> p h n", h=2)
                self.decay, self.attn, self.a_t = quad(0), quad(1), quad(2)
                self.inv, self.inv_t, self.v, self.k = quad(3), quad(4), quad(5), quad(6)
                self.y = self.decay
                self.w_t, self.state = two(at + 1024), two(at + 1280)
                self.u, self.grown = self.inv, two(at + 1536)
                self.q = two(at + 3584)

        DELTA = [Delta(10240 + 3840 * j) for j in range(2)]

        def in_turn(*programs):
            programs = list(programs)
            while programs:
                programs = [g for g in programs if next(g, "end") != "end"]
        ZB = up(6144, 2048).rearrange("p (t n) -> p t n", t=2)
        SGA = up(8192, 2048).rearrange("p (t n) -> p t n", t=2)
        SGB = up(10240, 2048).rearrange("p (t n) -> p t n", t=2)
        HBN = up(12288, 2048).rearrange("p (t n) -> p t n", t=2)
        LNG = up(14336, 4096).rearrange("p (i n) -> p i n", i=4)
        HFF = up(4096, FT * SEQ).rearrange("p (f n) -> p f n", f=FT)
        assert base2 + 14336 + 4096 <= ARENA
        NEG_B1, SCALE_A = 15.0, A_DK ** -0.5
        FF_TILES = [4, 4, 4, 4, 4, 2]

        def turn_pairs(src):
            done = []
            for j in range(4):
                u = pe.unit()
                if u >= BANKS:
                    nc.tensor.wait_ge(free[u % BANKS], pe.uses(u - BANKS))
                for k in range(2):
                    for t in range(2):
                        last = turn(U(u)[:, k * SEQ + t * P:k * SEQ + (t + 1) * P],
                                    src[:, t, (2 * j + k) * P:(2 * j + k + 1) * P])
                last.then_inc(full[u % BANKS], 1)
                done.append(u)
            for n_out in done:
                nc.tensor.wait_ge(free[n_out % BANKS], pe.uses(n_out))

        def take_pairs(e, dst, gain=None):
            for j in range(4):
                if (j % 2 == 1) != (e is ac):
                    e.unit()
                    continue
                u = e.unit()
                e.eng.wait_ge(full[u % BANKS], e.uses(u))
                if gain is None:
                    o, i = dst[:, 2 * j:2 * j + 2, :].rearrange("p k n -> p (k n)"), U(u)[:, :]
                    (nc.scalar.copy(o, i) if e is ac else nc.vector.tensor_copy(o, i)).then_inc(free[u % BANKS], 1)
                    e.eng.wait_ge(free[u % BANKS], e.uses(u))
                    continue
                for k in range(2):
                    o, i, g = dst[:, 2 * j + k, :], U(u)[:, k * SEQ:(k + 1) * SEQ], gain(2 * j + k)
                    ins = (nc.scalar.activation(o, i, ACT.Copy, scale=g) if e is ac
                           else nc.vector.tensor_scalar(o, i, g, None, ALU.mult))
                    if k:
                        ins.then_inc(free[u % BANKS], 1)
                        e.eng.wait_ge(free[u % BANKS], e.uses(u))
                    else:
                        ins.then_inc(sem[e.name + "_step"], 1)
                        e.eng.wait_ge(sem[e.name + "_step"], e.due(e.name + "_step"))

        def tiles(l):
            return range(4) if l < DEPTH - 1 else range(2)

        def streams(l):
            return range(2) if l < DEPTH - 1 else range(1)

        def jobs(l):
            return [(kind, t, h) for t in tiles(l) for kind in "CD" for h in range(HEADS)]

        PROJ_CHUNKS = [(0, 512), (512, 512), (1024, 512), (1536, 512), (2048, 256)]

        def proj_tiles(l, c):
            return tiles(l) if c == 0 else range(4)

        @block.sync
        def _(eng):
            count = [0]

            def load(src, kt=KT, n=CN):
                q = count[0]
                count[0] += 1
                if q >= RING:
                    nc.sync.wait_ge(sem["chunk_used"], sp.due("chunk_used"))
                elif q == 1:
                    eng.dma_start(X[:, 0:2, :], A["x"][0].rearrange("(t p) n -> p t n", p=P)).then_inc(sem["tokens_in"], 16)
                    eng.dma_start(X[:, 2:4, :], A["ctx"][0].rearrange("(t p) n -> p t n", p=P)).then_inc(sem["tokens_in"], 16)
                    nc.sync.wait_ge(sem["rows_in"], sp.due("rows_in", 16 * 9))
                elif q == 3:
                    nc.sync.wait_ge(sem["smalls"], sp.due("smalls", 16 * 7))
                eng.dma_start(slot[q % RING][:, 0:kt, 0:n], src.rearrange("(k p) n -> p k n", p=P)
                              ).then_inc(sem[f"chunk{q % RING}"], 16)

            for l in range(DEPTH):
                for j in range(4):
                    load(A["ada_w"][l, :, j * CN:(j + 1) * CN])
                for at, n in PROJ_CHUNKS:
                    load(A["w_in"][l, :, at:at + n], n=n)
                for j in range(4, 12):
                    load(A["ada_w"][l, :, j * CN:(j + 1) * CN])
                for c in range(2):
                    load(A["w_out"][l, :, c * CN:(c + 1) * CN])
                with sp.loop(4, expert_turn(len(streams(l)))) as g:
                    for e in range(4):
                        for c in range(2):
                            for w in ("exp_w_gate", "exp_w_up"):
                                load(A[w][l, g * 4 + e, :, c * CN:(c + 1) * CN])
                        for c in range(2):
                            load(A["exp_w_down"][l, g * 4 + e, :, c * CN:(c + 1) * CN])
            with_2 = A["w_in_2"]
            for l in range(DEPTH):
                for at in (W2_QA, W2_KA, W2_VA, W2_VA + CN, W2_OA, W2_OA + CN):
                    load(with_2[l, :, at:at + CN])
                for i in range(6):
                    load(with_2[l, :, W2_QKV + i * CN:W2_QKV + (i + 1) * CN])
                for first in (W2_Z, W2_GA):
                    for c in range(2):
                        load(with_2[l, :, first + c * CN:first + (c + 1) * CN])
                for c in range(2):
                    load(A["w_branch_a_2"][l, :, c * CN:(c + 1) * CN])
                for c in range(2):
                    load(with_2[l, :, W2_GB + c * CN:W2_GB + (c + 1) * CN])
                for c in range(2):
                    load(A["w_branch_b_2"][l, :, c * CN:(c + 1) * CN])
                for c in range(2):
                    load(A["w_out_2"][l, :, c * CN:(c + 1) * CN])
                for i, n in enumerate(FF_TILES):
                    for half in range(2):
                        at = half * D_FF + i * CN
                        load(A["w_ffn_up_2"][l, :, at:at + n * P], n=n * P)
                for c in range(2):
                    for i in range(3):
                        k1 = min(FT, 8 * i + 8)
                        load(A["w_ffn_down_2"][l, 8 * i * P:k1 * P, c * CN:(c + 1) * CN], kt=k1 - 8 * i)

        @block.gpsimd
        def _(eng):
            def get(dst, src, what):
                eng.dma_start(dst, src).then_inc(sem[what], 16)

            def get_rows(l):
                at = 0
                for src in (A["norm1_g"][l].rearrange("(k p) -> k p", p=P), A["norm2_g"][l].rearrange("(k p) -> k p", p=P),
                            A["head_out_g"][l].rearrange("(k p) -> k p", p=P), A["sgu_b"][l],
                            A["c"][0].rearrange("(k p) -> k p", p=P), A["c_ctx"].rearrange("(k p) -> k p", p=P),
                            A["ada_b"][l].rearrange("(k p) -> k p", p=P)):
                    get(ROWS[at:at + src.shape[0], :], src, "rows_in")
                    at += src.shape[0]

            def get_gains(l):
                at = 0
                for name in ("diff_qn_g", "diff_kn_g", "na_qn_g", "na_kn_g"):
                    w = A[name].shape[1]
                    get(m["gains_qk"][:, at:at + w], A[name][l].partition_broadcast(P), "smalls")
                    at += w
                get(m["lam_rows"], A["diff_lambda"][l].rearrange("a b -> (a b)").partition_broadcast(P), "smalls")
                get(RW, A["router_w"][l].rearrange("(k p) e -> p k e", p=P), "smalls")

            def get_first(l):
                get(SGU, A["sgu_w"][l].rearrange("h p q -> p h q"), "smalls")

            get(ident, A["c_ident"], "rows_in")
            get_rows(0)
            get(m["fold"], A["c_fold"], "rows_in")
            get_first(0)
            get_gains(0)
            get(ones, A["c_ones"][:, 0:4], "consts")
            get(m["rope"].rearrange("p (t c) -> p t c", t=2), A["c_rope"].rearrange("(t p) c -> p t c", p=P), "consts")
            get(m["window"], A["c_window"], "consts")
            get(m["slots"], A["c_slots"], "consts")
            get(SEQDFT, A["c_seq_dft"].rearrange("(k p) n -> p k n", p=P), "consts")
            get(HDFT, A["c_head_dft"], "consts")
            rpb = A["na_rpb"]
            for l in range(DEPTH):
                for h in range(HEADS):
                    at = ((l * HEADS + h) * 15 + 4) * 31 + 15 - (GRID_W - 1)
                    src = bass.AP(rpb.tensor, at, [[31, 7], [0, GRID_W], [1, BAND]])
                    get(band[l, h], src, "band_out")
            for l in range(DEPTH):
                if l:
                    nc.gpsimd.wait_ge(sem["x_ready"], gp.due("x_ready", 2))
                if l == 0:
                    nc.gpsimd.wait_ge(sem["band_out"], gp.due("band_out", 16 * DEPTH * HEADS))
                for h in range(HEADS):
                    for r in range(4):
                        at = ((l * HEADS + h) * 7 + 3 - r) * GRID_W * BAND + GRID_W - 1
                        src = bass.AP(band.tensor, at, [[BAND - 1, GRID_W], [GRID_W * BAND, 4], [1, GRID_W]])
                        p0 = (r % 2) * GRID_W
                        dst = BIAS[p0:p0 + GRID_W, r // 2, h, :].rearrange("p (a b) -> p a b", a=4)
                        get(dst, src, "bias_in")
                nc.gpsimd.wait_ge(sem["row_ready"], gp.due("row_ready"))
                for g in range(2):
                    eng.dma_start(gate_scratch[l, g].rearrange("s (k p) -> k s p", p=P),
                                  GATE_ROWS[:, SEQ * g:SEQ * (g + 1)].rearrange("k (s p) -> k s p", s=2)
                                  ).then_inc(sem["row_saved"], 16)
                nc.gpsimd.wait_ge(sem["row_saved"], gp.due("row_saved", 32))
                nc.gpsimd.wait_ge(sem["bias_used"], gp.due("bias_used"))
                for s in streams(l):
                    get(GATE1[:, s, :], gate_scratch[l, 0, s, :].partition_broadcast(P), "gate1_in")
                ns = len(streams(l))
                nc.gpsimd.wait_ge(sem["xg_ready"], gp.due("xg_ready"))
                if l < DEPTH - 1:
                    get_rows(l + 1)
                    get_gains(l + 1)
                if ns == 1:
                    get(GATE2[1][:, 0, :], gate_scratch[l, 1, 0, :].partition_broadcast(P), "gate2_in")
                if l == 0:
                    for j in range(2):
                        eng.memset(XGC[:, j, :, :], 0.0).then_inc(sem["xg_used"], 1)
                        nc.gpsimd.wait_ge(sem["xg_used"], gp.due("xg_used"))
                    gp.local["xg_used"] -= 2
                with gp.loop(4, expert_turn(ns)) as g:
                    for e in range(4):
                        nc.gpsimd.wait_ge(sem["xg_used"], gp.due("xg_used"))
                        eng.tensor_copy(
                            XGC[:, e % 2, :, 0:32 * ns],
                            m["proj"][:, 0:8192].rearrange("p (k e c) -> p k (e c)", k=KT, e=N_EXP)
                            [:, :, bass.ds(g * (4 * 64) + e * 64, 32 * ns)]).then_inc(sem["xgc_ready"], 1)
                        nc.gpsimd.wait_ge(sem["xgc_ready"], gp.due("xgc_ready"))
                nc.gpsimd.wait_ge(sem["moe_done"], gp.due("moe_done"))
                if ns == 2:
                    for s in streams(l):
                        get(GATE2[0][:, s, :], gate_scratch[l, 1, s, :].partition_broadcast(P), "gate2_in")
                if l < DEPTH - 1:
                    get_first(l + 1)
                    get(SEQDFT, A["c_seq_dft"].rearrange("(k p) n -> p k n", p=P), "smalls")
            for l in range(DEPTH):
                if l == 0:
                    get(CAUSAL, A["c_causal_t"], "smalls2")
                    get(STRICT, A["c_strict_t"], "smalls2")
                    get(m2["levels"], A["c_levels"], "smalls2")
                    get(PICK[:, 0:31], A["c_pick"], "smalls2")
                get(m2["rows"][0:96, :], A["conv_w_2"][l].rearrange("i (t p) -> (i t) p", p=P), "smalls2")
                get(m2["rows"][96:104, :], A["g_mlstm_norm_2"][l].rearrange("(k p) -> k p", p=P), "smalls2")
                get(m2["rows"][104:105, :], A["g_gdn_norm_2"][l:l + 1, :], "smalls2")
                get(WG[:, :, 0:8], A["w_in_2"][l, :, W2_I:W2_I + 8].rearrange("(k p) n -> p k n", p=P), "smalls2")
                get(WG[:, :, 8:24], A["w_in_2"][l, :, W2_BETA:W2_BETA + 16].rearrange("(k p) n -> p k n", p=P), "smalls2")
                for i, (name, n) in enumerate((("b_igate_2", 4), ("b_fgate_2", 4), ("dt_bias_2", 8), ("a_log_2", 8))):
                    get(VEC[0:n, i:i + 1], A[name][l].rearrange("(n a) -> n a", a=1), "smalls2")
                nc.gpsimd.wait_ge(sem["heads_done"], gp.due("heads_done"))
                for i, name in enumerate(("ln1_g_2", "ln1_b_2", "ln2_g_2", "ln2_b_2")):
                    get(LNG[:, i, :], A[name][l].partition_broadcast(P), "ln_gains")
            nc.gpsimd.wait_ge(sem["x_ready"], gp.due("x_ready", 4))
            eng.dma_start(out[0].rearrange("(t p) n -> p t n", p=P), X2).then_inc(sem["out_done"], 16)
            nc.gpsimd.wait_ge(sem["out_done"], gp.due("out_done", 16))

        chunks, held, pending = [0], [0], [0]

        def next_chunk():
            q = chunks[0]
            chunks[0] += 1
            nc.tensor.wait_ge(sem[f"chunk{q % RING}"], pe.due(f"chunk{q % RING}", 16))
            pending[0] = held[0]
            held[0] = 1
            return slot[q % RING]

        def release(ins):
            ins.then_inc(sem["chunk_used"], 1)
            held[0] = pending[0] = 0

        def product(o, lhs, rhs, kt, start=True, stop=True):
            for k in range(kt):
                last = mm(o, lhs(k), rhs(k), start=start and k == 0, stop=stop and k == kt - 1)
                if pending[0]:
                    last.then_inc(sem["chunk_used"], 1)
                    pending[0] = 0
            return last

        def halved(o, rows, lhs, rhs):
            for k in range(KT):
                g = k % 2
                last = mm(o[g * rows:(g + 1) * rows, :], lhs(k), rhs(k), start=(k < 2), stop=(k >= KT - 2))
                if pending[0]:
                    last.then_inc(sem["chunk_used"], 1)
                    pending[0] = 0
            return last

        def pe_turn_tiles(src, nt):
            done = []
            for k in range(KT):
                u = pe.unit()
                if u >= BANKS:
                    nc.tensor.wait_ge(free[u % BANKS], pe.uses(u - BANKS))
                for t in range(nt):
                    last = turn(U(u)[:, t * P:(t + 1) * P], src[:, t, k * P:(k + 1) * P])
                last.then_inc(full[u % BANKS], 1)
                done.append(u)
            return done

        @block.tensor
        def _(eng):
            for l in range(DEPTH):
                ns, nt = len(streams(l)), len(tiles(l))
                nc.tensor.wait_ge(sem["rows_in"], pe.due("rows_in", 16 * (9 if l == 0 else 7)))
                u = pe.unit()
                if u >= BANKS:
                    nc.tensor.wait_ge(free[u % BANKS], pe.uses(u - BANKS))
                turn(U(u)[:, 0:92], ROWS[0:92, :]).then_inc(full[u % BANKS], 1)
                if l == 0:
                    nc.tensor.wait_ge(sem["silu_c"], pe.due("silu_c"))

                def ada(j):
                    w = next_chunk()
                    u = pe.unit()
                    if u >= BANKS:
                        nc.tensor.wait_ge(free[u % BANKS], pe.uses(u - BANKS))
                    for k in range(KT):
                        g = k % 4
                        last = mm(U(u)[32 * g:32 * g + 32, :], m["silu_c"][:, 2 * k:2 * k + 32], w[:, k, :],
                                  start=(k < 4), stop=(k >= 4))
                        if pending[0]:
                            last.then_inc(sem["chunk_used"], 1)
                            pending[0] = 0
                    last.then_inc(full[u % BANKS], 1)
                    return u

                def ada_fold(j):
                    nc.tensor.wait_ge(free[rows_of[j] % BANKS], pe.uses(rows_of[j]))
                    u = pe.unit()
                    if u >= BANKS:
                        nc.tensor.wait_ge(free[u % BANKS], pe.uses(u - BANKS))
                    for i in range(4):
                        last = mm(U(u)[:, 2 * i:2 * i + 2], ROWBUF[:, j % 2, i * P:(i + 1) * P], FOLD_ROWS,
                                  start=True, stop=True)
                    last.then_inc(full[u % BANKS], 1)

                rows_of = {0: ada(0)}
                for j in range(4):
                    if j < 3:
                        rows_of[j + 1] = ada(j + 1)
                    ada_fold(j)
                nc.tensor.wait_ge(sem["smalls"], pe.due("smalls", 16 * (7 + (l > 0))))
                u = pe.unit()
                if u >= BANKS:
                    nc.tensor.wait_ge(free[u % BANKS], pe.uses(u - BANKS))
                for h in range(HEADS):
                    last = turn(U(u)[:, h * P:(h + 1) * P], SGU[:, h, :])
                last.then_inc(full[u % BANKS], 1)
                nc.tensor.wait_ge(sem["xn_ready"], pe.due("xn_ready", 4))
                ht = pe_turn_tiles(XN, 4)
                for n_out in ht:
                    nc.tensor.wait_ge(free[n_out % BANKS], pe.uses(n_out))
                proj = {}
                for c, (at, n) in enumerate(PROJ_CHUNKS):
                    w = next_chunk()
                    for t in proj_tiles(l, c):
                        u = pe.unit()
                        if u >= BANKS:
                            nc.tensor.wait_ge(free[u % BANKS], pe.uses(u - BANKS))
                        product(U(u)[:, 0:n], lambda k: HT[:, k, t * P:(t + 1) * P],
                                                 lambda k: w[:, k, 0:n], KT).then_inc(full[u % BANKS], 1)
                        proj[c, t] = u
                if l == 0:
                    nc.tensor.wait_ge(sem["consts"], pe.due("consts", 16 * 6))
                for n_out in [u for (c, t), u in proj.items() if c == 1]:
                    nc.tensor.wait_ge(free[n_out % BANKS], pe.uses(n_out))
                first = {}
                for s in streams(l):
                    for b in range(2):
                        u = pe.unit()
                        if u >= BANKS:
                            nc.tensor.wait_ge(free[u % BANKS], pe.uses(u - BANKS))
                        for t in range(2):
                            last = mm(U(u)[:, :], PROJ[:, 2 * s + t, B_Z + b * P:B_Z + (b + 1) * P],
                                      SEQDFT[:, t, :], start=(t == 0), stop=(t == 1))
                            if held[0]:
                                release(last)
                        last.then_inc(full[u % BANKS], 1)
                        first[s, b] = u
                for s in streams(l):
                    for n_out in (first[s, 0], first[s, 1]):
                        nc.tensor.wait_ge(free[n_out % BANKS], pe.uses(n_out))
                    for t in range(2):
                        u = pe.unit()
                        if u >= BANKS:
                            nc.tensor.wait_ge(free[u % BANKS], pe.uses(u - BANKS))
                        for b in range(2):
                            for part in range(2):
                                last = mm(U(u)[:, b * P:(b + 1) * P],
                                          PT[:, s, b, part * SEQ + t * P:part * SEQ + (t + 1) * P],
                                          HDFT[:, part * P:(part + 1) * P], start=(part == 0), stop=(part == 1))
                        last.then_inc(full[u % BANKS], 1)
                for t in tiles(l):
                    nc.tensor.wait_ge(sem["vn_ready"], pe.due("vn_ready"))
                    u = pe.unit()
                    if u >= BANKS:
                        nc.tensor.wait_ge(free[u % BANKS], pe.uses(u - BANKS))
                    for h in range(HEADS):
                        last = mm(U(u)[:, h * HD:(h + 1) * HD], SGUT[:, h, :],
                                  PROJ[:, t, A_V + h * HD:A_V + (h + 1) * HD], start=True, stop=True)
                    last.then_inc(full[u % BANKS], 1)
                last_proj = [u for (c, t), u in proj.items()]
                qk = []
                for t in range(4):
                    nc.tensor.wait_ge(sem["qk_ready"], pe.due("qk_ready"))
                    for at in (C_Q, D_Q):
                        u = pe.unit()
                        if u >= BANKS:
                            nc.tensor.wait_ge(free[u % BANKS], pe.uses(u - BANKS))
                        for b in range(4):
                            last = turn(U(u)[:, b * P:(b + 1) * P], PROJ[:, t, at + b * P:at + (b + 1) * P])
                        last.then_inc(full[u % BANKS], 1)
                        qk.append(u)
                for n_out in qk:
                    nc.tensor.wait_ge(free[n_out % BANKS], pe.uses(n_out))

                todo = jobs(l)

                def keys(t):
                    return (0, 512) if t < 2 else (SEQ, SEQ)

                def scores(i):
                    kind, t, h = todo[i]
                    k0, nk = keys(t)
                    for q in range(2 if kind == "C" else 1):
                        w = DIFF_D if kind == "C" else HD
                        r = (h % 2) * HD + q * DIFF_D
                        T = QKT[0 if kind == "C" else 1]
                        u = pe.unit()
                        if u >= BANKS:
                            nc.tensor.wait_ge(free[u % BANKS], pe.uses(u - BANKS))
                        score_of[i] = u
                        mm(U(u)[:, 0:nk], T[r:r + w, h // 2, t * P:(t + 1) * P],
                                            T[r:r + w, 2 + h // 2, k0:k0 + nk], start=True, stop=True).then_inc(full[u % BANKS], 1)

                wt_of, score_of = {}, {}

                def turn_weights(i):
                    kind, t, h = todo[i]
                    k0, nk = keys(t)
                    if kind == "C":
                        nc.tensor.wait_ge(sem["w_diff"], pe.due("w_diff"))
                    else:
                        nc.tensor.wait_ge(free[score_of[i] % BANKS], pe.uses(score_of[i]))
                    u = pe.unit()
                    if u >= BANKS:
                        nc.tensor.wait_ge(free[u % BANKS], pe.uses(u - BANKS))
                    for b in range(nk // P):
                        last = turn(U(u)[:, b * P:(b + 1) * P], W[:, i % 2, b * P:(b + 1) * P])
                    last.then_inc(full[u % BANKS], 1)
                    wt_of[i] = u

                def values(i):
                    kind, t, h = todo[i]
                    k0, nk = keys(t)
                    v = (C_V if kind == "C" else D_V) + h * HD
                    nc.tensor.wait_ge(free[wt_of[i] % BANKS], pe.uses(wt_of[i]))
                    u = pe.unit()
                    if u >= BANKS:
                        nc.tensor.wait_ge(free[u % BANKS], pe.uses(u - BANKS))
                    for b in range(nk // P):
                        last = mm(U(u)[:, 0:HD], WT[:, i % 2, b * P:(b + 1) * P],
                                  PROJ[:, k0 // P + b, v:v + HD], start=(b == 0), stop=(b == nk // P - 1))
                    last.then_inc(full[u % BANKS], 1)

                n = len(todo)
                scores(0)
                scores(1)
                for i in range(n):
                    if i + 2 < n:
                        scores(i + 2)
                    turn_weights(i)
                    if i:
                        values(i - 1)
                    if i % (n // 8) == 0:
                        j = 4 + i // (n // 8)
                        rows_of[j] = ada(j)
                        if j > 4:
                            ada_fold(j - 1)
                values(n - 1)
                ada_fold(11)
                nc.tensor.wait_ge(sem["mod_ready"], pe.due("mod_ready"))
                u = pe.unit()
                if u >= BANKS:
                    nc.tensor.wait_ge(free[u % BANKS], pe.uses(u - BANKS))
                for g in range(2):
                    for s in range(2):
                        last = turn(U(u)[0:8, (2 * g + s) * P:(2 * g + s + 1) * P], MOD[:, 16 + 24 * g:24 + 24 * g, s])
                last.then_inc(full[u % BANKS], 1)
                nc.tensor.wait_ge(sem["xn_ready"], pe.due("xn_ready", nt))
                ht = pe_turn_tiles(XN, nt)
                for n_out in ht:
                    nc.tensor.wait_ge(free[n_out % BANKS], pe.uses(n_out))
                for c in range(2):
                    w = next_chunk()
                    for t in tiles(l):
                        u = pe.unit()
                        if u >= BANKS:
                            nc.tensor.wait_ge(free[u % BANKS], pe.uses(u - BANKS))
                        product(U(u)[:, :], lambda k: HT[:, k, t * P:(t + 1) * P],
                                                 lambda k: w[:, k, :], KT).then_inc(full[u % BANKS], 1)
                nc.tensor.wait_ge(sem["xn_ready"], pe.due("xn_ready", nt))
                ht = pe_turn_tiles(XN, nt)
                for n_out in ht:
                    nc.tensor.wait_ge(free[n_out % BANKS], pe.uses(n_out))
                u = pe.unit()
                if u >= BANKS:
                    nc.tensor.wait_ge(free[u % BANKS], pe.uses(u - BANKS))
                for k in range(KT):
                    last = mm(U(u)[0:N_EXP, 0:nt * P], RW[:, k, :], HT[:, k, 0:nt * P],
                              start=(k == 0), stop=(k == KT - 1))
                last.then_inc(full[u % BANKS], 1)
                nc.tensor.wait_ge(free[u % BANKS], pe.uses(u))
                u = pe.unit()
                if u >= BANKS:
                    nc.tensor.wait_ge(free[u % BANKS], pe.uses(u - BANKS))
                for t in tiles(l):
                    last = turn(U(u)[:, t * N_EXP:(t + 1) * N_EXP], AFFT[0:N_EXP, t * P:(t + 1) * P])
                last.then_inc(full[u % BANKS], 1)
                nc.tensor.wait_ge(sem["aff_ready"], pe.due("aff_ready"))
                u = pe.unit()
                if u >= BANKS:
                    nc.tensor.wait_ge(free[u % BANKS], pe.uses(u - BANKS))
                for t in tiles(l):
                    last = turn(U(u)[0:N_EXP, t * P:(t + 1) * P], AFF[:, t, :])
                last.then_inc(full[u % BANKS], 1)
                nc.tensor.wait_ge(sem["rank_ready"], pe.due("rank_ready"))
                u = pe.unit()
                if u >= BANKS:
                    nc.tensor.wait_ge(free[u % BANKS], pe.uses(u - BANKS))
                for t in tiles(l):
                    last = turn(U(u)[:, t * N_EXP:(t + 1) * N_EXP], RANK[0:N_EXP, t * P:(t + 1) * P])
                last.then_inc(full[u % BANKS], 1)
                nc.tensor.wait_ge(sem["sel_ready"], pe.due("sel_ready", nt))
                for k in range(KT):
                    for s in streams(l):
                        u = pe.unit()
                        if u >= BANKS:
                            nc.tensor.wait_ge(free[u % BANKS], pe.uses(u - BANKS))
                        for t in range(2):
                            last = mm(U(u)[:, :], XN[:, 2 * s + t, k * P:(k + 1) * P],
                                      SEL[:, 2 * s + t, :, :].rearrange("p e c -> p (e c)"),
                                      start=(t == 0), stop=(t == 1))
                        last.then_inc(full[u % BANKS], 1)
                for t in tiles(l):
                    nc.tensor.wait_ge(sem["selg_ready"], pe.due("selg_ready"))
                    u = pe.unit()
                    if u >= BANKS:
                        nc.tensor.wait_ge(free[u % BANKS], pe.uses(u - BANKS))
                    for b in range(4):
                        last = turn(U(u)[:, b * P:(b + 1) * P],
                                    SEL[:, t, 4 * b:4 * b + 4, :].rearrange("p e c -> p (e c)"))
                    last.then_inc(full[u % BANKS], 1)
                M = 32 * ns
                with pe.loop(4, expert_turn(ns)) as g:
                    for e in range(4):
                        nc.tensor.wait_ge(sem["xgc_ready"], pe.due("xgc_ready"))
                        ups, halves = [], []
                        for c in range(2):
                            for w_i in range(2):
                                w = next_chunk()
                                u = pe.unit()
                                if u >= BANKS:
                                    nc.tensor.wait_ge(free[u % BANKS], pe.uses(u - BANKS))
                                last = halved(U(u), M, lambda k: XGC[:, e % 2, k, 0:M], lambda k: w[:, k, :])
                                last.then_inc(full[u % BANKS], 1)
                                ups.append(u)
                        for c in range(2):
                            for n_out in (ups[2 * c], ups[2 * c + 1]):
                                nc.tensor.wait_ge(free[n_out % BANKS], pe.uses(n_out))
                            u = pe.unit()
                            if u >= BANKS:
                                nc.tensor.wait_ge(free[u % BANKS], pe.uses(u - BANKS))
                            for j, parts in enumerate((GATE_PARTS, UP_PARTS)):
                                for i in range(4):
                                    last = mm(U(u)[:, (4 * j + i) * M:(4 * j + i + 1) * M],
                                              parts[0:2 * M, c, i * P:(i + 1) * P], FOLD[M], start=True, stop=True)
                                    if c == 0 and i == 0 and j == 0:
                                        last.then_inc(sem["xg_used"], 1)
                            last.then_inc(full[u % BANKS], 1)
                            halves.append(u)
                        for n_out in halves:
                            nc.tensor.wait_ge(free[n_out % BANKS], pe.uses(n_out))
                        for c in range(2):
                            w = next_chunk()
                            u = pe.unit()
                            if u >= BANKS:
                                nc.tensor.wait_ge(free[u % BANKS], pe.uses(u - BANKS))
                            last = halved(U(u), M, lambda k: HIDT[:, k, 0:M], lambda k: w[:, k, :])
                            last.then_inc(full[u % BANKS], 1)
                nc.tensor.wait_ge(sem["moe_done"], pe.due("moe_done"))
                for c in range(2):
                    for t in tiles(l):
                        s = t // 2
                        u = pe.unit()
                        if u >= BANKS:
                            nc.tensor.wait_ge(free[u % BANKS], pe.uses(u - BANKS))
                        for b in range(4):
                            last = mm(U(u)[:, :], SELT[:, s, b, (t % 2) * P:(t % 2 + 1) * P],
                                      OEXP[s][:, b, c * CN:(c + 1) * CN], start=(b == 0), stop=(b == 3))
                            if held[0]:
                                release(last)
                        last.then_inc(full[u % BANKS], 1)
            def across(row, n):
                return ident[0:n, row:row + 1].broadcast_to([n, P])

            def by_features(tiles_n):
                w = next_chunk()
                us = []
                for j in range(0, tiles_n, 2):
                    u = pe.unit()
                    if u >= BANKS:
                        nc.tensor.wait_ge(free[u % BANKS], pe.uses(u - BANKS))
                    for c in range(2):
                        last = product(U(u)[:, c * SEQ:(c + 1) * SEQ], lambda k: w[:, k, (j + c) * P:(j + c + 1) * P],
                                       lambda k: XT2[:, k, :], KT)
                    last.then_inc(full[u % BANKS], 1)
                    us.append(u)
                return us

            def by_tokens(T, n_chunks=2):
                us = []
                for c in range(n_chunks):
                    w = next_chunk()
                    for t in range(2):
                        u = pe.unit()
                        if u >= BANKS:
                            nc.tensor.wait_ge(free[u % BANKS], pe.uses(u - BANKS))
                        product(U(u)[:, :], lambda k: T[:, k, t * P:(t + 1) * P],
                                                 lambda k: w[:, k, :], KT).then_inc(full[u % BANKS], 1)
                        us.append(u)
                return us

            for l in range(DEPTH):
                nc.tensor.wait_ge(sem["smalls2"], pe.due("smalls2", 16 * (13 if l == 0 else 9)))
                u = pe.unit()
                if u >= BANKS:
                    nc.tensor.wait_ge(free[u % BANKS], pe.uses(u - BANKS))
                turn(U(u)[:, 0:105], m2["rows"][0:105, :]).then_inc(full[u % BANKS], 1)
                if l:
                    nc.tensor.wait_ge(sem["x_ready"], pe.due("x_ready", 1))
                else:
                    nc.tensor.wait_ge(sem["x_ready"], pe.due("x_ready", 4))
                turn_pairs(X2)
                u = pe.unit()
                if u >= BANKS:
                    nc.tensor.wait_ge(free[u % BANKS], pe.uses(u - BANKS))
                for i in range(2):
                    last = product(U(u)[0:4, i * SEQ:(i + 1) * SEQ], lambda k: WG[:, k, 4 * i:4 * i + 4],
                                   lambda k: XT2[:, k, :], KT)
                last.then_inc(full[u % BANKS], 1)
                qk = by_features(4) + by_features(4)
                va = by_tokens(XT2) 
                by_tokens(XT2)
                nc.tensor.wait_ge(sem["mg_rows"], pe.due("mg_rows"))
                nc.tensor.wait_ge(sem["mg_en"], pe.due("mg_en"))
                u = pe.unit()
                if u >= BANKS:
                    nc.tensor.wait_ge(free[u % BANKS], pe.uses(u - BANKS))
                for i, r in enumerate((4, 6)):
                    for t in range(2):
                        last = turn(U(u)[:, 8 * i + 4 * t:8 * i + 4 * t + 4], GR[0:4, r, t * P:(t + 1) * P])
                last.then_inc(full[u % BANKS], 1)
                for n_out in qk:
                    nc.tensor.wait_ge(free[n_out % BANKS], pe.uses(n_out))
                for pair in range(2):
                    u = pe.unit()
                    if u >= BANKS:
                        nc.tensor.wait_ge(free[u % BANKS], pe.uses(u - BANKS))
                    for j in range(2):
                        last = mm(U(u)[:, j * SEQ:(j + 1) * SEQ], across(2 * pair + j, 4), GR[0:4, 5, :],
                                  start=True, stop=True)
                    last.then_inc(full[u % BANKS], 1)
                    scored = []
                    for j in range(2):
                        h = 2 * pair + j
                        u = pe.unit()
                        if u >= BANKS:
                            nc.tensor.wait_ge(free[u % BANKS], pe.uses(u - BANKS))
                        mm(U(u)[:, 0:SEQ], KA[:, h, 0:P], QA[:, h, :], start=True, stop=True)
                        mm(U(u)[:, SEQ:SEQ + P], KA[:, h, P:SEQ], QA[:, h, P:SEQ], start=True, stop=True).then_inc(full[u % BANKS], 1)
                        scored.append(u)
                    for n_out in va:
                        nc.tensor.wait_ge(free[n_out % BANKS], pe.uses(n_out))
                    for j in range(2):
                        h = 2 * pair + j
                        nc.tensor.wait_ge(free[scored[j] % BANKS], pe.uses(scored[j]))
                        u = pe.unit()
                        if u >= BANKS:
                            nc.tensor.wait_ge(free[u % BANKS], pe.uses(u - BANKS))
                        mm(U(u)[:, 0:257], PA[:, h, 0:P], VA[:, 0, h, :], start=True, stop=True).then_inc(full[u % BANKS], 1)
                        u = pe.unit()
                        if u >= BANKS:
                            nc.tensor.wait_ge(free[u % BANKS], pe.uses(u - BANKS))
                        mm(U(u)[:, 0:257], PA[:, h, P:SEQ], VA[:, 0, h, :], start=True, stop=False)
                        mm(U(u)[:, 0:257], PA[:, h, SEQ:SEQ + P], VA[:, 1, h, :], start=False, stop=True).then_inc(full[u % BANKS], 1)
                u = pe.unit()
                if u >= BANKS:
                    nc.tensor.wait_ge(free[u % BANKS], pe.uses(u - BANKS))
                for i in range(2):
                    last = product(U(u)[0:8, i * SEQ:(i + 1) * SEQ], lambda k: WG[:, k, 8 + 8 * i:16 + 8 * i],
                                   lambda k: XT2[:, k, :], KT)
                last.then_inc(full[u % BANKS], 1)
                for i in range(6):
                    by_features(4)
                    if i == 2:
                        nc.tensor.wait_ge(sem["ha_ready"], pe.due("ha_ready", 2))
                        turn_pairs(HA)
                u = pe.unit()
                if u >= BANKS:
                    nc.tensor.wait_ge(free[u % BANKS], pe.uses(u - BANKS))
                for r in range(16):
                    if r % 2 == 0:
                        nc.tensor.wait_ge(sem["sq_ready"], pe.due("sq_ready"))
                    last = mm(U(u)[0:16, 0:SEQ], PICK[:, 15 - r:31 - r],
                              SCR2[:, 1024 + 512 * (r // 2 % 2) + SEQ * (r % 2):1024 + 512 * (r // 2 % 2) + SEQ * (r % 2) + SEQ],
                              start=(r == 0), stop=(r == 15))
                    if r % 2 and r < 15:
                        last.then_inc(sem["sq_used"], 1)
                last.then_inc(full[u % BANKS], 1)
                nc.tensor.wait_ge(sem["rn_ready"], pe.due("rn_ready"))
                units = []
                for r in range(0, 16, 2):
                    u = pe.unit()
                    if u >= BANKS:
                        nc.tensor.wait_ge(free[u % BANKS], pe.uses(u - BANKS))
                    for j in range(2):
                        last = mm(U(u)[:, j * SEQ:(j + 1) * SEQ], across(r + j, 16), R16[0:16, :], start=True, stop=True)
                    last.then_inc(full[u % BANKS], 1)
                    units.append(u)
                for n_out in units:
                    nc.tensor.wait_ge(free[n_out % BANKS], pe.uses(n_out))
                nc.tensor.wait_ge(sem["bg_rows"], pe.due("bg_rows"))
                u = pe.unit()
                if u >= BANKS:
                    nc.tensor.wait_ge(free[u % BANKS], pe.uses(u - BANKS))
                for i, (r, t) in enumerate(((0, 0), (0, 1), (1, 0), (1, 1), (2, 1), (3, 0))):
                    last = turn(U(u)[:, 8 * i:8 * i + 8], GR[0:8, r, t * P:(t + 1) * P])
                last.then_inc(full[u % BANKS], 1)
                nc.tensor.wait_ge(free[u % BANKS], pe.uses(u))

                def delta(b):
                    m = DELTA[b % 2]
                    hs = (2 * b, 2 * b + 1)
                    quad_of = [(h, c) for h in hs for c in range(2)]

                    def four(lhs, rhs, n=4):
                        u = pe.unit()
                        if u >= BANKS:
                            nc.tensor.wait_ge(free[u % BANKS], pe.uses(u - BANKS))
                        for i in range(n):
                            last = mm(U(u)[:, i * P:(i + 1) * P], lhs(i), rhs(i), start=True, stop=True)
                        last.then_inc(full[u % BANKS], 1)
                        return u

                    def four_turned(src):
                        u = pe.unit()
                        if u >= BANKS:
                            nc.tensor.wait_ge(free[u % BANKS], pe.uses(u - BANKS))
                        for i in range(4):
                            last = turn(U(u)[:, i * P:(i + 1) * P], src(i))
                        last.then_inc(full[u % BANKS], 1)
                        return u

                    tok = lambda T: (lambda i: T[:, quad_of[i][0], quad_of[i][1] * P:(quad_of[i][1] + 1) * P])
                    for r in (4, 0):
                        u = pe.unit()
                        if u >= BANKS:
                            nc.tensor.wait_ge(free[u % BANKS], pe.uses(u - BANKS))
                        for j in range(2):
                            last = mm(U(u)[:, j * SEQ:(j + 1) * SEQ], across(hs[j], 8), GR[0:8, r, :],
                                      start=True, stop=True)
                        last.then_inc(full[u % BANKS], 1)
                    four(tok(KB), tok(QB))
                    four(tok(KB), tok(KB))
                    k_unit = four_turned(tok(KB))
                    v_unit = four_turned(tok(VB))
                    yield
                    nc.tensor.wait_ge(sem["at_ready"], pe.due("at_ready"))
                    four_turned(lambda i: m.a_t[:, i, :])
                    yield
                    nc.tensor.wait_ge(sem["x0_ready"], pe.due("x0_ready"))
                    for s in range(1, 7):
                        y = four(lambda i: m.a_t[:, i, :], lambda i: m.inv[:, i, :])
                        yield
                        nc.tensor.wait_ge(free[y % BANKS], pe.uses(y))
                        ups = []
                        if s < 6:
                            ups.append(four(lambda i: m.inv_t[:, i, :], lambda i: m.y[:, i, :]))
                        ups.append(four(lambda i: m.y[:, i, :], lambda i: m.inv_t[:, i, :]))
                        yield
                        for n_out in ups:
                            nc.tensor.wait_ge(free[n_out % BANKS], pe.uses(n_out))
                    for n_out in (k_unit, v_unit):
                        nc.tensor.wait_ge(free[n_out % BANKS], pe.uses(n_out))
                    uu = four(lambda i: m.inv_t[:, i, :], lambda i: m.v[:, i, :])
                    wt = four(lambda j: m.k[:, 2 * j + 1, :], lambda j: m.inv_t[:, 2 * j + 1, :], n=2)
                    yield
                    nc.tensor.wait_ge(free[uu % BANKS], pe.uses(uu))
                    st = four(lambda j: m.k[:, 2 * j, :], lambda j: m.u[:, 2 * j, :], n=2)
                    yield
                    for n_out in (wt, st):
                        nc.tensor.wait_ge(free[n_out % BANKS], pe.uses(n_out))
                    ws = four(lambda j: m.w_t[:, j, :], lambda j: m.state[:, j, :], n=2)
                    yield
                    nc.tensor.wait_ge(free[ws % BANKS], pe.uses(ws))
                    u = pe.unit()
                    if u >= BANKS:
                        nc.tensor.wait_ge(free[u % BANKS], pe.uses(u - BANKS))
                    for i in range(4):
                        second = i % 2 == 1
                        last = mm(U(u)[:, i * P:(i + 1) * P], m.attn[:, i, :], m.u[:, i, :], start=True, stop=not second)
                        if second:
                            last = mm(U(u)[:, i * P:(i + 1) * P], m.q[:, i // 2, :], m.state[:, i // 2, :],
                                      start=False, stop=True)
                    last.then_inc(full[u % BANKS], 1)

                for b in (0, 2):
                    in_turn(delta(b), delta(b + 1))
                by_tokens(XT2)
                by_tokens(XT2)
                by_tokens(HAT)
                by_tokens(XT2)
                nc.tensor.wait_ge(sem["hb_ready"], pe.due("hb_ready", 2))
                turn_pairs(HBN)
                by_tokens(XT2)
                nc.tensor.wait_ge(sem["y_ready"], pe.due("y_ready"))
                turn_pairs(SGA)
                by_tokens(HAT)
                nc.tensor.wait_ge(sem["ln_ready"], pe.due("ln_ready", 2))
                turn_pairs(X2)
                for n in FF_TILES:
                    by_features(n)
                    ffn = by_features(n)
                for n_out in ffn:
                    nc.tensor.wait_ge(free[n_out % BANKS], pe.uses(n_out))
                for c in range(2):
                    us = [pe.unit(), pe.unit()]
                    for n_out in us:
                        nc.tensor.wait_ge(free[n_out % BANKS], pe.uses(n_out - BANKS))
                    for i in range(3):
                        w = next_chunk()
                        k1 = min(FT, 8 * i + 8)
                        for t in range(2):
                            last = product(U(us[t])[:, :], lambda k: HFF[:, 8 * i + k, t * P:(t + 1) * P],
                                           lambda k: w[:, k, :], k1 - 8 * i, start=(i == 0), stop=(i == 2))
                            if i == 2:
                                last.then_inc(full[us[t] % BANKS], 1)

        def ac_roots(src, n_terms):
            return nc.scalar.activation(src, src, ACT.Sqrt, scale=1.0 / n_terms, bias=EPS)

        def ac_square_sums(nt):
            for t in range(nt):
                nc.scalar.activation(XN[:, t, :], X[:, t, :], ACT.Square, accum_out=SST[:, t:t + 1]).then_inc(sem["scalar_step"], 1)
                nc.scalar.wait_ge(sem["scalar_step"], ac.due("scalar_step"))
            ac_roots(SST[:, 0:nt], D).then_inc(sem["root"], 1)
            nc.scalar.wait_ge(sem["root"], ac.due("root"))

        def modulated(e, k, n, nt, gain, shift):
            u = e.unit()
            e.eng.wait_ge(full[u % BANKS], e.uses(u))
            for s in range(nt // 2):
                o, i = HT[:, k, s * SEQ:(s + 1) * SEQ], U(u)[:, s * SEQ:(s + 1) * SEQ]
                g, b = gain[:, k, s:s + 1], shift[:, k, s:s + 1]
                if e is ac:
                    ins = nc.scalar.activation(o, i, ACT.Identity, scale=g, bias=b)
                else:
                    ins = nc.vector.tensor_scalar(o, i, g, b, ALU.mult, ALU.add)
                if s == nt // 2 - 1:
                    ins.then_inc(free[u % BANKS], 1)
                    e.eng.wait_ge(free[u % BANKS], e.uses(u))
            return u

        def gathered(e, k, s):
            u = e.unit()
            e.eng.wait_ge(full[u % BANKS], e.uses(u))
            o = XG[:, k, :, 32 * s:32 * s + 32]
            i = U(u)[:, :].rearrange("p (e c) -> p e c", e=N_EXP)
            g, b = GAIN[1][:, k, s:s + 1], SHIFT[1][:, k, s:s + 1]
            if e is ac:
                nc.scalar.activation(o, i, ACT.Identity, scale=g, bias=b).then_inc(free[u % BANKS], 1)
                e.eng.wait_ge(free[u % BANKS], e.uses(u))
            else:
                nc.vector.tensor_scalar(o, i, g, b, ALU.mult, ALU.add).then_inc(free[u % BANKS], 1)
                e.eng.wait_ge(free[u % BANKS], e.uses(u))
            return u

        @block.scalar
        def _(eng):
            act = nc.scalar.activation
            for l in range(DEPTH):
                ns, nt = len(streams(l)), len(tiles(l))
                u_cols = ac.unit()
                if l == 0:
                    nc.scalar.wait_ge(free[u_cols % BANKS], ac.uses(u_cols))
                    act(SC, COLS[:, 28:44].rearrange("p (s k) -> p k s", s=2), ACT.Silu).then_inc(sem["silu_c"], 1)
                    nc.scalar.wait_ge(sem["silu_c"], ac.due("silu_c"))
                    nc.scalar.wait_ge(sem["tokens_in"], ac.due("tokens_in", 32))
                ac.unit(4 + 4 + 1)
                if l:
                    nc.scalar.wait_ge(sem["x_ready"], ac.due("x_ready"))
                ac_square_sums(4)
                for k in range(KT):
                    if k % 2:
                        if k == 1:
                            nc.scalar.wait_ge(sem["lam_dot"], ac.due("lam_dot"))
                        modulated(ac, k, 4, 4, GAIN[0], SHIFT[0])
                    else:
                        ac.unit()
                for c, (at, n) in enumerate(PROJ_CHUNKS):
                    for t in proj_tiles(l, c):
                        if c == 0:
                            u = ac.unit()
                            nc.scalar.wait_ge(full[u % BANKS], ac.uses(u))
                            act(PROJ[:, t, at:at + n], U(u)[:, 0:n], ACT.Gelu_apprx_tanh).then_inc(free[u % BANKS], 1)
                            nc.scalar.wait_ge(free[u % BANKS], ac.uses(u))
                        elif t % 2:
                            u = ac.unit()
                            nc.scalar.wait_ge(full[u % BANKS], ac.uses(u))
                            nc.scalar.copy(PROJ[:, t, at:at + n], U(u)[:, 0:n]).then_inc(free[u % BANKS], 1)
                            nc.scalar.wait_ge(free[u % BANKS], ac.uses(u))
                        else:
                            ac.unit()
                    if c == 2:
                        nc.scalar.wait_ge(sem["stat"], ac.due("stat"))
                        ac_roots(SS28[:, 0:nt, 0:4], HD).then_inc(sem["scalar_step"], 1)
                        nc.scalar.wait_ge(sem["scalar_step"], ac.due("scalar_step"))
                        ac_roots(SS28[:, :, 4:20], DIFF_D).then_inc(sem["root"], 1)
                        nc.scalar.wait_ge(sem["root"], ac.due("root"))
                    elif c == 3:
                        nc.scalar.wait_ge(sem["stat"], ac.due("stat"))
                        ac_roots(SS28[:, :, 20:28], HD).then_inc(sem["root"], 1)
                        nc.scalar.wait_ge(sem["root"], ac.due("root"))
                act(m["lam"][:, 0:2], m["lam"][:, 0:2], ACT.Exp).then_inc(sem["lam_exp"], 1)
                nc.scalar.wait_ge(sem["lam_exp"], ac.due("lam_exp"))
                for s in streams(l):
                    for b in range(2):
                        u = ac.unit()
                        nc.scalar.wait_ge(full[u % BANKS], ac.uses(u))
                        nc.scalar.copy(PT[:, s, b, :], U(u)[:, :]).then_inc(free[u % BANKS], 1)
                        nc.scalar.wait_ge(free[u % BANKS], ac.uses(u))
                for t in tiles(l):
                    u = ac.unit()
                    nc.scalar.wait_ge(full[u % BANKS], ac.uses(u))
                    nc.scalar.copy(PROJ[:, t, B_Z:B_Z + 256], U(u)[:, 0:256]).then_inc(free[u % BANKS], 1)
                    nc.scalar.wait_ge(free[u % BANKS], ac.uses(u))
                ac.unit(nt)
                for t in range(4):
                    for T in QKT:
                        u = ac.unit()
                        nc.scalar.wait_ge(full[u % BANKS], ac.uses(u))
                        nc.scalar.copy(T[:, :, t * P:(t + 1) * P],
                                                       U(u)[:, :].rearrange("p (b n) -> p b n", b=4)).then_inc(free[u % BANKS], 1)
                        nc.scalar.wait_ge(free[u % BANKS], ac.uses(u))
                todo = jobs(l)
                n = len(todo)

                score_of = {}

                def scores(i):
                    for q in range(2 if todo[i][0] == "C" else 1):
                        score_of[i, q] = ac.unit()

                def exps(i):
                    kind, t, h = todo[i]
                    nk = 512 if t < 2 else SEQ
                    scale = (DIFF_D if kind == "C" else HD) ** -0.5
                    for q in range(2 if kind == "C" else 1):
                        u = score_of[i, q]
                        nc.scalar.wait_ge(full[u % BANKS], ac.uses(u))
                        nc.scalar.wait_ge(sem["row_max"], ac.due("row_max"))
                        o = EXPS[:, i % 2, q, 0:nk] if kind == "C" else W[:, i % 2, 0:nk]
                        col = 2 * (i % 2) + q
                        act(o, U(u)[:, 0:nk], ACT.Exp, scale=scale, bias=SMALL[:, col:col + 1],
                                            accum_out=SMALL[:, 4 + col:5 + col]).then_inc(free[u % BANKS], 1)
                        nc.scalar.wait_ge(free[u % BANKS], ac.uses(u))

                scores(0)
                scores(1)
                exps(0)
                for i in range(n):
                    if i + 2 < n:
                        scores(i + 2)
                    if i + 1 < n:
                        exps(i + 1)
                    nk = 512 if todo[i][1] < 2 else SEQ
                    u = ac.unit()
                    nc.scalar.wait_ge(full[u % BANKS], ac.uses(u))
                    nc.scalar.copy(WT[:, i % 2, 0:nk], U(u)[:, 0:nk]).then_inc(free[u % BANKS], 1)
                    nc.scalar.wait_ge(free[u % BANKS], ac.uses(u))
                    if i:
                        ac.unit()
                    if i % (n // 8) == 0:
                        ac.unit(2 if i else 1)
                ac.unit(3)
                nc.scalar.wait_ge(sem["stat"], ac.due("stat"))
                ac_roots(SS[:, 0:16 * nt], HD).then_inc(sem["root"], 1)
                nc.scalar.wait_ge(sem["root"], ac.due("root"))
                for k in range(KT):
                    if k % 2:
                        u = ac.unit()
                        nc.scalar.wait_ge(full[u % BANKS], ac.uses(u))
                        act(HT[:, k, 0:nt * P], U(u)[:, 0:nt * P], ACT.Copy, scale=COLS[:, 16 + k:17 + k]).then_inc(free[u % BANKS], 1)
                        nc.scalar.wait_ge(free[u % BANKS], ac.uses(u))
                    else:
                        ac.unit()
                ac.unit(2 * nt)
                nc.scalar.wait_ge(sem["x_ready"], ac.due("x_ready", 1))
                ac_square_sums(nt)
                for k in range(KT):
                    if k % 2:
                        modulated(ac, k, 4, nt, GAIN[1], SHIFT[1])
                    else:
                        ac.unit()
                ac.unit(2)
                nc.scalar.wait_ge(sem["logit"], ac.due("logit"))
                act(AFF[:, 0:nt, :], AFF[:, 0:nt, :], ACT.Exp).then_inc(sem["logit_exp"], 1)
                nc.scalar.wait_ge(sem["logit_exp"], ac.due("logit_exp"))
                ac.unit(2)
                for k in range(KT):
                    for s in streams(l):
                        if k % 2:
                            gathered(ac, k, s)
                        else:
                            ac.unit()
                for t in tiles(l):
                    u = ac.unit()
                    nc.scalar.wait_ge(full[u % BANKS], ac.uses(u))
                    nc.scalar.copy(SELT[:, t // 2, :, (t % 2) * P:(t % 2 + 1) * P],
                                                   U(u)[:, :].rearrange("p (b n) -> p b n", b=4)).then_inc(free[u % BANKS], 1)
                    nc.scalar.wait_ge(free[u % BANKS], ac.uses(u))
                M = 32 * ns
                with ac.loop(4, expert_turn(ns)) as g:
                    for e in range(4):
                        for c in range(2):
                            u = ac.unit()
                            nc.scalar.wait_ge(full[u % BANKS], ac.uses(u))
                            nc.scalar.copy(GATE_PARTS[0:2 * M, c, :], U(u)[0:2 * M, :]).then_inc(free[u % BANKS], 1)
                            nc.scalar.wait_ge(free[u % BANKS], ac.uses(u))
                            ac.unit()
                        for c in range(2):
                            u = ac.unit()
                            nc.scalar.wait_ge(full[u % BANKS], ac.uses(u))
                            act(HIDT[:, 4 * c:4 * c + 4, 0:M],
                                                    U(u)[:, 0:4 * M].rearrange("p (k c) -> p k c", k=4), ACT.Silu).then_inc(sem["hid_silu"], 1)
                            nc.scalar.wait_ge(sem["hid_silu"], ac.due("hid_silu"))
                        for c in range(2):
                            if c:
                                nc.scalar.wait_ge(free[u % BANKS], ac.uses(u))
                            u = ac.unit()
                            nc.scalar.wait_ge(full[u % BANKS], ac.uses(u))
                            nc.scalar.copy(DOWN_PART[0:M, :], U(u)[M:2 * M, :]).then_inc(sem["down_part"], 1)
                            nc.scalar.wait_ge(sem["down_part"], ac.due("down_part"))
                ac.unit(2 * nt)
            for l in range(DEPTH):
                u = ac.unit()
                nc.scalar.wait_ge(free[u % BANKS], ac.uses(u))
                take_pairs(ac, XT2)
                nc.scalar.wait_ge(sem["vecs_ready"], ac.due("vecs_ready"))
                u = ac.unit()
                nc.scalar.wait_ge(full[u % BANKS], ac.uses(u))
                act(GR[0:4, 0, :], U(u)[0:4, 0:SEQ], ACT.Tanh, scale=1 / NEG_B1, bias=VEC[0:4, 4:5]).then_inc(sem["scalar_step"], 1)
                nc.scalar.wait_ge(sem["scalar_step"], ac.due("scalar_step"))
                act(GR[0:4, 1, :], U(u)[0:4, SEQ:2 * SEQ], ACT.Tanh, scale=1 / NEG_B1, bias=VEC[0:4, 5:6]).then_inc(free[u % BANKS], 1)
                nc.scalar.wait_ge(free[u % BANKS], ac.uses(u))
                act(GR[0:4, 1, :], GR[0:4, 1, :], ACT.Exp, scale=-NEG_B1).then_inc(sem["scalar_step"], 1)
                nc.scalar.wait_ge(sem["scalar_step"], ac.due("scalar_step"))
                act(GR[0:4, 2, :], GR[0:4, 1, :], ACT.Ln, bias=1.0).then_inc(sem["mg_soft"], 1)
                nc.scalar.wait_ge(sem["mg_soft"], ac.due("mg_soft"))
                for T in (QA, KA):
                    for j in range(2):
                        if j:
                            u = ac.unit()
                            nc.scalar.wait_ge(full[u % BANKS], ac.uses(u))
                            nc.scalar.copy(T[:, 2 * j:2 * j + 2, :].rearrange("p h n -> p (h n)"), U(u)[:, :]).then_inc(free[u % BANKS], 1)
                            nc.scalar.wait_ge(free[u % BANKS], ac.uses(u))
                        else:
                            ac.unit()
                for c in range(2):
                    for t in range(2):
                        if t:
                            u = ac.unit()
                            nc.scalar.wait_ge(full[u % BANKS], ac.uses(u))
                            nc.scalar.copy(VA[:, t, 2 * c:2 * c + 2, 0:256],
                                                           U(u)[:, :].rearrange("p (h n) -> p h n", h=2)).then_inc(free[u % BANKS], 1)
                            nc.scalar.wait_ge(free[u % BANKS], ac.uses(u))
                        else:
                            ac.unit()
                for c in range(2):
                    for t in range(2):
                        u = ac.unit()
                        nc.scalar.wait_ge(full[u % BANKS], ac.uses(u))
                        act(OA[:, t, c * CN:(c + 1) * CN], U(u)[:, :], ACT.Sigmoid).then_inc(free[u % BANKS], 1)
                        nc.scalar.wait_ge(free[u % BANKS], ac.uses(u))
                nc.scalar.wait_ge(sem["mg_rows"], ac.due("mg_rows"))
                act(GR[0:4, 6, :], GR[0:4, 6, :], ACT.Exp, scale=-1.0).then_inc(sem["mg_en"], 1)
                nc.scalar.wait_ge(sem["mg_en"], ac.due("mg_en"))
                u = ac.unit()
                nc.scalar.wait_ge(free[u % BANKS], ac.uses(u))
                for pair in range(2):
                    ac.unit(3)
                    for j in range(2):
                        h = 2 * pair + j
                        nc.scalar.wait_ge(sem["mexp_in"], ac.due("mexp_in"))
                        act(EA[:, h, 0:SEQ], EA[:, h, 0:SEQ], ACT.Exp, bias=GC[:, h:h + 1]).then_inc(sem["scalar_step"], 1)
                        nc.scalar.wait_ge(sem["scalar_step"], ac.due("scalar_step"))
                        act(EA[:, h, SEQ:SEQ + P], EA[:, h, SEQ:SEQ + P], ACT.Exp, bias=GC[:, 4 + h:5 + h]).then_inc(sem["mexp"], 1)
                        nc.scalar.wait_ge(sem["mexp"], ac.due("mexp"))
                    ac.unit(4)
                u = ac.unit()
                nc.scalar.wait_ge(full[u % BANKS], ac.uses(u))
                act(GR[0:8, 0, :], U(u)[0:8, 0:SEQ], ACT.Exp, scale=-1.0).then_inc(sem["bg_exp"], 1)
                nc.scalar.wait_ge(sem["bg_exp"], ac.due("bg_exp"))
                nc.scalar.wait_ge(sem["bg_in"], ac.due("bg_in"))
                act(GR[0:8, 5, :], GR[0:8, 5, :], ACT.Exp, scale=-1.0).then_inc(sem["scalar_step"], 1)
                nc.scalar.wait_ge(sem["scalar_step"], ac.due("scalar_step"))
                act(GR[0:8, 5, :], GR[0:8, 5, :], ACT.Ln, bias=1.0).then_inc(sem["scalar_step"], 1)
                nc.scalar.wait_ge(sem["scalar_step"], ac.due("scalar_step"))
                act(VEC[0:8, 3:4], VEC[0:8, 3:4], ACT.Exp).then_inc(sem["bg_ln"], 1)
                nc.scalar.wait_ge(sem["bg_ln"], ac.due("bg_ln"))
                nc.scalar.wait_ge(sem["bg_cum"], ac.due("bg_cum"))
                act(GR[0:8, 2, P:SEQ], GR[0:8, 4, P:SEQ], ACT.Exp).then_inc(sem["scalar_step"], 1)
                nc.scalar.wait_ge(sem["scalar_step"], ac.due("scalar_step"))
                act(GR[0:8, 3, 0:P], GR[0:8, 4, 0:P], ACT.Exp, scale=-1.0, bias=GR[0:8, 4, P - 1:P]).then_inc(sem["bg_exp"], 1)
                nc.scalar.wait_ge(sem["bg_exp"], ac.due("bg_exp"))
                for i in range(6):
                    T = (QB, KB, VB)[i // 2]
                    for j in range(2):
                        u = ac.unit()
                        nc.scalar.wait_ge(free[u % BANKS], ac.uses(u))
                        acc = SCR2[:, 512 * (j % 2):512 * (j % 2) + 512]
                        h = 4 * (i % 2) + 2 * j
                        o = T[:, h:h + 2, :].rearrange("p h n -> p (h n)")
                        act(o, acc, ACT.Silu).then_inc(sem["conv_done"], 1)
                        nc.scalar.wait_ge(sem["conv_done"], ac.due("conv_done"))
                    if i == 0:
                        nc.scalar.wait_ge(sem["stat"], ac.due("stat"))
                        ac_roots(SS2[:, 0:8], A_DV).then_inc(sem["root"], 1)
                        nc.scalar.wait_ge(sem["root"], ac.due("root"))
                    elif i == 2:
                        take_pairs(ac, HAT, lambda k: COLS2[:, 96 + k:97 + k])
                for j in range(8):
                    T = QB if j < 4 else KB
                    if j >= 2:
                        nc.scalar.wait_ge(sem["sq_used"], ac.due("sq_used"))
                    h = 2 * (j % 4)
                    act(SCR2[:, 1024 + 512 * (j % 2):1536 + 512 * (j % 2)],
                                            T[:, h:h + 2, :].rearrange("p h n -> p (h n)"), ACT.Square).then_inc(sem["sq_ready"], 1)
                    nc.scalar.wait_ge(sem["sq_ready"], ac.due("sq_ready"))
                ac.local["sq_used"] += 2 - 1
                u = ac.unit()
                nc.scalar.wait_ge(full[u % BANKS], ac.uses(u))
                act(R16[0:16, :], U(u)[0:16, 0:SEQ], ACT.Sqrt, bias=EPS).then_inc(free[u % BANKS], 1)
                nc.scalar.wait_ge(free[u % BANKS], ac.uses(u))
                ac.unit(8)
                u = ac.unit()
                nc.scalar.wait_ge(free[u % BANKS], ac.uses(u))
                def delta(b):
                    m = DELTA[b % 2]
                    u_decay = ac.unit()
                    nc.scalar.wait_ge(full[u_decay % BANKS], ac.uses(u_decay))
                    ac.unit(3)
                    nc.scalar.wait_ge(sem["e_in"], ac.due("e_in"))
                    act(m.grown, U(u_decay)[:, :].rearrange("p (h c n) -> p h c n", h=2, c=2)[:, :, 1, :], ACT.Exp).then_inc(free[u_decay % BANKS], 1)
                    nc.scalar.wait_ge(free[u_decay % BANKS], ac.uses(u_decay))
                    for i in range(4):
                        h, c = 2 * b + i // 2, i % 2
                        ins = act(m.decay[:, i, :], m.decay[:, i, :], ACT.Exp, bias=GC[:, 16 + 8 * c + h:17 + 8 * c + h])
                        if i == 3:
                            ins.then_inc(sem["e_exp"], 1)
                            nc.scalar.wait_ge(sem["e_exp"], ac.due("e_exp"))
                        else:
                            ins.then_inc(sem["scalar_step"], 1)
                            nc.scalar.wait_ge(sem["scalar_step"], ac.due("scalar_step"))
                    ac.unit()
                    u = ac.unit()
                    nc.scalar.wait_ge(full[u % BANKS], ac.uses(u))
                    for i in range(4):
                        h, c = 2 * b + i // 2, i % 2
                        ins = act(m.v[:, i, :], U(u)[:, i * P:(i + 1) * P], ACT.Copy, scale=GC[:, 8 * c + h:8 * c + h + 1])
                        if i == 3:
                            ins.then_inc(free[u % BANKS], 1)
                            nc.scalar.wait_ge(free[u % BANKS], ac.uses(u))
                        else:
                            ins.then_inc(sem["scalar_step"], 1)
                            nc.scalar.wait_ge(sem["scalar_step"], ac.due("scalar_step"))
                    yield
                    ac.unit()
                    yield
                    for s in range(1, 7):
                        ac.unit()
                        yield
                        ac.unit(2 if s < 6 else 1)
                        yield
                    u = ac.unit()
                    nc.scalar.wait_ge(full[u % BANKS], ac.uses(u))
                    nc.scalar.copy(m.u, U(u)[:, :].rearrange("p (m n) -> p m n", m=4)).then_inc(free[u % BANKS], 1)
                    nc.scalar.wait_ge(free[u % BANKS], ac.uses(u))
                    u = ac.unit()
                    nc.scalar.wait_ge(full[u % BANKS], ac.uses(u))
                    nc.scalar.copy(m.w_t, U(u)[:, 0:SEQ].rearrange("p (m n) -> p m n", m=2)).then_inc(free[u % BANKS], 1)
                    nc.scalar.wait_ge(free[u % BANKS], ac.uses(u))
                    yield
                    u = ac.unit()
                    nc.scalar.wait_ge(full[u % BANKS], ac.uses(u))
                    nc.scalar.copy(m.state, U(u)[:, 0:SEQ].rearrange("p (m n) -> p m n", m=2)).then_inc(free[u % BANKS], 1)
                    nc.scalar.wait_ge(free[u % BANKS], ac.uses(u))
                    yield
                    ac.unit()
                    yield
                    ac.unit()

                for b in (0, 2):
                    in_turn(delta(b), delta(b + 1))
                nc.scalar.wait_ge(sem["stat"], ac.due("stat"))
                ac_roots(SS2[:, 0:16], P).then_inc(sem["root"], 1)
                nc.scalar.wait_ge(sem["root"], ac.due("root"))

                def gate_units(T, func):
                    for c in range(2):
                        for t in range(2):
                            u = ac.unit()
                            nc.scalar.wait_ge(full[u % BANKS], ac.uses(u))
                            act(T[:, t, c * CN:(c + 1) * CN], U(u)[:, :], func).then_inc(free[u % BANKS], 1)
                            nc.scalar.wait_ge(free[u % BANKS], ac.uses(u))

                gate_units(ZB, ACT.Silu)
                gate_units(SGA, ACT.Sigmoid)
                ac.unit(4)
                gate_units(SGB, ACT.Sigmoid)
                take_pairs(ac, XT2, lambda k: COLS2[:, 104:105])
                ac.unit(4)
                take_pairs(ac, HAT)
                ac.unit(4)
                for t in range(2):
                    nc.scalar.wait_ge(sem["stat"], ac.due("stat"))
                    nc.scalar.activation(SS2[:, 32 + t:33 + t], SS2[:, 32 + t:33 + t], ACT.Sqrt, bias=LN_EPS).then_inc(sem["root"], 1)
                    nc.scalar.wait_ge(sem["root"], ac.due("root"))
                take_pairs(ac, XT2)
                ups = []
                for n in FF_TILES:
                    gs = []
                    for j in range(0, n, 2):
                        u = ac.unit()
                        nc.scalar.wait_ge(full[u % BANKS], ac.uses(u))
                        p = len(ups) + len(gs)
                        if p >= 4:
                            nc.scalar.wait_ge(free[ups[p - 4] % BANKS], ac.uses(ups[p - 4]))
                        gs.append(u)
                        act(SCR2[:, 512 * (p % 4):512 * (p % 4) + 512], U(u)[:, :], ACT.Silu).then_inc(free[u % BANKS], 1)
                        nc.scalar.wait_ge(free[u % BANKS], ac.uses(u))
                    for j in range(0, n, 2):
                        ups.append(ac.unit())
                ac.unit(4)
                for t in range(2):
                    nc.scalar.wait_ge(sem["stat"], ac.due("stat"))
                    nc.scalar.activation(SS2[:, 32 + t:33 + t], SS2[:, 32 + t:33 + t], ACT.Sqrt, bias=LN_EPS).then_inc(sem["root"], 1)
                    nc.scalar.wait_ge(sem["root"], ac.due("root"))

        @block.vector
        def _(eng):
            v = nc.vector
            tt, ts, stt, red = v.tensor_tensor, v.tensor_scalar, v.scalar_tensor_tensor, v.tensor_reduce
            def normed(nt):
                nc.vector.wait_ge(sem["root"], dv.due("root"))
                v.reciprocal(SST[:, 0:nt], SST[:, 0:nt]).then_inc(sem["vector_step"], 1)
                nc.vector.wait_ge(sem["vector_step"], dv.due("vector_step"))
                for t in range(nt):
                    ts(XN[:, t, :], X[:, t, :], SST[:, t:t + 1], None, ALU.mult).then_inc(sem["xn_ready"], 1)
                    nc.vector.wait_ge(sem["xn_ready"], dv.due("xn_ready"))

            def added(l, gate):
                for c in range(2):
                    for t in tiles(l):
                        cols = slice(c * CN, (c + 1) * CN)
                        u = dv.unit()
                        nc.vector.wait_ge(full[u % BANKS], dv.uses(u))
                        tt(SCR[:, 0:CN], U(u)[:, :], gate[:, t // 2, cols], ALU.mult).then_inc(free[u % BANKS], 1)
                        nc.vector.wait_ge(free[u % BANKS], dv.uses(u))
                        add = tt(X[:, t, cols], X[:, t, cols], SCR[:, 0:CN], ALU.add)
                        if c == 1 and t == tiles(l)[-1]:
                            add.then_inc(sem["x_ready"], 1)
                            nc.vector.wait_ge(sem["x_ready"], dv.due("x_ready"))
                        else:
                            add.then_inc(sem["vector_step"], 1)
                            nc.vector.wait_ge(sem["vector_step"], dv.due("vector_step"))

            for l in range(DEPTH):
                lam_init = 0.8 - 0.6 * math.exp(-0.3 * l)
                ns, nt = len(streams(l)), len(tiles(l))
                if l == 0:
                    v.memset(m["silu_c"][:, 16:48], 0.0).then_inc(sem["vector_step"], 1)
                    nc.vector.wait_ge(sem["vector_step"], dv.due("vector_step"))
                u = dv.unit()
                nc.vector.wait_ge(full[u % BANKS], dv.uses(u))
                v.tensor_copy(MOD, bc(U(u)[:, 44:92], 2, [P, 48, 2])).then_inc(sem["vector_step"], 1)
                nc.vector.wait_ge(sem["vector_step"], dv.due("vector_step"))
                v.tensor_copy(COLS, U(u)[:, 0:44]).then_inc(free[u % BANKS], 1)
                nc.vector.wait_ge(free[u % BANKS], dv.uses(u))
                ts(COLS[:, 20:22], COLS[:, 20:22], 1.0 - lam_init, None, ALU.mult).then_inc(sem["vector_step"], 1)
                nc.vector.wait_ge(sem["vector_step"], dv.due("vector_step"))

                def mod_rows(j):
                    u = dv.unit()
                    nc.vector.wait_ge(full[u % BANKS], dv.uses(u))
                    v.tensor_copy(ROWBUF[:, j % 2, :], U(u)[:, :]).then_inc(free[u % BANKS], 1)
                    nc.vector.wait_ge(free[u % BANKS], dv.uses(u))

                def mod_cols(j):
                    u = dv.unit()
                    nc.vector.wait_ge(full[u % BANKS], dv.uses(u))
                    cols = MOD[:, 4 * j:4 * j + 4, :].rearrange("p j s -> p (j s)")
                    tt(cols, cols, U(u)[:, 0:8], ALU.add).then_inc(free[u % BANKS], 1)
                    nc.vector.wait_ge(free[u % BANKS], dv.uses(u))

                def gain(i):
                    g = COLS[:, 8 * i:8 * i + 8]
                    stt(GAIN[i], MOD[:, 24 * i + 8:24 * i + 16, :], 1.0, bc(g, 2, [P, KT, 2]), ALU.add, ALU.mult).then_inc(sem["vector_step"], 1)
                    nc.vector.wait_ge(sem["vector_step"], dv.due("vector_step"))

                mod_rows(0)
                mod_rows(1)
                mod_cols(0)
                if l == 0:
                    nc.vector.wait_ge(sem["tokens_in"], dv.due("tokens_in", 32))
                normed(4)
                for j in range(1, 4):
                    if j < 3:
                        mod_rows(j + 1)
                    mod_cols(j)
                gain(0)
                u = dv.unit()
                nc.vector.wait_ge(full[u % BANKS], dv.uses(u))
                v.tensor_copy(m["sgu_t"], U(u)[:, :]).then_inc(free[u % BANKS], 1)
                nc.vector.wait_ge(free[u % BANKS], dv.uses(u))
                lr = m["lam_rows"].rearrange("p (a b c) -> p a b c", a=2, b=2)
                nc.vector.wait_ge(sem["smalls"], dv.due("smalls", 16 * (7 + (l > 0))))
                tt(SCR[:, 1400:1464].rearrange("p (a c) -> p a c", a=2), lr[:, :, 0, :], lr[:, :, 1, :], ALU.mult).then_inc(sem["vector_step"], 1)
                nc.vector.wait_ge(sem["vector_step"], dv.due("vector_step"))
                red(m["lam"][:, 0:2], SCR[:, 1400:1464].rearrange("p (a c) -> p a c", a=2), AXX, ALU.add).then_inc(sem["lam_dot"], 1)
                nc.vector.wait_ge(sem["lam_dot"], dv.due("lam_dot"))
                ht = []
                for k in range(KT):
                    ht.append(dv.unit() if k % 2 else modulated(dv, k, 4, 4, GAIN[0], SHIFT[0]))
                def squares(todo):
                    for t, at, n, g, o in todo:
                        src = PROJ[:, t, at:at + n]
                        tt(SCR[:, 0:n], src, src, ALU.mult).then_inc(sem["vector_step"], 1)
                        nc.vector.wait_ge(sem["vector_step"], dv.due("vector_step"))
                        ins = red(SS28[:, t, o:o + g], SCR[:, 0:n].rearrange("p (g w) -> p g w", g=g), AXX, ALU.add)
                        if (t, at) == todo[-1][:2]:
                            ins.then_inc(sem["stat"], 1)
                            nc.vector.wait_ge(sem["stat"], dv.due("stat"))
                        else:
                            ins.then_inc(sem["vector_step"], 1)
                            nc.vector.wait_ge(sem["vector_step"], dv.due("vector_step"))

                def normed_heads(t, at, g, w, o, go):
                    x = PROJ[:, t, at:at + 512].rearrange("p (g w) -> p g w", g=g)
                    tt(x, x, bc(SS28[:, t, o:o + g], 2, [P, g, w]), ALU.mult).then_inc(sem["vector_step"], 1)
                    nc.vector.wait_ge(sem["vector_step"], dv.due("vector_step"))
                    x4 = PROJ[:, t, at:at + 512].rearrange("p (j g w) -> p j g w", j=2, w=w)
                    gains = m["gains_qk"][:, go:go + 2 * w].rearrange("p (j w) -> p j w", j=2)
                    return tt(x4, x4, bc(gains, 2, [P, 2, g // 2, w]), ALU.mult)

                def rotated(t):
                    x = PROJ[:, t, C_Q:C_Q + 512].rearrange("p (g w) -> p g w", g=16)
                    xr = PROJ[:, t, C_Q:C_Q + 512].rearrange("p (g r h e) -> p g r h e", g=16, r=2, h=2)
                    sr = SCR[:, 0:512].rearrange("p (g r h e) -> p g r h e", g=16, r=2, h=2)
                    sin = ROPE[:, t, 32:64].rearrange("p (r h e) -> p r h e", r=2, h=2)
                    for h in range(2):
                        tt(sr[:, :, :, h, :], xr[:, :, :, 1 - h, :],
                                   bc(sin[:, :, h, :], 1, [P, 16, 2, 8]), ALU.mult).then_inc(sem["vector_step"], 1)
                        nc.vector.wait_ge(sem["vector_step"], dv.due("vector_step"))
                    tt(x, x, bc(ROPE[:, t, 0:32], 1, [P, 16, 32]), ALU.mult).then_inc(sem["vector_step"], 1)
                    nc.vector.wait_ge(sem["vector_step"], dv.due("vector_step"))
                    tt(PROJ[:, t, C_Q:C_Q + 512], PROJ[:, t, C_Q:C_Q + 512], SCR[:, 0:512], ALU.add).then_inc(sem["vector_step"], 1)
                    nc.vector.wait_ge(sem["vector_step"], dv.due("vector_step"))

                proj = []
                for c, (at, n) in enumerate(PROJ_CHUNKS):
                    units = []
                    for t in proj_tiles(l, c):
                        if c == 0 or t % 2:
                            units.append(dv.unit())
                        else:
                            u = dv.unit()
                            nc.vector.wait_ge(full[u % BANKS], dv.uses(u))
                            v.tensor_copy(PROJ[:, t, at:at + n], U(u)[:, 0:n]).then_inc(free[u % BANKS], 1)
                            nc.vector.wait_ge(free[u % BANKS], dv.uses(u))
                    proj += units
                    if c == 2:
                        for n_out in proj:
                            nc.vector.wait_ge(free[n_out % BANKS], dv.uses(n_out))
                        squares([(t, A_V, 256, 4, 0) for t in tiles(l)] + [(t, C_Q, 512, 16, 4) for t in range(4)])
                    elif c == 3:
                        nc.vector.wait_ge(sem["root"], dv.due("root"))
                        v.reciprocal(SS28[:, 0:nt, 0:4], SS28[:, 0:nt, 0:4]).then_inc(sem["vector_step"], 1)
                        nc.vector.wait_ge(sem["vector_step"], dv.due("vector_step"))
                        v.reciprocal(SS28[:, :, 4:20], SS28[:, :, 4:20]).then_inc(sem["vector_step"], 1)
                        nc.vector.wait_ge(sem["vector_step"], dv.due("vector_step"))
                        for n_out in units:
                            nc.vector.wait_ge(free[n_out % BANKS], dv.uses(n_out))
                        squares([(t, D_Q, 512, 8, 20) for t in range(4)])
                    elif c == 4:
                        if l == 0:
                            nc.vector.wait_ge(sem["consts"], dv.due("consts", 16 * 6))
                        for t in range(4):
                            normed_heads(t, C_Q, 16, DIFF_D, 4, 0).then_inc(sem["vector_step"], 1)
                            nc.vector.wait_ge(sem["vector_step"], dv.due("vector_step"))
                            if t < 2:
                                rotated(t)
                for n_out in proj:
                    nc.vector.wait_ge(free[n_out % BANKS], dv.uses(n_out))
                nc.vector.wait_ge(sem["lam_exp"], dv.due("lam_exp"))
                tt(m["lam"][:, 2:3], m["lam"][:, 0:1], m["lam"][:, 1:2], ALU.subtract).then_inc(sem["vector_step"], 1)
                nc.vector.wait_ge(sem["vector_step"], dv.due("vector_step"))
                ts(m["lam"][:, 2:3], m["lam"][:, 2:3], lam_init, None, ALU.add).then_inc(sem["vector_step"], 1)
                nc.vector.wait_ge(sem["vector_step"], dv.due("vector_step"))
                nc.vector.wait_ge(sem["bias_in"], dv.due("bias_in", 256))
                bias = m["gate"].rearrange("p (a k) -> p a k", a=8)
                stt(bias, bias, float(HD ** 0.5), bc(m["window"], 1, [P, 8, SEQ]), ALU.mult, ALU.add).then_inc(sem["vector_step"], 1)
                nc.vector.wait_ge(sem["vector_step"], dv.due("vector_step"))
                u_four = dv.unit(2 * ns)
                four = [dv.unit() for t in tiles(l)]
                for t in tiles(l):
                    x = PROJ[:, t, A_V:A_V + 256].rearrange("p (g w) -> p g w", g=4)
                    tt(x, x, bc(SS28[:, t, 0:4], 2, [P, 4, HD]), ALU.mult).then_inc(sem["vn_ready"], 1)
                    nc.vector.wait_ge(sem["vn_ready"], dv.due("vn_ready"))
                nc.vector.wait_ge(sem["root"], dv.due("root"))
                v.reciprocal(SS28[:, :, 20:28], SS28[:, :, 20:28]).then_inc(sem["vector_step"], 1)
                nc.vector.wait_ge(sem["vector_step"], dv.due("vector_step"))
                for t in range(4):
                    normed_heads(t, D_Q, 8, HD, 20, 64).then_inc(sem["qk_ready"], 1)
                    nc.vector.wait_ge(sem["qk_ready"], dv.due("qk_ready"))
                for t in tiles(l):
                    u = dv.unit()
                    nc.vector.wait_ge(full[u % BANKS], dv.uses(u))
                    sv = SCR[:, 0:256].rearrange("p (h w) -> p h w", h=4)
                    tt(sv, U(u)[:, 0:256].rearrange("p (h w) -> p h w", h=4),
                                       bc(COLS[:, 24:28], 2, [P, 4, HD]), ALU.add).then_inc(free[u % BANKS], 1)
                    nc.vector.wait_ge(free[u % BANKS], dv.uses(u))
                    tt(PROJ[:, t, 0:256], PROJ[:, t, 0:256], SCR[:, 0:256], ALU.mult).then_inc(sem["vector_step"], 1)
                    nc.vector.wait_ge(sem["vector_step"], dv.due("vector_step"))
                dv.unit(8)
                todo = jobs(l)
                n = len(todo)
                score_of = {}

                def maxima(i):
                    kind, t, h = todo[i]
                    nk = 512 if t < 2 else SEQ
                    scale = (DIFF_D if kind == "C" else HD) ** -0.5
                    for q in range(2 if kind == "C" else 1):
                        u = dv.unit()
                        nc.vector.wait_ge(full[u % BANKS], dv.uses(u))
                        score_of[i, q] = u
                        if kind == "D" and t < 2:
                            tt(U(u)[:, 0:SEQ], U(u)[:, 0:SEQ], BIAS[:, t, h, :], ALU.add).then_inc(sem["vector_step"], 1)
                            nc.vector.wait_ge(sem["vector_step"], dv.due("vector_step"))
                        col = 2 * (i % 2) + q
                        red(SMALL[:, 8 + col:9 + col], U(u)[:, 0:nk], AXX, ALU.max).then_inc(sem["vector_step"], 1)
                        nc.vector.wait_ge(sem["vector_step"], dv.due("vector_step"))
                        ts(SMALL[:, col:col + 1], SMALL[:, 8 + col:9 + col], -scale, None, ALU.mult).then_inc(sem["row_max"], 1)
                        nc.vector.wait_ge(sem["row_max"], dv.due("row_max"))

                def weights(i):
                    kind, t, h = todo[i]
                    nk = 512 if t < 2 else SEQ
                    r = SMALL[:, 12 + 2 * (i % 3):14 + 2 * (i % 3)]
                    s = SMALL[:, 4 + 2 * (i % 2):6 + 2 * (i % 2)]
                    if kind == "D":
                        nc.vector.wait_ge(free[score_of[i, 0] % BANKS], dv.uses(score_of[i, 0]))
                        v.reciprocal(r[:, 0:1], s[:, 0:1]).then_inc(sem["vector_step"], 1)
                        nc.vector.wait_ge(sem["vector_step"], dv.due("vector_step"))
                        return
                    for n_out in (score_of[i, 0], score_of[i, 1]):
                        nc.vector.wait_ge(free[n_out % BANKS], dv.uses(n_out))
                    v.reciprocal(r, s).then_inc(sem["vector_step"], 1)
                    nc.vector.wait_ge(sem["vector_step"], dv.due("vector_step"))
                    tt(r[:, 1:2], r[:, 1:2], m["lam"][:, 2:3], ALU.mult).then_inc(sem["vector_step"], 1)
                    nc.vector.wait_ge(sem["vector_step"], dv.due("vector_step"))
                    e = EXPS[:, i % 2, :, 0:nk]
                    ts(e[:, 1, :], e[:, 1, :], r[:, 1:2], None, ALU.mult).then_inc(sem["vector_step"], 1)
                    nc.vector.wait_ge(sem["vector_step"], dv.due("vector_step"))
                    stt(W[:, i % 2, 0:nk], e[:, 0, :], r[:, 0:1], e[:, 1, :], ALU.mult, ALU.subtract).then_inc(sem["w_diff"], 1)
                    nc.vector.wait_ge(sem["w_diff"], dv.due("w_diff"))

                def values(i):
                    kind, t, h = todo[i]
                    r = SMALL[:, 12 + 2 * (i % 3):13 + 2 * (i % 3)]
                    u = dv.unit()
                    nc.vector.wait_ge(full[u % BANKS], dv.uses(u))
                    at = (C_Q if kind == "C" else D_Q) + h * HD
                    o = PROJ[:, t, at:at + HD]
                    (v.tensor_copy(o, U(u)[:, 0:HD]) if kind == "C" else
                                 ts(o, U(u)[:, 0:HD], r, None, ALU.mult)).then_inc(free[u % BANKS], 1)
                    nc.vector.wait_ge(free[u % BANKS], dv.uses(u))

                segs = ((0, 0, 256), (B_Z, 256, 512), (D_Q, 768, 256))

                def head_squares(t, free_at):
                    room = SCR[:, free_at:free_at + 512]
                    for o, pieces in ((0, ((0, 256), (B_Z, 256))), (8, ((C_Q, 256), (D_Q, 256)))):
                        for i, (at, w) in enumerate(pieces):
                            src = PROJ[:, t, at:at + w]
                            tt(room[:, 256 * i:256 * i + 256], src, src, ALU.mult).then_inc(sem["vector_step"], 1)
                            nc.vector.wait_ge(sem["vector_step"], dv.due("vector_step"))
                        ins = red(SS[:, 16 * t + o:16 * t + o + 8], room.rearrange("p (g w) -> p g w", g=8),
                                  AXX, ALU.add)
                        if (t, o) == (nt - 1, 8):
                            ins.then_inc(sem["stat"], 1)
                            nc.vector.wait_ge(sem["stat"], dv.due("stat"))
                        else:
                            ins.then_inc(sem["vector_step"], 1)
                            nc.vector.wait_ge(sem["vector_step"], dv.due("vector_step"))

                for n_out in four:
                    nc.vector.wait_ge(free[n_out % BANKS], dv.uses(n_out))
                maxima(0)
                maxima(1)
                for i in range(n):
                    weights(i)
                    if i + 2 < n:
                        maxima(i + 2)
                    dv.unit()
                    if i:
                        values(i - 1)
                    if i and i % 8 == 0:
                        head_squares(i // 8 - 1, 1024)
                    if i % (n // 8) == 0:
                        j = 4 + i // (n // 8)
                        mod_rows(j)
                        if j > 4:
                            mod_cols(j - 1)
                values(n - 1)
                mod_cols(11)
                v.memset(SMALL[:, 90:91], 0.0).then_inc(sem["mod_ready"], 1)
                nc.vector.wait_ge(sem["mod_ready"], dv.due("mod_ready"))
                u = dv.unit()
                nc.vector.wait_ge(full[u % BANKS], dv.uses(u))
                v.tensor_copy(GATE_ROWS, U(u)[0:8, :]).then_inc(free[u % BANKS], 1)
                nc.vector.wait_ge(free[u % BANKS], dv.uses(u))
                v.memset(SMALL[:, 90:91], 0.0).then_inc(sem["row_ready"], 1)
                nc.vector.wait_ge(sem["row_ready"], dv.due("row_ready"))
                gain(1)
                v.memset(SMALL[:, 90:91], 0.0).then_inc(sem["bias_used"], 1)
                nc.vector.wait_ge(sem["bias_used"], dv.due("bias_used"))
                head_squares(nt - 1, 0)
                nc.vector.wait_ge(sem["root"], dv.due("root"))
                v.reciprocal(SS[:, 0:16 * nt], SS[:, 0:16 * nt]).then_inc(sem["vector_step"], 1)
                nc.vector.wait_ge(sem["vector_step"], dv.due("vector_step"))
                for t in tiles(l):
                    for at, o, w in segs:
                        g = w // HD
                        r = SS[:, 16 * t + o // HD:16 * t + o // HD + g]
                        ins = tt(XN[:, t, o:o + w].rearrange("p (g w) -> p g w", g=g),
                                 PROJ[:, t, at:at + w].rearrange("p (g w) -> p g w", g=g), bc(r, 2, [P, g, HD]), ALU.mult)
                        if at == D_Q:
                            ins.then_inc(sem["xn_ready"], 1)
                            nc.vector.wait_ge(sem["xn_ready"], dv.due("xn_ready"))
                        else:
                            ins.then_inc(sem["vector_step"], 1)
                            nc.vector.wait_ge(sem["vector_step"], dv.due("vector_step"))
                for k in range(KT):
                    if k % 2:
                        dv.unit()
                    else:
                        u = dv.unit()
                        nc.vector.wait_ge(full[u % BANKS], dv.uses(u))
                        ts(HT[:, k, 0:nt * P], U(u)[:, 0:nt * P], COLS[:, 16 + k:17 + k], None, ALU.mult).then_inc(free[u % BANKS], 1)
                        nc.vector.wait_ge(free[u % BANKS], dv.uses(u))
                nc.vector.wait_ge(sem["gate1_in"], dv.due("gate1_in", 16 * ns))
                added(l, GATE1)
                normed(nt)
                for k in range(KT):
                    if k % 2:
                        dv.unit()
                    else:
                        modulated(dv, k, 4, nt, GAIN[1], SHIFT[1])
                u = dv.unit()
                nc.vector.wait_ge(full[u % BANKS], dv.uses(u))
                v.tensor_copy(AFFT[0:N_EXP, 0:nt * P], U(u)[0:N_EXP, 0:nt * P]).then_inc(free[u % BANKS], 1)
                nc.vector.wait_ge(free[u % BANKS], dv.uses(u))
                u = dv.unit()
                nc.vector.wait_ge(full[u % BANKS], dv.uses(u))
                lg = U(u)[:, 0:nt * N_EXP].rearrange("p (t e) -> p t e", t=nt)
                aff = AFF[:, 0:nt, :]
                mx = SMALL[:, 0:nt]
                red(mx, lg, AXX, ALU.max).then_inc(sem["vector_step"], 1)
                nc.vector.wait_ge(sem["vector_step"], dv.due("vector_step"))
                tt(aff, lg, bc(mx, 2, [P, nt, N_EXP]), ALU.subtract).then_inc(free[u % BANKS], 1)
                nc.vector.wait_ge(free[u % BANKS], dv.uses(u))
                v.memset(SMALL[:, 90:91], 0.0).then_inc(sem["logit"], 1)
                nc.vector.wait_ge(sem["logit"], dv.due("logit"))
                nc.vector.wait_ge(sem["logit_exp"], dv.due("logit_exp"))
                red(mx, aff, AXX, ALU.add).then_inc(sem["vector_step"], 1)
                nc.vector.wait_ge(sem["vector_step"], dv.due("vector_step"))
                v.reciprocal(mx, mx).then_inc(sem["vector_step"], 1)
                nc.vector.wait_ge(sem["vector_step"], dv.due("vector_step"))
                tt(aff, aff, bc(mx, 2, [P, nt, N_EXP]), ALU.mult).then_inc(sem["aff_ready"], 1)
                nc.vector.wait_ge(sem["aff_ready"], dv.due("aff_ready"))
                u = dv.unit()
                nc.vector.wait_ge(full[u % BANKS], dv.uses(u))
                n = nt * P
                v.tensor_copy(AFFT[0:N_EXP, 0:n], U(u)[0:N_EXP, 0:n]).then_inc(sem["vector_step"], 1)
                nc.vector.wait_ge(sem["vector_step"], dv.due("vector_step"))
                v.tensor_copy(WORK[0:N_EXP, 0:n], U(u)[0:N_EXP, 0:n]).then_inc(free[u % BANKS], 1)
                nc.vector.wait_ge(free[u % BANKS], dv.uses(u))
                for s in streams(l):
                    wk = WORK[0:N_EXP, s * SEQ:(s + 1) * SEQ]
                    top = SMALL[0:N_EXP, 16:24]
                    for i in range(CAP // 8):
                        v.max(top, wk).then_inc(sem["vector_step"], 1)
                        nc.vector.wait_ge(sem["vector_step"], dv.due("vector_step"))
                        v.match_replace(wk, top, wk, -1.0).then_inc(sem["vector_step"], 1)
                        nc.vector.wait_ge(sem["vector_step"], dv.due("vector_step"))
                wk = WORK[0:N_EXP, 0:n]
                tt(wk, wk, AFFT[0:N_EXP, 0:n], ALU.not_equal).then_inc(sem["vector_step"], 1)
                nc.vector.wait_ge(sem["vector_step"], dv.due("vector_step"))
                for s in streams(l):
                    cols = slice(s * SEQ, (s + 1) * SEQ)
                    v.tensor_tensor_scan(RANK[0:N_EXP, cols], ones[0:N_EXP, 0:1].broadcast_to([N_EXP, SEQ]),
                                                 WORK[0:N_EXP, cols], 0.0, ALU.mult, ALU.add).then_inc(sem["vector_step"], 1)
                    nc.vector.wait_ge(sem["vector_step"], dv.due("vector_step"))
                tt(RANK[0:N_EXP, 0:n], RANK[0:N_EXP, 0:n], wk, ALU.mult).then_inc(sem["rank_ready"], 1)
                nc.vector.wait_ge(sem["rank_ready"], dv.due("rank_ready"))
                u = dv.unit()
                nc.vector.wait_ge(full[u % BANKS], dv.uses(u))
                v.tensor_copy(POS[:, 0:nt, :], U(u)[:, 0:nt * N_EXP].rearrange("p (t e) -> p t e", t=nt)).then_inc(free[u % BANKS], 1)
                nc.vector.wait_ge(free[u % BANKS], dv.uses(u))
                for t in tiles(l):
                    tt(SEL[:, t, :, :], bc(m["slots"], 1, [P, N_EXP, CAP]),
                                            bc(POS[:, t, :], 2, [P, N_EXP, CAP]), ALU.is_equal).then_inc(sem["sel_ready"], 1)
                    nc.vector.wait_ge(sem["sel_ready"], dv.due("sel_ready"))
                gat = []
                for k in range(KT):
                    for s in streams(l):
                        gat.append(dv.unit() if k % 2 else gathered(dv, k, s))
                for n_out in gat:
                    nc.vector.wait_ge(free[n_out % BANKS], dv.uses(n_out))
                v.memset(SMALL[:, 90:91], 0.0).then_inc(sem["xg_ready"], 1)
                nc.vector.wait_ge(sem["xg_ready"], dv.due("xg_ready"))
                for t in tiles(l):
                    tt(SEL[:, t, :, :], SEL[:, t, :, :], bc(AFF[:, t, :], 2, [P, N_EXP, CAP]), ALU.mult).then_inc(sem["selg_ready"], 1)
                    nc.vector.wait_ge(sem["selg_ready"], dv.due("selg_ready"))
                selt = [dv.unit() for t in tiles(l)]
                for n_out in selt:
                    nc.vector.wait_ge(free[n_out % BANKS], dv.uses(n_out))
                M = 32 * ns
                with dv.loop(4, expert_turn(ns)) as g:
                    for e in range(4):
                        for c in range(2):
                            dv.unit()
                            u = dv.unit()
                            nc.vector.wait_ge(full[u % BANKS], dv.uses(u))
                            v.tensor_copy(UP_PARTS[0:2 * M, c, :], U(u)[0:2 * M, :]).then_inc(free[u % BANKS], 1)
                            nc.vector.wait_ge(free[u % BANKS], dv.uses(u))
                        for c in range(2):
                            u = dv.unit()
                            nc.vector.wait_ge(full[u % BANKS], dv.uses(u))
                            nc.vector.wait_ge(sem["hid_silu"], dv.due("hid_silu"))
                            h = HIDT[:, 4 * c:4 * c + 4, 0:M]
                            tt(h, h, U(u)[:, 4 * M:8 * M].rearrange("p (k c) -> p k c", k=4), ALU.mult).then_inc(free[u % BANKS], 1)
                            nc.vector.wait_ge(free[u % BANKS], dv.uses(u))
                        for c in range(2):
                            u = dv.unit()
                            nc.vector.wait_ge(full[u % BANKS], dv.uses(u))
                            nc.vector.wait_ge(sem["down_part"], dv.due("down_part"))
                            for s in streams(l):
                                o = [m["ht"], m["xn"]][s][32 * e:32 * e + 32, bass.ds(g * D + c * CN, CN)]
                                ins = tt(o, U(u)[32 * s:32 * s + 32, :], DOWN_PART[32 * s:32 * s + 32, :], ALU.add)
                                if s == ns - 1:
                                    ins.then_inc(free[u % BANKS], 1)
                                    nc.vector.wait_ge(free[u % BANKS], dv.uses(u))
                                else:
                                    ins.then_inc(sem["vector_step"], 1)
                                    nc.vector.wait_ge(sem["vector_step"], dv.due("vector_step"))
                v.memset(SMALL[:, 90:91], 0.0).then_inc(sem["moe_done"], 1)
                nc.vector.wait_ge(sem["moe_done"], dv.due("moe_done"))
                nc.vector.wait_ge(sem["gate2_in"], dv.due("gate2_in", 16 * ns))
                added(l, GATE2[2 - ns])

            def bn_place(t, c):
                at = (40, 0)[t] + 6 * c
                return SS2[:, at:at + 6]

            def layer_norm(first, t):
                v.bn_stats(bn_place(t, 1), X2[:, t, CN:2 * CN]).then_inc(sem["vector_step"], 1)
                nc.vector.wait_ge(sem["vector_step"], dv.due("vector_step"))
                v.bn_aggr(SS2[:, 34 + 2 * t:36 + 2 * t], SS2[:, (40, 0)[t]:(52, 12)[t]]).then_inc(sem["vector_step"], 1)
                nc.vector.wait_ge(sem["vector_step"], dv.due("vector_step"))
                v.tensor_copy(SS2[:, 32 + t:33 + t], SS2[:, 35 + 2 * t:36 + 2 * t]).then_inc(sem["stat"], 1)
                nc.vector.wait_ge(sem["stat"], dv.due("stat"))
                nc.vector.wait_ge(sem["root"], dv.due("root"))
                v.reciprocal(SS2[:, 32 + t:33 + t], SS2[:, 32 + t:33 + t]).then_inc(sem["vector_step"], 1)
                nc.vector.wait_ge(sem["vector_step"], dv.due("vector_step"))
                ts(X2[:, t, :], X2[:, t, :], SS2[:, 34 + 2 * t:35 + 2 * t], SS2[:, 32 + t:33 + t],
                           ALU.subtract, ALU.mult).then_inc(sem["vector_step"], 1)
                nc.vector.wait_ge(sem["vector_step"], dv.due("vector_step"))
                tt(X2[:, t, :], X2[:, t, :], LNG[:, 0 if first else 2, :], ALU.mult).then_inc(sem["vector_step"], 1)
                nc.vector.wait_ge(sem["vector_step"], dv.due("vector_step"))
                ins = tt(X2[:, t, :], X2[:, t, :], LNG[:, 1 if first else 3, :], ALU.add)
                if first:
                    ins.then_inc(sem["ln_ready"], 1)
                    nc.vector.wait_ge(sem["ln_ready"], dv.due("ln_ready"))
                elif t:
                    ins.then_inc(sem["x_ready"], 1)
                    nc.vector.wait_ge(sem["x_ready"], dv.due("x_ready"))
                else:
                    ins.then_inc(sem["vector_step"], 1)
                    nc.vector.wait_ge(sem["vector_step"], dv.due("vector_step"))

            def residual_norm(first):
                for c in range(2):
                    for t in range(2):
                        u = dv.unit()
                        nc.vector.wait_ge(full[u % BANKS], dv.uses(u))
                        residual(u, t, c)
                        if c == 0:
                            v.bn_stats(bn_place(t, 0), X2[:, t, 0:CN]).then_inc(sem["vector_step"], 1)
                            nc.vector.wait_ge(sem["vector_step"], dv.due("vector_step"))
                            continue
                        if first and t == 0:
                            nc.vector.wait_ge(sem["ln_gains"], dv.due("ln_gains", 64))
                        layer_norm(first, t)

            def residual(u, t, c):
                cols = slice(c * CN, (c + 1) * CN)
                stt(X2[:, t, cols], X2[:, t, cols], ALPHA, U(u)[:, :], ALU.mult, ALU.add).then_inc(free[u % BANKS], 1)
                nc.vector.wait_ge(free[u % BANKS], dv.uses(u))

            for l in range(DEPTH):
                nc.vector.wait_ge(sem["smalls2"], dv.due("smalls2", 16 * (13 if l == 0 else 9)))
                u = dv.unit()
                nc.vector.wait_ge(full[u % BANKS], dv.uses(u))
                v.tensor_copy(COLS2[:, 0:105], U(u)[:, 0:105]).then_inc(free[u % BANKS], 1)
                nc.vector.wait_ge(free[u % BANKS], dv.uses(u))
                v.memset(VA[:, :, :, 256:257], 1.0).then_inc(sem["vector_step"], 1)
                nc.vector.wait_ge(sem["vector_step"], dv.due("vector_step"))
                ts(VEC[0:4, 4:6], VEC[0:4, 0:2], 1 / NEG_B1, None, ALU.mult).then_inc(sem["vecs_ready"], 1)
                nc.vector.wait_ge(sem["vecs_ready"], dv.due("vecs_ready"))
                take_pairs(dv, XT2)
                dv.unit()
                nc.vector.wait_ge(sem["mg_soft"], dv.due("mg_soft"))
                one = ones[:, 0:1]
                v.tensor_tensor_scan(GR[0:4, 3, :], one[0:4].broadcast_to([4, SEQ]), GR[0:4, 2, :], 0.0,
                                             ALU.mult, ALU.subtract).then_inc(sem["vector_step"], 1)
                nc.vector.wait_ge(sem["vector_step"], dv.due("vector_step"))
                stt(GR[0:4, 4, :], GR[0:4, 0, :], NEG_B1, GR[0:4, 3, :], ALU.mult, ALU.subtract).then_inc(sem["vector_step"], 1)
                nc.vector.wait_ge(sem["vector_step"], dv.due("vector_step"))
                v.tensor_tensor_scan(GR[0:4, 5, :], one[0:4].broadcast_to([4, SEQ]), GR[0:4, 4, :], 0.0,
                                             ALU.mult, ALU.max).then_inc(sem["vector_step"], 1)
                nc.vector.wait_ge(sem["vector_step"], dv.due("vector_step"))
                tt(GR[0:4, 6, :], GR[0:4, 3, :], GR[0:4, 5, :], ALU.add).then_inc(sem["vector_step"], 1)
                nc.vector.wait_ge(sem["vector_step"], dv.due("vector_step"))
                ts(GR[0:4, 6, :], GR[0:4, 6, :], -80.0, None, ALU.max).then_inc(sem["vector_step"], 1)
                nc.vector.wait_ge(sem["vector_step"], dv.due("vector_step"))
                ts(GR[0:4, 5, :], GR[0:4, 5, :], -1.0, None, ALU.mult).then_inc(sem["mg_rows"], 1)
                nc.vector.wait_ge(sem["mg_rows"], dv.due("mg_rows"))
                for T in (QA, KA):
                    for j in range(2):
                        if j:
                            dv.unit()
                        else:
                            u = dv.unit()
                            nc.vector.wait_ge(full[u % BANKS], dv.uses(u))
                            v.tensor_copy(T[:, 0:2, :].rearrange("p h n -> p (h n)"), U(u)[:, :]).then_inc(free[u % BANKS], 1)
                            nc.vector.wait_ge(free[u % BANKS], dv.uses(u))
                for c in range(2):
                    for t in range(2):
                        if t:
                            dv.unit()
                        else:
                            u = dv.unit()
                            nc.vector.wait_ge(full[u % BANKS], dv.uses(u))
                            v.tensor_copy(VA[:, 0, 2 * c:2 * c + 2, 0:256],
                                                          U(u)[:, :].rearrange("p (h n) -> p h n", h=2)).then_inc(free[u % BANKS], 1)
                            nc.vector.wait_ge(free[u % BANKS], dv.uses(u))
                oa = [dv.unit() for i in range(4)]
                u = dv.unit()
                nc.vector.wait_ge(full[u % BANKS], dv.uses(u))
                v.tensor_copy(GC[:, 0:16], U(u)[:, 0:16]).then_inc(free[u % BANKS], 1)
                nc.vector.wait_ge(free[u % BANKS], dv.uses(u))
                for pair in range(2):
                    u = dv.unit()
                    nc.vector.wait_ge(full[u % BANKS], dv.uses(u))
                    for j in range(2):
                        h = 2 * pair + j
                        b = U(u)[:, j * SEQ:(j + 1) * SEQ]
                        tt(EA[:, h, 0:SEQ], b, CAUSAL, ALU.add).then_inc(sem["vector_step"], 1)
                        nc.vector.wait_ge(sem["vector_step"], dv.due("vector_step"))
                        ins = tt(EA[:, h, SEQ:SEQ + P], b[:, P:SEQ], CAUSAL[:, 0:P], ALU.add)
                        if j == 0:
                            ins.then_inc(sem["vector_step"], 1)
                            nc.vector.wait_ge(sem["vector_step"], dv.due("vector_step"))
                        else:
                            ins.then_inc(free[u % BANKS], 1)
                            nc.vector.wait_ge(free[u % BANKS], dv.uses(u))
                        v.memset(SS2[:, 63:64], 0.0).then_inc(sem["mexp_in"], 1)
                        nc.vector.wait_ge(sem["mexp_in"], dv.due("mexp_in"))
                    for j in range(2):
                        h = 2 * pair + j
                        nc.vector.wait_ge(sem["mexp"], dv.due("mexp"))
                        u = dv.unit()
                        nc.vector.wait_ge(full[u % BANKS], dv.uses(u))
                        stt(PA[:, h, :], U(u)[:, 0:384], SCALE_A, EA[:, h, :], ALU.mult, ALU.mult).then_inc(free[u % BANKS], 1)
                        nc.vector.wait_ge(free[u % BANKS], dv.uses(u))
                    for j in range(2):
                        h = 2 * pair + j
                        for t in range(2):
                            u = dv.unit()
                            nc.vector.wait_ge(full[u % BANKS], dv.uses(u))
                            den = SS2[:, 60:61]
                            v.tensor_copy(den, U(u)[:, 256:257]).then_inc(sem["vector_step"], 1)
                            nc.vector.wait_ge(sem["vector_step"], dv.due("vector_step"))
                            stt(SS2[:, 61:62], den, -1.0, den, ALU.mult, ALU.max).then_inc(sem["vector_step"], 1)
                            nc.vector.wait_ge(sem["vector_step"], dv.due("vector_step"))
                            tt(SS2[:, 61:62], SS2[:, 61:62], GC[:, 8 + 4 * t + h:9 + 4 * t + h], ALU.max).then_inc(sem["vector_step"], 1)
                            nc.vector.wait_ge(sem["vector_step"], dv.due("vector_step"))
                            v.reciprocal(SS2[:, 61:62], SS2[:, 61:62]).then_inc(sem["vector_step"], 1)
                            nc.vector.wait_ge(sem["vector_step"], dv.due("vector_step"))
                            ts(HA[:, t, h * 256:(h + 1) * 256], U(u)[:, 0:256], SS2[:, 61:62], None, ALU.mult).then_inc(free[u % BANKS], 1)
                            nc.vector.wait_ge(free[u % BANKS], dv.uses(u))
                nc.vector.wait_ge(sem["bg_exp"], dv.due("bg_exp"))
                u = dv.unit()
                nc.vector.wait_ge(full[u % BANKS], dv.uses(u))
                ts(GR[0:8, 0, :], GR[0:8, 0, :], 1.0, None, ALU.add).then_inc(sem["vector_step"], 1)
                nc.vector.wait_ge(sem["vector_step"], dv.due("vector_step"))
                v.reciprocal(GR[0:8, 0, :], GR[0:8, 0, :]).then_inc(sem["vector_step"], 1)
                nc.vector.wait_ge(sem["vector_step"], dv.due("vector_step"))
                ts(GR[0:8, 4, :], U(u)[0:8, SEQ:2 * SEQ], VEC[0:8, 2:3], None, ALU.add).then_inc(free[u % BANKS], 1)
                nc.vector.wait_ge(free[u % BANKS], dv.uses(u))
                stt(GR[0:8, 5, :], GR[0:8, 4, :], -1.0, GR[0:8, 4, :], ALU.mult, ALU.max).then_inc(sem["bg_in"], 1)
                nc.vector.wait_ge(sem["bg_in"], dv.due("bg_in"))
                nc.vector.wait_ge(sem["bg_ln"], dv.due("bg_ln"))
                stt(GR[0:8, 6, :], GR[0:8, 4, :], 0.0, GR[0:8, 5, :], ALU.max, ALU.add).then_inc(sem["vector_step"], 1)
                nc.vector.wait_ge(sem["vector_step"], dv.due("vector_step"))
                ts(GR[0:8, 6, :], GR[0:8, 6, :], VEC[0:8, 3:4], None, ALU.mult).then_inc(sem["vector_step"], 1)
                nc.vector.wait_ge(sem["vector_step"], dv.due("vector_step"))
                for c in range(2):
                    cols = slice(c * P, (c + 1) * P)
                    ins = v.tensor_tensor_scan(GR[0:8, 4, cols], one[0:8].broadcast_to([8, P]), GR[0:8, 6, cols], 0.0,
                                               ALU.mult, ALU.subtract)
                    if c:
                        ins.then_inc(sem["bg_cum"], 1)
                        nc.vector.wait_ge(sem["bg_cum"], dv.due("bg_cum"))
                    else:
                        ins.then_inc(sem["vector_step"], 1)
                        nc.vector.wait_ge(sem["vector_step"], dv.due("vector_step"))
                ts(GR[0:8, 1, :], GR[0:8, 4, :], -1.0, None, ALU.mult).then_inc(sem["vector_step"], 1)
                nc.vector.wait_ge(sem["vector_step"], dv.due("vector_step"))
                nc.vector.wait_ge(sem["bg_exp"], dv.due("bg_exp"))
                tt(GR[0:8, 2, P:SEQ], GR[0:8, 2, P:SEQ], GR[0:8, 0, P:SEQ], ALU.mult).then_inc(sem["bg_rows"], 1)
                nc.vector.wait_ge(sem["bg_rows"], dv.due("bg_rows"))
                for i in range(6):
                    for j in range(2):
                        u = dv.unit()
                        nc.vector.wait_ge(full[u % BANKS], dv.uses(u))
                        if 2 * i + j >= 2:
                            nc.vector.wait_ge(sem["conv_done"], dv.due("conv_done"))
                        for c in range(2):
                            tile = 4 * i + 2 * j + c
                            acc = SCR2[:, 512 * (j % 2) + SEQ * c:512 * (j % 2) + SEQ * (c + 1)]
                            src = U(u)[:, c * SEQ:(c + 1) * SEQ]
                            ts(acc, src, CONVW[:, 3, tile:tile + 1], None, ALU.mult).then_inc(sem["vector_step"], 1)
                            nc.vector.wait_ge(sem["vector_step"], dv.due("vector_step"))
                            for d in range(1, 4):
                                ins = stt(acc[:, d:SEQ], src[:, 0:SEQ - d], CONVW[:, 3 - d, tile:tile + 1],
                                          acc[:, d:SEQ], ALU.mult, ALU.add)
                                if (c, d) == (1, 3):
                                    ins.then_inc(free[u % BANKS], 1)
                                    nc.vector.wait_ge(free[u % BANKS], dv.uses(u))
                                else:
                                    ins.then_inc(sem["vector_step"], 1)
                                    nc.vector.wait_ge(sem["vector_step"], dv.due("vector_step"))
                    if i == 0:
                        for n_out in oa:
                            nc.vector.wait_ge(free[n_out % BANKS], dv.uses(n_out))
                        for t in range(2):
                            tt(SCR2[:, D:2 * D], HA[:, t, :], HA[:, t, :], ALU.mult).then_inc(sem["vector_step"], 1)
                            nc.vector.wait_ge(sem["vector_step"], dv.due("vector_step"))
                            ins = red(SS2[:, 4 * t:4 * t + 4], SCR2[:, D:2 * D].rearrange("p (h n) -> p h n", h=4), AXX, ALU.add)
                            if t:
                                ins.then_inc(sem["stat"], 1)
                                nc.vector.wait_ge(sem["stat"], dv.due("stat"))
                            else:
                                ins.then_inc(sem["vector_step"], 1)
                                nc.vector.wait_ge(sem["vector_step"], dv.due("vector_step"))
                    elif i == 1:
                        nc.vector.wait_ge(sem["root"], dv.due("root"))
                        v.reciprocal(SS2[:, 0:8], SS2[:, 0:8]).then_inc(sem["vector_step"], 1)
                        nc.vector.wait_ge(sem["vector_step"], dv.due("vector_step"))
                        for t in range(2):
                            x = HA[:, t, :].rearrange("p (h n) -> p h n", h=4)
                            tt(x, x, bc(SS2[:, 4 * t:4 * t + 4], 2, [P, 4, 256]), ALU.mult).then_inc(sem["vector_step"], 1)
                            nc.vector.wait_ge(sem["vector_step"], dv.due("vector_step"))
                            tt(HA[:, t, :], HA[:, t, :], OA[:, t, :], ALU.mult).then_inc(sem["ha_ready"], 1)
                            nc.vector.wait_ge(sem["ha_ready"], dv.due("ha_ready"))
                    elif i == 2:
                        take_pairs(dv, HAT, lambda k: COLS2[:, 96 + k:97 + k])
                nc.vector.wait_ge(sem["conv_done"], dv.due("conv_done", 2))
                u = dv.unit()
                nc.vector.wait_ge(free[u % BANKS], dv.uses(u))
                v.reciprocal(R16[0:16, :], R16[0:16, :]).then_inc(sem["vector_step"], 1)
                nc.vector.wait_ge(sem["vector_step"], dv.due("vector_step"))
                ts(R16[0:8, :], R16[0:8, :], SCALE_A, None, ALU.mult).then_inc(sem["rn_ready"], 1)
                nc.vector.wait_ge(sem["rn_ready"], dv.due("rn_ready"))
                for r in range(0, 16, 2):
                    T = QB if r < 8 else KB
                    h = r % 8
                    x = T[:, h:h + 2, :].rearrange("p h n -> p (h n)")
                    u = dv.unit()
                    nc.vector.wait_ge(full[u % BANKS], dv.uses(u))
                    tt(x, x, U(u)[:, :], ALU.mult).then_inc(free[u % BANKS], 1)
                    nc.vector.wait_ge(free[u % BANKS], dv.uses(u))
                u = dv.unit()
                nc.vector.wait_ge(full[u % BANKS], dv.uses(u))
                v.tensor_copy(GC[:, 0:48], U(u)[:, 0:48]).then_inc(free[u % BANKS], 1)
                nc.vector.wait_ge(free[u % BANKS], dv.uses(u))
                flat = lambda T: T.rearrange("p m n -> p (m n)")

                def delta(b):
                    m = DELTA[b % 2]
                    masked = lambda i: bc(i, 1, [P, 4, P])
                    by_four = lambda u: U(u)[:, :].rearrange("p (m n) -> p m n", m=4)
                    u_decay, u_beta, u_kq, u_kk = dv.unit(), dv.unit(), dv.unit(), dv.unit()
                    for n_in in (u_decay, u_beta, u_kq, u_kk):
                        nc.vector.wait_ge(full[n_in % BANKS], dv.uses(n_in))
                    tt(m.decay, by_four(u_decay), masked(CAUSAL[:, 0:P]), ALU.add).then_inc(sem["e_in"], 1)
                    nc.vector.wait_ge(sem["e_in"], dv.due("e_in"))
                    u = dv.unit()
                    nc.vector.wait_ge(full[u % BANKS], dv.uses(u))
                    for i in range(4):
                        h, c = 2 * b + i // 2, i % 2
                        g = GC[:, 32 + h:33 + h] if c else GC[:, 40 + h:41 + h]
                        ins = ts(m.k[:, i, :], U(u)[:, i * P:(i + 1) * P], g, None, ALU.mult)
                        if i == 3:
                            ins.then_inc(free[u % BANKS], 1)
                            nc.vector.wait_ge(free[u % BANKS], dv.uses(u))
                        else:
                            ins.then_inc(sem["vector_step"], 1)
                            nc.vector.wait_ge(sem["vector_step"], dv.due("vector_step"))
                    dv.unit()
                    nc.vector.wait_ge(sem["e_exp"], dv.due("e_exp"))
                    tt(flat(m.attn), U(u_kq)[:, :], flat(m.decay), ALU.mult).then_inc(free[u_kq % BANKS], 1)
                    nc.vector.wait_ge(free[u_kq % BANKS], dv.uses(u_kq))
                    tt(m.decay, m.decay, masked(STRICT), ALU.mult).then_inc(sem["vector_step"], 1)
                    nc.vector.wait_ge(sem["vector_step"], dv.due("vector_step"))
                    tt(flat(m.decay), flat(m.decay), U(u_kk)[:, :], ALU.mult).then_inc(free[u_kk % BANKS], 1)
                    nc.vector.wait_ge(free[u_kk % BANKS], dv.uses(u_kk))
                    tt(flat(m.a_t), flat(m.decay), U(u_beta)[:, :], ALU.mult).then_inc(free[u_beta % BANKS], 1)
                    nc.vector.wait_ge(free[u_beta % BANKS], dv.uses(u_beta))
                    tt(m.q, QB[:, 2 * b:2 * b + 2, P:SEQ], m.grown, ALU.mult).then_inc(sem["at_ready"], 1)
                    nc.vector.wait_ge(sem["at_ready"], dv.due("at_ready"))
                    yield
                    u = dv.unit()
                    nc.vector.wait_ge(full[u % BANKS], dv.uses(u))
                    tt(m.inv, by_four(u), masked(LEVEL[:, 0, :]), ALU.mult).then_inc(free[u % BANKS], 1)
                    nc.vector.wait_ge(free[u % BANKS], dv.uses(u))
                    tt(m.inv, masked(ident), m.inv, ALU.subtract).then_inc(sem["vector_step"], 1)
                    nc.vector.wait_ge(sem["vector_step"], dv.due("vector_step"))
                    tt(m.inv_t, m.a_t, masked(LEVEL[:, 7, :]), ALU.mult).then_inc(sem["vector_step"], 1)
                    nc.vector.wait_ge(sem["vector_step"], dv.due("vector_step"))
                    tt(m.inv_t, masked(ident), m.inv_t, ALU.subtract).then_inc(sem["x0_ready"], 1)
                    nc.vector.wait_ge(sem["x0_ready"], dv.due("x0_ready"))
                    yield
                    for s in range(1, 7):
                        u = dv.unit()
                        nc.vector.wait_ge(full[u % BANKS], dv.uses(u))
                        tt(m.y, by_four(u), masked(LEVEL[:, s, :]), ALU.mult).then_inc(free[u % BANKS], 1)
                        nc.vector.wait_ge(free[u % BANKS], dv.uses(u))
                        yield
                        for T in ((m.inv, m.inv_t) if s < 6 else (m.inv_t,)):
                            u = dv.unit()
                            nc.vector.wait_ge(full[u % BANKS], dv.uses(u))
                            tt(flat(T), flat(T), U(u)[:, :], ALU.subtract).then_inc(free[u % BANKS], 1)
                            nc.vector.wait_ge(free[u % BANKS], dv.uses(u))
                        yield
                    dv.unit(2)
                    yield
                    dv.unit()
                    yield
                    u = dv.unit()
                    nc.vector.wait_ge(full[u % BANKS], dv.uses(u))
                    tt(m.u[:, 1::2, :], m.u[:, 1::2, :], U(u)[:, 0:SEQ].rearrange("p (m n) -> p m n", m=2), ALU.subtract).then_inc(free[u % BANKS], 1)
                    nc.vector.wait_ge(free[u % BANKS], dv.uses(u))
                    yield
                    u = dv.unit()
                    nc.vector.wait_ge(full[u % BANKS], dv.uses(u))
                    v.tensor_copy(QB[:, 2 * b:2 * b + 2, :].rearrange("p h n -> p (h n)"), U(u)[:, :]).then_inc(free[u % BANKS], 1)
                    nc.vector.wait_ge(free[u % BANKS], dv.uses(u))

                for b in (0, 2):
                    in_turn(delta(b), delta(b + 1))
                v.memset(SS2[:, 63:64], 0.0).then_inc(sem["heads_done"], 1)
                nc.vector.wait_ge(sem["heads_done"], dv.due("heads_done"))
                o = up(4096, 2048)
                tt(SCR2, o, o, ALU.mult).then_inc(sem["vector_step"], 1)
                nc.vector.wait_ge(sem["vector_step"], dv.due("vector_step"))
                red(SS2[:, 0:16], SCR2.rearrange("p (g n) -> p g n", g=16), AXX, ALU.add).then_inc(sem["stat"], 1)
                nc.vector.wait_ge(sem["stat"], dv.due("stat"))
                nc.vector.wait_ge(sem["root"], dv.due("root"))
                v.reciprocal(SS2[:, 0:16], SS2[:, 0:16]).then_inc(sem["vector_step"], 1)
                nc.vector.wait_ge(sem["vector_step"], dv.due("vector_step"))
                og = o.rearrange("p (g n) -> p g n", g=16)
                tt(og, og, bc(SS2[:, 0:16], 2, [P, 16, P]), ALU.mult).then_inc(sem["vector_step"], 1)
                nc.vector.wait_ge(sem["vector_step"], dv.due("vector_step"))
                z = [dv.unit() for i in range(4)]
                for n_out in z:
                    nc.vector.wait_ge(free[n_out % BANKS], dv.uses(n_out))
                for t in range(2):
                    tt(HBN[:, t, :].rearrange("p (h n) -> p h n", h=8), QB[:, :, t * P:(t + 1) * P],
                                           ZB[:, t, :].rearrange("p (h n) -> p h n", h=8), ALU.mult).then_inc(sem["hb_ready"], 1)
                    nc.vector.wait_ge(sem["hb_ready"], dv.due("hb_ready"))
                ga = [dv.unit() for i in range(4)]
                for n_out in ga:
                    nc.vector.wait_ge(free[n_out % BANKS], dv.uses(n_out))
                for c in range(2):
                    for t in range(2):
                        x = SGA[:, t, c * CN:(c + 1) * CN]
                        u = dv.unit()
                        nc.vector.wait_ge(full[u % BANKS], dv.uses(u))
                        tt(x, x, U(u)[:, :], ALU.mult).then_inc(free[u % BANKS], 1)
                        nc.vector.wait_ge(free[u % BANKS], dv.uses(u))
                gb = [dv.unit() for i in range(4)]
                for n_out in gb:
                    nc.vector.wait_ge(free[n_out % BANKS], dv.uses(n_out))
                take_pairs(dv, XT2, lambda k: COLS2[:, 104:105])
                for c in range(2):
                    for t in range(2):
                        x, g = SGA[:, t, c * CN:(c + 1) * CN], SGB[:, t, c * CN:(c + 1) * CN]
                        u = dv.unit()
                        nc.vector.wait_ge(full[u % BANKS], dv.uses(u))
                        tt(SCR2[:, 0:CN], g, U(u)[:, :], ALU.mult).then_inc(free[u % BANKS], 1)
                        nc.vector.wait_ge(free[u % BANKS], dv.uses(u))
                        ins = tt(x, x, SCR2[:, 0:CN], ALU.add)
                        if (c, t) == (1, 1):
                            ins.then_inc(sem["y_ready"], 1)
                            nc.vector.wait_ge(sem["y_ready"], dv.due("y_ready"))
                        else:
                            ins.then_inc(sem["vector_step"], 1)
                            nc.vector.wait_ge(sem["vector_step"], dv.due("vector_step"))
                take_pairs(dv, HAT)
                residual_norm(True)
                take_pairs(dv, XT2)
                tile = 0
                for n in FF_TILES:
                    gs = [dv.unit() for j in range(0, n, 2)]
                    for j in range(0, n, 2):
                        u = dv.unit()
                        nc.vector.wait_ge(full[u % BANKS], dv.uses(u))
                        nc.vector.wait_ge(free[gs[j // 2] % BANKS], dv.uses(gs[j // 2]))
                        p = (tile // 2) % 4
                        tt(HFF[:, tile:tile + 2, :].rearrange("p f n -> p (f n)"),
                                           SCR2[:, 512 * p:512 * p + 512], U(u)[:, :], ALU.mult).then_inc(free[u % BANKS], 1)
                        nc.vector.wait_ge(free[u % BANKS], dv.uses(u))
                        tile += 2
                residual_norm(False)

_INS = [
    "x", "c", "ctx", "c_ctx", "ada_w", "ada_b", "norm1_g", "norm2_g", "w_in", "w_out", "head_out_g", "sgu_w", "sgu_b",
    "diff_qn_g", "diff_kn_g", "diff_lambda", "na_qn_g", "na_kn_g", "na_rpb", "router_w", "exp_w_gate", "exp_w_up",
    "exp_w_down", "w_in_2", "b_igate_2", "b_fgate_2", "g_mlstm_norm_2", "conv_w_2", "a_log_2", "dt_bias_2",
    "g_gdn_norm_2", "w_branch_a_2", "w_branch_b_2", "w_out_2", "ln1_g_2", "ln1_b_2", "w_ffn_up_2",
    "w_ffn_down_2", "ln2_g_2", "ln2_b_2",
]


def kernel(**inputs):
    import numpy as _np
    import concourse.bacc as _bacc
    from concourse import mybir as _mybir
    from concourse.bass_utils import run_bass_kernel_spmd as _run

    nc = _bacc.Bacc("TRN2", target_bir_lowering=False, num_devices=1)
    arrays, args = {}, {}
    for name in _INS:
        arrays[f"in_{name}_dram"] = _np.ascontiguousarray(inputs[name])
    for name, a in constants().items():
        arrays[f"in_c_{name}_dram"] = a
    for key, a in arrays.items():
        args[key[3:-5]] = nc.dram_tensor(key, a.shape, _mybir.dt.from_np(a.dtype), kind="ExternalInput").ap()
    out = nc.dram_tensor("out_0_dram", (1, SEQ, D), F32, kind="ExternalOutput").ap()
    gate_scratch = nc.dram_tensor("gate_scratch", (DEPTH, 2, 2, D), F32, kind="Internal").ap()
    band = nc.dram_tensor("band", (DEPTH, HEADS, 7, GRID_W, BAND), F32, kind="Internal").ap()
    build(nc, args, out, gate_scratch, band)
    r = _run(nc, [arrays], core_ids=[0])
    return r.results[0]["out_0_dram"]
```
